# Optimizing a Trainium2 kernel written in Bass

```python
import math
import jax, jax.numpy as jnp
from jax import lax
import numpy as np

D_MODEL = 1024
BATCH = 1
SEQ = 512
DEPTH = 2

HEAD_DIM = 64
NSA_HEADS = 16
NSA_GROUPS = 2
NSA_HPG = NSA_HEADS // NSA_GROUPS
NSA_WIDTH = NSA_HEADS * HEAD_DIM
CMP_BLOCK = 32
CMP_STRIDE = 16
CMP_HIDDEN = 2 * HEAD_DIM
SEL_BLOCK = 64
SEL_TOPK = 8
WINDOW = 512
SEL_Q_BLOCK = 64
FOX_HEADS = 16
FOX_WIDTH = FOX_HEADS * HEAD_DIM
Q_BLOCK = 128
ROPE_THETA = 10000.0
RMS_EPS = 1e-6
NEG_INF = -1e30
FORCED_SCORE = 1e4

SPLITS = (
    NSA_WIDTH,
    3 * 2 * NSA_GROUPS * HEAD_DIM,
    3 * NSA_HEADS,
    NSA_WIDTH,
    FOX_WIDTH,
    FOX_WIDTH,
    FOX_WIDTH,
    FOX_HEADS,
    FOX_WIDTH,
    2 * D_MODEL,
)
IN_COLS = sum(SPLITS)

kernel_name = 'nsa_fox_gated_hybrid'

def rms_norm(x, g):
    xf = x.astype(jnp.float32)
    y = xf * lax.rsqrt(jnp.mean(xf * xf, axis=-1, keepdims=True) + RMS_EPS)
    return (y * g.astype(jnp.float32)).astype(x.dtype)

def rope_tables(T, dtype):
    inv = ROPE_THETA ** (-jnp.arange(0, HEAD_DIM, 2, dtype=jnp.float32) / HEAD_DIM)
    ang = jnp.arange(T, dtype=jnp.float32)[:, None] * inv[None, :]
    return jnp.cos(ang).astype(dtype), jnp.sin(ang).astype(dtype)

def rope(x, cos, sin):
    d2 = HEAD_DIM // 2
    shape = (1, x.shape[1]) + (1,) * (x.ndim - 3) + (d2,)
    c, s = cos.reshape(shape), sin.reshape(shape)
    x1, x2 = x[..., :d2], x[..., d2:]
    return jnp.concatenate([x1 * c - x2 * s, x2 * c + x1 * s], axis=-1)

def masked_softmax(s, mask):
    p = jax.nn.softmax(jnp.where(mask, s, NEG_INF), axis=-1)
    return jnp.where(mask, p, 0.0)

def compress(k, pe, w1, w2):
    T = k.shape[1]
    n_cmp = (T - CMP_BLOCK) // CMP_STRIDE + 1
    idx = np.arange(n_cmp)[:, None] * CMP_STRIDE + np.arange(CMP_BLOCK)[None, :]
    blk = k[:, idx] + pe[None, None, :, None, :]
    hid = jax.nn.silu(jnp.einsum('bnlgd,ldh->bngh', blk, w1.reshape(CMP_BLOCK, HEAD_DIM, CMP_HIDDEN)))
    return jnp.einsum('bngh,hd->bngd', hid, w2)

def nsa_mixer(q, kv, gate_logits, pe_k, w1_k, w2_k, pe_v, w1_v, w2_v, cos, sin):
    B, T = q.shape[0], q.shape[1]
    G, HPG, D = NSA_GROUPS, NSA_HPG, HEAD_DIM
    scale = D ** -0.5
    q = q.reshape(B, T, NSA_HEADS, D)
    kv = kv.reshape(B, T, 6, G, D)
    k_c, v_c, k_s, v_s, k_w, v_w = [kv[:, :, i] for i in range(6)]
    t = jnp.arange(T)

    k_cmp = compress(k_c, pe_k, w1_k, w2_k)
    v_cmp = compress(v_c, pe_v, w1_v, w2_v)
    n_cmp = k_cmp.shape[1]
    qg = q.reshape(B, T, G, HPG, D)
    s_cmp = jnp.einsum('btghd,bngd->bghtn', qg, k_cmp).astype(jnp.float32) * scale
    blk_end = jnp.arange(n_cmp) * CMP_STRIDE + CMP_BLOCK - 1
    cmp_mask = blk_end[None, :] <= t[:, None]
    p_cmp = masked_softmax(s_cmp, cmp_mask)
    o_cmp = jnp.einsum('bghtn,bngd->btghd', p_cmp.astype(v_cmp.dtype), v_cmp)

    n_sel = T // SEL_BLOCK
    ci = np.arange(n_cmp)[:, None] * CMP_STRIDE
    sj = np.arange(n_sel)[None, :] * SEL_BLOCK
    overlap = jnp.asarray(((ci < sj + SEL_BLOCK) & (ci + CMP_BLOCK > sj)).astype(np.float32))
    imp = jnp.einsum('bghtn,nj->bgtj', p_cmp, overlap)
    sel_ids = jnp.arange(n_sel)
    cur = t // SEL_BLOCK
    forced = (sel_ids[None, :] == 0) | (sel_ids[None, :] == cur[:, None]) | (sel_ids[None, :] == cur[:, None] - 1)
    valid = sel_ids[None, :] * SEL_BLOCK <= t[:, None]
    score = jnp.where(forced, FORCED_SCORE, jnp.where(valid, imp, -1.0))
    k_top = min(SEL_TOPK, n_sel)
    _, sel_idx = lax.top_k(score, k_top)

    qr = rope(q, cos, sin).reshape(B, T, G, HPG, D)
    kb = rope(k_s, cos, sin).reshape(B, n_sel, SEL_BLOCK, G, D).transpose(0, 3, 1, 2, 4)
    vb = v_s.reshape(B, n_sel, SEL_BLOCK, G, D).transpose(0, 3, 1, 2, 4)
    n_qs = T // SEL_Q_BLOCK
    q_chunks = jnp.moveaxis(qr.reshape(B, n_qs, SEL_Q_BLOCK, G, HPG, D), 1, 0)
    idx_chunks = jnp.moveaxis(sel_idx.reshape(B, G, n_qs, SEL_Q_BLOCK, k_top), 2, 0)
    t_chunks = t.reshape(n_qs, SEL_Q_BLOCK)
    bi = jnp.arange(B)[:, None, None, None]
    gi = jnp.arange(G)[None, :, None, None]

    def sel_step(args):
        qc, ic, tc = args
        kg = kb[bi, gi, ic]
        vg = vb[bi, gi, ic]
        s = jnp.einsum('bqghd,bgqnld->bghqnl', qc, kg).astype(jnp.float32) * scale
        tok = ic[..., None] * SEL_BLOCK + jnp.arange(SEL_BLOCK)
        mask = (tok <= tc[None, None, :, None, None])[:, :, None]
        p = masked_softmax(s.reshape(B, G, HPG, SEL_Q_BLOCK, k_top * SEL_BLOCK),
                           mask.reshape(B, G, 1, SEL_Q_BLOCK, k_top * SEL_BLOCK))
        p = p.reshape(B, G, HPG, SEL_Q_BLOCK, k_top, SEL_BLOCK)
        return jnp.einsum('bghqnl,bgqnld->bqghd', p.astype(vg.dtype), vg)

    o_slc = lax.map(sel_step, (q_chunks, idx_chunks, t_chunks))
    o_slc = jnp.moveaxis(o_slc, 0, 1).reshape(B, T, G, HPG, D)

    kwp = jnp.pad(rope(k_w, cos, sin), ((0, 0), (WINDOW, 0), (0, 0), (0, 0)))
    vwp = jnp.pad(v_w, ((0, 0), (WINDOW, 0), (0, 0), (0, 0)))
    n_qw = T // Q_BLOCK
    qw_chunks = jnp.moveaxis(qr.reshape(B, n_qw, Q_BLOCK, G, HPG, D), 1, 0)
    starts = jnp.arange(n_qw, dtype=jnp.int32) * Q_BLOCK

    def win_step(args):
        qc, s0 = args
        kc = lax.dynamic_slice_in_dim(kwp, s0, WINDOW + Q_BLOCK, axis=1)
        vc = lax.dynamic_slice_in_dim(vwp, s0, WINDOW + Q_BLOCK, axis=1)
        tq = s0 + jnp.arange(Q_BLOCK)
        sk = s0 - WINDOW + jnp.arange(WINDOW + Q_BLOCK)
        mask = (sk[None, :] <= tq[:, None]) & (sk[None, :] > tq[:, None] - WINDOW) & (sk[None, :] >= 0)
        s = jnp.einsum('bqghd,bkgd->bghqk', qc, kc).astype(jnp.float32) * scale
        p = masked_softmax(s, mask)
        return jnp.einsum('bghqk,bkgd->bqghd', p.astype(vc.dtype), vc)

    o_win = lax.map(win_step, (qw_chunks, starts))
    o_win = jnp.moveaxis(o_win, 0, 1).reshape(B, T, G, HPG, D)

    g = jax.nn.sigmoid(gate_logits).reshape(B, T, 3, G, HPG)[..., None]
    o = g[:, :, 0] * o_cmp + g[:, :, 1] * o_slc + g[:, :, 2] * o_win
    return o.reshape(B, T, NSA_WIDTH)

def fox_mixer(q, k, v, f_logits, b_f):
    B, T = q.shape[0], q.shape[1]
    H, D = FOX_HEADS, HEAD_DIM
    scale = D ** -0.5
    q = q.reshape(B, T, H, D)
    k = k.reshape(B, T, H, D)
    v = v.reshape(B, T, H, D)
    log_f = jax.nn.log_sigmoid(f_logits.astype(jnp.float32) + b_f.astype(jnp.float32))
    F = jnp.cumsum(log_f, axis=1).transpose(0, 2, 1)
    n_q = T // Q_BLOCK
    q_chunks = jnp.moveaxis(q.reshape(B, n_q, Q_BLOCK, H, D), 1, 0)
    F_chunks = jnp.moveaxis(F.reshape(B, H, n_q, Q_BLOCK), 2, 0)
    starts = jnp.arange(n_q, dtype=jnp.int32) * Q_BLOCK
    key_pos = jnp.arange(T)

    def fox_step(args):
        qc, Fq, s0 = args
        s = jnp.einsum('bqhd,bkhd->bhqk', qc, k).astype(jnp.float32) * scale
        s = s + Fq[..., None] - F[:, :, None, :]
        mask = key_pos[None, :] <= (s0 + jnp.arange(Q_BLOCK))[:, None]
        p = masked_softmax(s, mask)
        return jnp.einsum('bhqk,bkhd->bqhd', p.astype(v.dtype), v)

    o = lax.map(fox_step, (q_chunks, F_chunks, starts))
    return jnp.moveaxis(o, 0, 1).reshape(B, T, FOX_WIDTH)

def setup_inputs(seed: int = 0) -> dict:
    key = jax.random.key(seed)
    ks = jax.random.split(key, 14)
    f32 = jnp.float32

    def nrm(k, shape, scale):
        return jax.random.normal(k, shape, f32) * scale

    return {
        'x': nrm(ks[0], (BATCH, SEQ, D_MODEL), 1.0),
        'norm_g': 1.0 + nrm(ks[1], (DEPTH, D_MODEL), 0.01),
        'w_in': nrm(ks[2], (DEPTH, D_MODEL, IN_COLS), D_MODEL ** -0.5),
        'b_forget': jax.random.uniform(ks[3], (DEPTH, FOX_HEADS), f32, 1.0, 5.0),
        'cmp_pe_k': nrm(ks[4], (DEPTH, CMP_BLOCK, HEAD_DIM), 0.1),
        'cmp_w1_k': nrm(ks[5], (DEPTH, CMP_BLOCK * HEAD_DIM, CMP_HIDDEN), (CMP_BLOCK * HEAD_DIM) ** -0.5),
        'cmp_w2_k': nrm(ks[6], (DEPTH, CMP_HIDDEN, HEAD_DIM), CMP_HIDDEN ** -0.5),
        'cmp_pe_v': nrm(ks[7], (DEPTH, CMP_BLOCK, HEAD_DIM), 0.1),
        'cmp_w1_v': nrm(ks[8], (DEPTH, CMP_BLOCK * HEAD_DIM, CMP_HIDDEN), (CMP_BLOCK * HEAD_DIM) ** -0.5),
        'cmp_w2_v': nrm(ks[9], (DEPTH, CMP_HIDDEN, HEAD_DIM), CMP_HIDDEN ** -0.5),
        'w_proj_nsa': nrm(ks[10], (DEPTH, NSA_WIDTH, D_MODEL), NSA_WIDTH ** -0.5),
        'w_proj_fox': nrm(ks[11], (DEPTH, FOX_WIDTH, D_MODEL), FOX_WIDTH ** -0.5),
        'w_out': nrm(ks[12], (DEPTH, D_MODEL, D_MODEL), D_MODEL ** -0.5),
        'final_g': 1.0 + nrm(ks[13], (D_MODEL,), 0.01),
    }

def reference(x, norm_g, w_in, b_forget, cmp_pe_k, cmp_w1_k, cmp_w2_k, cmp_pe_v, cmp_w1_v, cmp_w2_v,
              w_proj_nsa, w_proj_fox, w_out, final_g):
    T = x.shape[1]
    cos, sin = rope_tables(T, x.dtype)
    split_at = np.cumsum(SPLITS)[:-1].tolist()
    for l in range(DEPTH):
        h = rms_norm(x, norm_g[l])
        proj = jnp.einsum('btd,dc->btc', h, w_in[l])
        q_a, kv_a, g_a, z_a, q_b, k_b, v_b, f_b, z_b, merge = jnp.split(proj, split_at, axis=-1)
        y_a = nsa_mixer(q_a, kv_a, g_a, cmp_pe_k[l], cmp_w1_k[l], cmp_w2_k[l],
                        cmp_pe_v[l], cmp_w1_v[l], cmp_w2_v[l], cos, sin) * jax.nn.silu(z_a)
        y_b = fox_mixer(q_b, k_b, v_b, f_b, b_forget[l]) * jax.nn.silu(z_b)
        r_a, r_b = jnp.split(merge, 2, axis=-1)
        merged = (jax.nn.sigmoid(r_a) * jnp.einsum('btc,cd->btd', y_a, w_proj_nsa[l])
                  + jax.nn.sigmoid(r_b) * jnp.einsum('btc,cd->btd', y_b, w_proj_fox[l]))
        x = x + jnp.einsum('btd,de->bte', merged, w_out[l])
    return rms_norm(x, final_g)


_drawn_inputs = setup_inputs


def setup_inputs(seed=0):
    import zlib

    import numpy as np

    out = dict(_drawn_inputs(seed))
    spreads = {}
    factors = {'norm_g': 8.0,
     'cmp_pe_k': 8.0,
     'cmp_w1_k': 2.826,
     'cmp_w2_k': 2.778,
     'cmp_pe_v': 4.951,
     'final_g': 5.485}
    for name, (base, spread) in spreads.items():
        noise = np.random.default_rng([zlib.crc32(name.encode()), seed]).standard_normal(out[name].shape)
        drawn = base * np.exp(spread * noise) if base else spread * noise
        out[name] = __import__('jax').numpy.asarray(drawn.astype(out[name].dtype))
    for name, factor in factors.items():
        out[name] = (out[name] * factor).astype(out[name].dtype)
    return out
```

```python
from contextlib import ExitStack

import numpy as np

import concourse.bass as bass
from concourse import mybir

F32 = mybir.dt.float32
F32R = mybir.dt.float32r
ALU = mybir.AluOpType
ACT = mybir.ActivationFunctionType
AX_X = mybir.AxisListType.X

P = 128
T = 512
D = 1024
DEPTH = 2
HD = 64
HEADS = 16
PAIRS = HEADS // 2
GROUPS = 2
KT = D // P
QT = T // P
CMP_BLOCK, CMP_STRIDE = 32, 16
N_CMP = (T - CMP_BLOCK) // CMP_STRIDE + 1
N_PAD = 32
CJ = CMP_BLOCK // 2
NEG = -1.0e30
BIG = 3.0e38
SCALE = HD ** -0.5
EPS = 1e-6

C_QA = 0
C_KV = C_QA + D
C_G = C_KV + 3 * 2 * GROUPS * HD
C_ZA = C_G + 3 * HEADS
C_QB = C_ZA + D
C_KB = C_QB + D
C_VB = C_KB + D
C_F = C_VB + D
C_ZB = C_F + HEADS
C_RA = C_ZB + D
C_RB = C_RA + D
IN_COLS = C_RB + D
KV_UNITS = [(C_KV + 2 * P, P), (C_KV + 4 * P, P), (C_KV + 3 * P, P), (C_KV + 5 * P, P),
            (C_KV, P), (C_KV + P, P), (C_G, 3 * HEADS), (C_F, HEADS)]

U_NSA, U_FOX, U_MERGE, U_OUT, U_ALL = 8, 24, 56, 88, 96
S_FOX, S_ALL = 4 * 4 * PAIRS, 4 * 4 * PAIRS + 4 * 2 * PAIRS
A_FOX, A_ALL = 4 * PAIRS, 6 * PAIRS
SM_RING = 4
PT_COLS = 3 * 384 + T


def spread(total, slots):
    return [total * (s + 1) // slots for s in range(slots)]


class Body:

    def __init__(self, att, proj):
        self.att, self.proj = att, proj
        self.steps = 0 if att is None else (16 if att.nsa else 8)
        self.slots = self.steps + 3 if att is not None else (8 if proj.nsa else 16)
        n = 0 if proj is None else (2 if proj.nsa else 4)
        self.cum = spread(24 * n, self.slots)
        self.begin, self.end = {}, {}
        for u in range(n):
            first = next(s for s in range(self.slots) if self.cum[s] > 24 * u)
            last = next(s for s in range(self.slots) if self.cum[s] >= 24 * u + 24)
            self.begin.setdefault(first, []).append(u)
            self.end[u] = last
        self.n_units = n

    def at_end(self, part, lag):
        return min(self.end[part] + lag, self.slots + lag)


class Pair:

    def __init__(self, nsa, l, i, parity, group=0, first=False):
        self.first = first
        self.nsa, self.l, self.i, self.b, self.g = nsa, l, i, parity, group
        if nsa:
            self.half = l * (U_ALL // 2) + U_NSA // 2 + i
            self.s0 = l * S_ALL + 16 * i
            self.a0 = l * A_ALL + 4 * i
            self.r = l * (2 * PAIRS) + i
        else:
            self.half = l * (U_ALL // 2) + U_FOX // 2 + 2 * i
            self.s0 = l * S_ALL + S_FOX + 8 * i
            self.a0 = l * A_ALL + A_FOX + 2 * i
            self.r = l * (2 * PAIRS) + PAIRS + i

    def unit(self, part):
        return self.half + part // 2, part % 2

    def atts(self):
        if self.nsa:
            return [(h, self.g, s, 1 + s) for h in range(2) for s in range(2)]
        return [(h, self.b, h, None) for h in range(2)]


def bass_trunk(nc, x, norm_g, w_in, b_forget, pe_k, w1_k, w2_k, pe_v, w1_v, w2_v, w_nsa, w_fox,
               w_out, final_g, rope_c, rope_s, out):
    ctx = ExitStack()
    with ctx:
        scope = [ctx]

        def sb(name, shape, dt=F32):
            return scope[-1].enter_context(nc.sbuf_tensor(name, shape, dt))

        def psum(name, shape):
            return ctx.enter_context(nc.psum_tensor(name, shape, F32))

        def sem(name):
            return ctx.enter_context(nc.semaphore(name))

        xT = sb("xT", [P, KT, T])
        h_hi = sb("h_hi", [P, KT, T], F32R)
        h_lo = sb("h_lo", [P, KT, T], F32R)
        w_raw = sb("w_raw", [P, 2, KT, P])
        w_hi = sb("w_hi", [P, 2, KT, P], F32R)
        w_lo = sb("w_lo", [P, 2, KT, P], F32R)
        cosT = sb("cosT", [P, T])
        sinT = sb("sinT", [P, T])
        causal = sb("causal", [P, T])
        cmp_mask = sb("cmp_mask", [P, QT, 2, N_PAD])
        ident = sb("ident", [P, P])
        ones = sb("ones", [P, P])
        sel_f = sb("sel_f", [4, 2, P])
        sel = sb("sel", [4, 2, P], F32R)
        past_first = sb("past_first", [P, 1])
        gains = sb("gains", [P, DEPTH + 1, KT])
        b_f = sb("b_f", [HEADS, DEPTH])
        gates = sb("gates", [P, QT, 3 * HEADS])
        kcb = sb("kcb", [P, GROUPS, 2 * N_PAD])
        vcb = sb("vcb", [2 * N_PAD, GROUPS, P])
        pool_note = sb("pool_note", [P, 1])
        row_max = sb("row_max", [P, SM_RING])
        row_sum = sb("row_sum", [P, SM_RING])
        row_inv = sb("row_inv", [P, SM_RING])

        with ExitStack() as own:
            scope.append(own)
            pt_hi = sb("pt_hi", [P, 2, PT_COLS], F32R)
            pt_lo = sb("pt_lo", [P, 2, PT_COLS], F32R)
            prob = sb("prob", [P, SM_RING, T])
            y_raw = sb("y_raw", [P, T])
            y_hi = sb("y_hi", [P, T], F32R)
            y_lo = sb("y_lo", [P, T], F32R)
            q_st = sb("q_st", [P, 2, 2, T], F32R)
            kk_hi = sb("kk_hi", [P, 2, 2, T], F32R)
            kk_lo = sb("kk_lo", [P, 2, 2, T], F32R)
            v_hi = sb("v_hi", [P, 2, 2, QT, 3 * HD], F32R)
            v_lo = sb("v_lo", [P, 2, 2, QT, 3 * HD], F32R)
            f_row = sb("f_row", [4, 2, T], F32R)
            q_raw = sb("q_raw", [P, T])
            q_swap = sb("q_swap", [P, T])
            q_rope = sb("q_rope", [P, T])
            part_hi = sb("part_hi", [P, T], F32R)
            part_lo = sb("part_lo", [P, T], F32R)
            z_tanh = sb("z_tanh", [P, T])
            z_silu = sb("z_silu", [P, 2, T])
            pc = sb("pc", [P, 2 * QT, N_PAD])
            pc_t = sb("pc_t", [2 * N_PAD, T])
            pc_max = sb("pc_max", [P, 2 * QT])
            pc_sum = sb("pc_sum", [P, 2 * QT])
            pc_inv = sb("pc_inv", [P, 2 * QT])
            scope.pop()
        with ExitStack() as own:
            scope.append(own)
            squares = sb("squares", [P, 2, T])
            rstd = sb("rstd", [P, T])
            h_raw = sb("h_raw", [P, 2, T])
            c_w1 = sb("c_w1", [P, 2, CJ, P])
            c_w2 = sb("c_w2", [P, 2, HD])
            c_pe = sb("c_pe", [P, 2, CJ])
            c_src = sb("c_src", [P, 2, GROUPS, T // 2])
            c_blk = sb("c_blk", [P, 2, CJ, GROUPS, N_PAD])
            c_th = sb("c_th", [P, 2, GROUPS * N_PAD])
            c_hid = sb("c_hid", [P, 2, GROUPS * N_PAD])
            scope.pop()
        with ExitStack() as own:
            scope.append(own)
            g_th = sb("g_th", [3 * HEADS, T])
            f_a = sb("f_a", [HEADS, T])
            f_b = sb("f_b", [HEADS, T])
            f_hi = sb("f_hi", [HEADS, T], F32R)
            f_lo = sb("f_lo", [HEADS, T], F32R)
            scope.pop()
        with ExitStack() as own:
            scope.append(own)
            yt_hi = sb("yt_hi", [P, 2, KT, T], F32R)
            yt_lo = sb("yt_lo", [P, 2, KT, T], F32R)
            m_hi = sb("m_hi", [P, KT, T], F32R)
            m_lo = sb("m_lo", [P, KT, T], F32R)
            m_th = sb("m_th", [P, 2, T])
            m_sum = sb("m_sum", [P, 2, T])
            scope.pop()
        with ExitStack() as own:
            scope.append(own)
            clear = sb("clear", [P, 5, T])
            x_nat = sb("x_nat", [P, QT, D])
            o_t = sb("o_t", [P, KT, T])
            o_nat = sb("o_nat", [P, QT, D])
            scope.pop()

        y_dram = nc.dram_tensor("y_scratch", [2, 2, PAIRS, P, T], F32R, kind="Internal").ap()
        f_dram = nc.dram_tensor("f_scratch", [HEADS, 2, T], F32R, kind="Internal").ap()

        acc = [psum(f"acc{n}", [P, T]) for n in range(2)]
        scores = [psum(f"scores{n}", [P, T]) for n in range(2)]
        turned = [psum(f"turned{n}", [P, T]) for n in range(2)]
        o_pair = psum("o_pair", [P, T])
        misc = psum("misc", [P, T])

        consts = sem("consts")
        consts_dma = sem("consts_dma")
        x_landed = sem("x_landed")
        x_turned = sem("x_turned")
        x_done = sem("x_done")
        w_landed = [sem(f"w_landed{n}") for n in range(2)]
        w_hi_done = sem("w_hi_done")
        w_lo_done = sem("w_lo_done")
        unit_mm = sem("unit_mm")
        sq_done = sem("sq_done")
        sq_used = sem("sq_used")
        var_done = sem("var_done")
        std_done = sem("std_done")
        rstd_done = sem("rstd_done")
        h_raw_done = sem("h_raw_done")
        h_hi_done = sem("h_hi_done")
        h_lo_done = sem("h_lo_done")
        pads = sem("pads")
        raw_done = sem("raw_done")
        swapped = sem("swapped")
        cos_done = sem("cos_done")
        sin_done = sem("sin_done")
        rope_done = sem("rope_done")
        part_hi_done = sem("part_hi_done")
        part_lo_done = sem("part_lo_done")
        q_stacked = sem("q_stacked")
        k_stacked = sem("k_stacked")
        v_raw_done = sem("v_raw_done")
        v_turned = sem("v_turned")
        v_hi_done = sem("v_hi_done")
        v_lo_done = sem("v_lo_done")
        c_landed = sem("c_landed")
        c_src_done = sem("c_src_done")
        c_blk_done = sem("c_blk_done")
        c_hid_mm = sem("c_hid_mm")
        c_th_done = sem("c_th_done")
        c_hid_done = sem("c_hid_done")
        c_out_mm = sem("c_out_mm")
        cb_ready = sem("cb_ready")
        g_th_done = sem("g_th_done")
        g_turned = sem("g_turned")
        gates_done = sem("gates_done")
        f_step = sem("f_step")
        f_exp = sem("f_exp")
        f_saved = sem("f_saved")
        f_landed = sem("f_landed")
        s_mm = sem("s_mm")
        s_max = sem("s_max")
        s_exp = sem("s_exp")
        s_inv = sem("s_inv")
        s_scaled = sem("s_scaled")
        s_turned = sem("s_turned")
        pt_hi_done = sem("pt_hi_done")
        pt_lo_done = sem("pt_lo_done")
        pv_mm = sem("pv_mm")
        cmp_s = sem("cmp_s")
        cmp_dve = sem("cmp_dve")
        cmp_exp = sem("cmp_exp")
        cmp_turned = sem("cmp_turned")
        cmp_pt = sem("cmp_pt")
        z_th_done = sem("z_th_done")
        z_done = sem("z_done")
        sel_done = sem("sel_done")
        y_mul = sem("y_mul")
        y_hi_done = sem("y_hi_done")
        y_lo_done = sem("y_lo_done")
        y_stored = sem("y_stored")
        y_free = sem("y_free")
        y_loaded = [sem(f"y_loaded{n}") for n in range(2)]
        m_th_done = sem("m_th_done")
        m_part = sem("m_part")
        m_sum_done = sem("m_sum_done")
        m_hi_done = sem("m_hi_done")
        m_lo_done = sem("m_lo_done")
        o_turned = sem("o_turned")
        o_copied = [sem(f"o_copied{n}") for n in range(2)]
        o_stored = sem("o_stored")

        w_view = w_in.rearrange("l (k p) c -> p l k c", p=P)
        wn_view = w_nsa.rearrange("l (k p) c -> p l k c", p=P)
        wf_view = w_fox.rearrange("l (k p) c -> p l k c", p=P)
        wo_view = w_out.rearrange("l (k p) c -> p l k c", p=P)

        kv_widths = [w for _, w in KV_UNITS]
        N_CONSTS = 12

        def apart(eng):
            eng.nop(nofuse=True)

        def key_cols(qt):
            return max(P * (qt + 1), 2 * P)

        def bodies(eng, l, body):
            body(l, None, Pair(True, l, 0, 0, first=True))
            with eng.Fori(0, 2) as j:
                body(l, Pair(True, l, 2 * j, 0, 0), Pair(True, l, 2 * j + 1, 1))
                body(l, Pair(True, l, 2 * j + 1, 1, 0), Pair(True, l, 2 * j + 2, 0))
            for i in range(4, 7):
                body(l, Pair(True, l, i, i % 2, 1), Pair(True, l, i + 1, (i + 1) % 2))
            body(l, Pair(True, l, 7, 1, 1), Pair(False, l, 0, 0, first=True))
            with eng.Fori(0, 3) as j:
                body(l, Pair(False, l, 2 * j, 0), Pair(False, l, 2 * j + 1, 1))
                body(l, Pair(False, l, 2 * j + 1, 1), Pair(False, l, 2 * j + 2, 0))
            body(l, Pair(False, l, 6, 0), Pair(False, l, 7, 1))
            body(l, Pair(False, l, 7, 1), None)

        def pt_tiles(pt, a, qt):
            first = P * qt
            return pt[:, a % 2, first:first + 384 * qt + P] if qt == 0 else \
                strided(pt, a % 2, first, qt + 1)

        def strided(pt, half, first, n):
            whole = pt[:, half, first:first + 384 * (n - 1) + P]
            ap = pt[:, half, first:first + 384 * n] if first + 384 * n <= PT_COLS else None
            if ap is not None:
                return ap.rearrange("p (k c) -> p k c", k=n)[:, :, 0:P]
            early = first - 256
            return pt[:, half, early:early + 384 * n].rearrange("p (k c) -> p k c", k=n)[:, :, 256:384]

        def turned_tiles(s, qt):
            bank = turned[s % 2][:, 0:P * (qt + 1)]
            return bank if qt == 0 else bank.rearrange("p (k c) -> p k c", k=qt + 1)

        block = ctx.enter_context(nc.Block())

        @block.sync
        def _(sp):
            def load(src, l, col, width, half, par, first=False):
                sp.wait_ge(w_lo_done, 2 * half + par + 1)
                sp.dma_start(w_raw[:, par:par + 1, :, 0:width],
                             src[:, bass.ds(l, 1), :, bass.ds(col, width)]).then_inc(w_landed[par], 16)

            sp.dma_start(x_nat[:, :, :], x[0].rearrange("(i p) d -> p i d", p=P)).then_inc(x_landed, 16)
            with sp.Fori(0, DEPTH) as l:
                base = l * (U_ALL // 2)
                for n, (col, width) in enumerate(KV_UNITS):
                    load(w_view, l, col, width, base + n // 2, n % 2)
                with sp.Fori(0, PAIRS) as i:
                    half = base + U_NSA // 2 + i
                    load(w_view, l, C_QA + P * i, P, half, 0)
                    load(w_view, l, C_ZA + P * i, P, half, 1)
                with sp.Fori(0, PAIRS) as i:
                    half = base + U_FOX // 2 + 2 * i
                    load(w_view, l, C_QB + P * i, P, half, 0)
                    load(w_view, l, C_KB + P * i, P, half, 1)
                    load(w_view, l, C_VB + P * i, P, half + 1, 0)
                    load(w_view, l, C_ZB + P * i, P, half + 1, 1)
                with sp.Fori(0, KT) as e:
                    half = base + U_MERGE // 2 + 2 * e
                    load(w_view, l, C_RA + P * e, P, half, 0)
                    load(w_view, l, C_RB + P * e, P, half, 1)
                    load(wn_view, l, P * e, P, half + 1, 0)
                    load(wf_view, l, P * e, P, half + 1, 1)
                with sp.Fori(0, KT // 2) as j:
                    half = base + U_OUT // 2 + j
                    load(wo_view, l, 2 * P * j, P, half, 0)
                    load(wo_view, l, 2 * P * j + P, P, half, 1)
            for i in range(QT):
                for n in range(2):
                    sp.wait_ge(o_copied[n], i + 1)
                sp.dma_start(out[0, i * P:(i + 1) * P, :], o_nat[:, i, :]).then_inc(o_stored, 16)
            sp.wait_ge(o_stored, 16 * QT)

        @block.gpsimd
        def _(pool):
            pool.memset(ident[:, :], 0.0).then_inc(consts, 1)
            pool.memset(ones[:, :], 1.0).then_inc(consts, 1)
            pool.memset(causal[:, :], 0.0).then_inc(consts, 1)
            pool.memset(cmp_mask[:, :, :, :], 0.0).then_inc(consts, 1)
            pool.memset(sel_f[:, :, :], 1.0).then_inc(consts, 1)
            pool.memset(past_first[:, :], 1.0).then_inc(consts, 1)
            pool.wait_ge(consts, 6)
            pool.affine_select(out=ident[:, :], in_=ident[:, :], compare_op=ALU.not_equal, fill=1.0,
                               base=0, pattern=[[-1, P]], channel_multiplier=1).then_inc(consts, 1)
            tri = causal[:, T - P:T]
            pool.affine_select(out=tri, in_=tri, compare_op=ALU.is_ge, fill=NEG, base=0,
                               pattern=[[-1, P]], channel_multiplier=1).then_inc(consts, 1)
            pool.affine_select(out=cmp_mask[:, :, :, :], in_=cmp_mask[:, :, :, :], compare_op=ALU.is_ge,
                               fill=NEG, base=1 - CMP_BLOCK,
                               pattern=[[P, QT], [0, 2], [-CMP_STRIDE, N_PAD]],
                               channel_multiplier=1).then_inc(consts, 1)
            pool.affine_select(out=sel_f[:, 0, :], in_=sel_f[:, 0, :], compare_op=ALU.is_ge, fill=0.0,
                               base=1, pattern=[[0, P]], channel_multiplier=-1).then_inc(consts, 1)
            pool.affine_select(out=sel_f[:, 1, :], in_=sel_f[:, 1, :], compare_op=ALU.is_ge, fill=0.0,
                               base=-2, pattern=[[0, P]], channel_multiplier=1).then_inc(consts, 1)
            pool.affine_select(out=past_first[:, :], in_=past_first[:, :], compare_op=ALU.is_ge, fill=0.0,
                               base=1 - CMP_BLOCK, pattern=[[0, 1]],
                               channel_multiplier=1).then_inc(consts, 1)
            pool.memset(kcb[:, :, :], 0.0).then_inc(pads, 1)
            pool.memset(vcb[:, :, :], 0.0).then_inc(pads, 1)
            pool.memset(row_sum[:, 0:1], 0.0).then_inc(y_free, 1)

            def swap_and_cos(c):
                pool.wait_ge(raw_done, c + 1)
                apart(pool)
                for n in range(4):
                    src = 32 * (n ^ 1)
                    pool.dma_start(q_swap[32 * n:32 * n + 32, :], q_raw[src:src + 32, :]).then_inc(swapped, 16)
                pool.tensor_tensor(q_rope[:, :], q_raw[:, :], cosT[:, :], ALU.mult).then_inc(cos_done, 1)

            def stack_q(b, parts, att):
                pool.wait_ge(part_lo_done, parts + 1)
                apart(pool)
                if att is not None:
                    pool.wait_ge(s_mm, att.s0 + 1)
                    apart(pool)
                    apart(pool)
                for h in range(2):
                    rows = slice(HD * h, HD * h + HD)
                    pool.dma_start(q_st[0:HD, b, h, :], part_hi[rows, :]).then_inc(q_stacked, 16)
                    pool.dma_start(q_st[HD:P, b, h, :], part_lo[rows, :]).then_inc(q_stacked, 16)

            def stack_k(places, parts, att):
                pool.wait_ge(part_lo_done, parts + 1)
                apart(pool)
                if att is not None:
                    pool.wait_ge(s_mm, att.s0 + 1)
                    apart(pool)
                for h, (b, s) in enumerate(places):
                    rows = slice(HD * h, HD * h + HD)
                    for half in range(2):
                        to = slice(HD * half, HD * half + HD)
                        pool.dma_start(kk_hi[to, b, s, :], part_hi[rows, :]).then_inc(k_stacked, 16)
                        pool.dma_start(kk_lo[to, b, s, :], part_lo[rows, :]).then_inc(k_stacked, 16)

            def store_y(pair, mixer):
                pool.wait_ge(y_lo_done, pair.r + 1)
                apart(pool)
                to = y_dram[mixer]
                pool.dma_start(to[0, bass.ds(pair.i, 1)].rearrange("a p t -> (a p) t"),
                               y_hi[:, :]).then_inc(y_stored, 16)
                pool.dma_start(to[1, bass.ds(pair.i, 1)].rearrange("a p t -> (a p) t"),
                               y_lo[:, :]).then_inc(y_stored, 16)
                pool.wait_ge(y_stored, 32 * (pair.r + 1))
                apart(pool)
                pool.memset(pool_note[:, :], 0.0).then_inc(y_free, 1)

            def body(l, att, proj):
                if proj is not None and proj.nsa:
                    swap_and_cos(l * 10 + 2 + proj.i)
                    stack_q(proj.b, l * 26 + 2 + proj.i, att)
                elif proj is not None:
                    pool.wait_ge(f_saved, 32 * (l + 1))
                    pool.wait_ge(s_mm, att.s0 + 1)
                    apart(pool)
                    pool.dma_start(f_row[:, proj.b, :],
                                   f_dram[bass.ds(2 * proj.i, 2)].rearrange("h a t -> (h a) t")
                                   ).then_inc(f_landed, 16)
                    stack_q(proj.b, l * 26 + 10 + 2 * proj.i, att)
                    stack_k([(proj.b, 0), (proj.b, 1)], l * 26 + 11 + 2 * proj.i, att)
                if att is not None:
                    store_y(att, 0 if att.nsa else 1)

            with pool.Fori(0, DEPTH) as l:
                pool.wait_ge(h_lo_done, KT * (l + 1))
                apart(pool)
                for v in (v_hi, v_lo):
                    flat = v[:, :, :, :, :].rearrange("p b s k c -> p (b s k) c")
                    pool.memset(flat[:, :, 0:HD].bitcast(F32), 0.0).then_inc(pads, 1)
                    pool.memset(flat[:, :, 2 * HD:3 * HD].bitcast(F32), 0.0).then_inc(pads, 1)
                pool.memset(c_blk[:, :, :, :, N_CMP:N_PAD].rearrange("p a j g n -> p (a j g) n"),
                            0.0).then_inc(pads, 1)
                for s in range(2):
                    swap_and_cos(l * 10 + s)
                    stack_k([(0, s), (1, s)], l * 26 + s, None)
                pool.wait_ge(f_step, 6 * (l + 1))
                apart(pool)
                pool.dma_start(f_dram[:, 0, :], f_hi[:, :]).then_inc(f_saved, 16)
                pool.dma_start(f_dram[:, 1, :], f_lo[:, :]).then_inc(f_saved, 16)
                pool.wait_ge(c_out_mm, 2 * (l + 1))
                apart(pool)
                for pt in (pt_hi, pt_lo):
                    pool.memset(pt[:, :, 3 * 384 + 2 * P:3 * 384 + 3 * P].bitcast(F32), 0.0).then_inc(pads, 1)
                bodies(pool, l, body)
                pool.wait_ge(y_stored, 32 * 2 * PAIRS * (l + 1))
                pool.wait_ge(pv_mm, A_ALL * (l + 1))
                apart(pool)
                for mixer in range(2):
                    for hl, yt in enumerate((yt_hi, yt_lo)):
                        pool.dma_start(yt[:, mixer, :, :],
                                       y_dram[mixer, hl].rearrange("k p t -> p k t")
                                       ).then_inc(y_loaded[mixer], 16)

        @block.scalar
        def _(act):
            def split_hi(half, par, width=P, wait=True):
                act.wait_ge(w_landed[par], 16 * (half + 1))
                if wait:
                    act.wait_ge(unit_mm, 2 * half + par - 1)
                act.activation(w_hi[:, par, :, 0:width], w_raw[:, par, :, 0:width],
                               ACT.Copy).then_inc(w_hi_done, 1)

            def norm(n, between=None, final=False):
                for k in range(KT):
                    act.wait_ge(x_done, KT * n + k + 1)
                    if k >= 2:
                        act.wait_ge(sq_used, KT * n + k - 1)
                    act.activation(squares[:, k % 2, :], xT[:, k, :], ACT.Square).then_inc(sq_done, 1)
                if between is not None:
                    between()
                act.wait_ge(var_done, n + 1)
                act.activation(rstd[:, :], rstd[:, :], ACT.Sqrt).then_inc(std_done, 1)
                if final:
                    return
                for k in range(KT):
                    act.wait_ge(h_raw_done, KT * n + k + 1)
                    act.activation(h_hi[:, k, :], h_raw[:, k % 2, :], ACT.Copy).then_inc(h_hi_done, 1)

            def raw_copy(half, par, c, waits):
                act.wait_ge(unit_mm, 2 * half + par + 1)
                for s, value in waits:
                    act.wait_ge(s, value)
                act.activation(q_raw[:, :], acc[par][:, :], ACT.Copy).then_inc(raw_done, 1)

            def rope_hi(c, waits):
                act.wait_ge(rope_done, c + 1)
                for s, value in waits:
                    act.wait_ge(s, value)
                act.activation(part_hi[:, :], q_rope[:, :], ACT.Copy).then_inc(part_hi_done, 1)

            def sums_hi(half, par, waits):
                act.wait_ge(unit_mm, 2 * half + par + 1)
                for s, value in waits:
                    act.wait_ge(s, value)
                act.activation(part_hi[:, :], acc[par][:, :], ACT.Copy).then_inc(part_hi_done, 1)

            def v_copy(half, par, waits):
                act.wait_ge(unit_mm, 2 * half + par + 1)
                for s, value in waits:
                    act.wait_ge(s, value)
                act.activation(q_raw[:, :], acc[par][:, :], ACT.Copy).then_inc(v_raw_done, 1)

            def v_round(n, to):
                act.wait_ge(v_turned, n + 1)
                act.activation(to, misc[:, :].rearrange("p (k s d) -> p s k d", k=QT, s=2),
                               ACT.Copy).then_inc(v_hi_done, 1)

            def z_tanh_of(half, par, r):
                act.wait_ge(unit_mm, 2 * half + par + 1)
                act.wait_ge(z_done, r + 1)
                act.activation(z_tanh[:, :], acc[par][:, :], ACT.Tanh, scale=0.5).then_inc(z_th_done, 1)

            def body(l, att, proj):
                plan = Body(att, proj)
                todo = {}

                def at(slot, what):
                    todo.setdefault(slot, []).append(what)

                if proj is not None:
                    for slot, units in plan.begin.items():
                        for u in units:
                            nxt = proj.unit(u + 1)
                            at(slot, lambda nxt=nxt: split_hi(*nxt))
                    if proj.nsa:
                        c = l * 10 + 2 + proj.i
                        first = att is None
                        raw_waits = [(v_turned, l * 10 + 2)] if first else [(cmp_s, att.l * PAIRS + att.i + 1)]
                        part_waits = [(k_stacked, 128 * (l * 10 + 2))] if first else [(q_stacked, 64 * proj.r)]
                        at(plan.at_end(0, 1), lambda: raw_copy(*proj.unit(0), c, raw_waits))
                        at(plan.at_end(0, 5), lambda: rope_hi(c, part_waits))
                        at(plan.at_end(1, 1), lambda: z_tanh_of(*proj.unit(1), proj.r))
                    else:
                        n = l * 10 + 2 + proj.i
                        q_waits = [(q_stacked, 64 * proj.r)] if att.nsa else [(k_stacked, 128 * n)]
                        v_waits = [(cmp_s, PAIRS * (l + 1))] if att.nsa else [(v_turned, n)]
                        at(plan.at_end(0, 1), lambda: sums_hi(*proj.unit(0), q_waits))
                        at(plan.at_end(1, 1), lambda: sums_hi(*proj.unit(1), [(q_stacked, 64 * (proj.r + 1))]))
                        at(plan.at_end(2, 1), lambda: v_copy(*proj.unit(2), v_waits))
                        at(plan.at_end(2, 2), lambda: v_round(n, v_hi[:, proj.b, :, :, HD:2 * HD]))
                        at(plan.at_end(3, 1), lambda: z_tanh_of(*proj.unit(3), proj.r))

                def exp_step(s):
                    t = att.s0 + s
                    ring, width = s % SM_RING, P * (s % QT + 1)
                    act.wait_ge(s_max, t + 1)
                    act.activation(prob[:, ring, 0:width], prob[:, ring, 0:width], ACT.Exp,
                                   bias=row_max[:, ring:ring + 1], scale=-1.0,
                                   accum_out=row_sum[:, ring:ring + 1]).then_inc(s_exp, 1)

                def hi_step(s):
                    a, qt = divmod(s, QT)
                    act.wait_ge(s_turned, att.s0 + s + 1)
                    if qt == 0 and a >= 2:
                        act.wait_ge(pv_mm, att.a0 + a - 1)
                    act.activation(pt_tiles(pt_hi, a, qt), turned_tiles(s, qt), ACT.Copy)\
                        .then_inc(pt_hi_done, 1)

                if att is not None and att.nsa:
                    m = att.l * PAIRS + att.i

                    def cmp_exponent():
                        act.wait_ge(cmp_dve, 7 * m + 3)
                        act.activation(pc[:, :, :], pc[:, :, :], ACT.Exp, scale=SCALE).then_inc(cmp_exp, 1)

                    def cmp_copy():
                        act.wait_ge(cmp_turned, m + 1)
                        act.activation(pc_t[:, :], misc[0:2 * N_PAD, :], ACT.Copy).then_inc(cmp_pt, 1)

                    at(2, cmp_exponent)
                    at(4, cmp_copy)

                last = max([plan.slots] + [k + 1 for k in todo])
                for s in range(last):
                    if s < plan.steps:
                        exp_step(s)
                    if 2 <= s < plan.steps + 2:
                        hi_step(s - 2)
                    for what in todo.get(s, []):
                        what()
                if att is not None:
                    act.wait_ge(y_mul, att.r + 2)
                    act.wait_ge(y_free, att.r + 1)
                    act.activation(y_hi[:, :], y_raw[:, :], ACT.Copy).then_inc(y_hi_done, 1)

            for n, (to, src) in enumerate(((cosT[:, :], rope_c), (sinT[:, :], rope_s))):
                act.dma_start(to, src).then_inc(consts_dma, 16)
            with nc.allow_non_contiguous_dma(reason="a few kB of per-channel constants"):
                for l in range(DEPTH):
                    act.dma_start(gains[:, l, :], norm_g[l].rearrange("(k p) -> p k", p=P)).then_inc(consts_dma, 16)
                act.dma_start(gains[:, DEPTH, :], final_g.rearrange("(k p) -> p k", p=P)).then_inc(consts_dma, 16)
                act.dma_start(b_f[:, :], b_forget.rearrange("l h -> h l")).then_inc(consts_dma, 16)

            with act.Fori(0, DEPTH) as l:
                half0 = l * (U_ALL // 2)
                norm(l, between=lambda: split_hi(half0, 0, kv_widths[0], wait=False))
                for a, w1, w2, pe in ((0, w1_k, w2_k, pe_k), (1, w1_v, w2_v, pe_v)):
                    for j in (slice(0, CJ // 2), slice(CJ // 2, CJ)):
                        act.dma_start(c_w1[:, a:a + 1, j, :],
                                      w1.rearrange("l (j p) h -> p l j h", p=P)[:, bass.ds(l, 1), j]
                                      ).then_inc(c_landed, 16)
                    act.dma_start(c_w2[:, a:a + 1, :],
                                  w2.rearrange("l h d -> h l d")[:, bass.ds(l, 1)]).then_inc(c_landed, 16)
                    with nc.allow_non_contiguous_dma(reason="8 kB of position vectors, transposed"):
                        for par in range(2):
                            act.dma_start(c_pe[HD * par:HD * par + HD, a:a + 1, :],
                                          pe.rearrange("l (j a) d -> a d l j", a=2)[par][:, bass.ds(l, 1)]
                                          ).then_inc(c_landed, 16)

                def kv(n):
                    return half0 + n // 2, n % 2

                split_hi(*kv(1), kv_widths[1], wait=False)
                split_hi(*kv(2), kv_widths[2])
                raw_copy(*kv(0), l * 10, [])
                split_hi(*kv(3), kv_widths[3])
                rope_hi(l * 10, [])
                raw_copy(*kv(1), l * 10 + 1, [(rope_done, l * 10 + 1)])
                split_hi(*kv(4), kv_widths[4])
                rope_hi(l * 10 + 1, [(k_stacked, 128 * (l * 10 + 1))])
                v_copy(*kv(2), [(rope_done, l * 10 + 2)])
                split_hi(*kv(5), kv_widths[5])
                v_round(l * 10, v_hi[:, :, 0, :, HD:2 * HD])
                v_copy(*kv(3), [(v_turned, l * 10 + 1)])
                split_hi(*kv(6), kv_widths[6])
                v_round(l * 10 + 1, v_hi[:, :, 1, :, HD:2 * HD])
                for a in range(2):
                    half, par_u = kv(4 + a)
                    act.wait_ge(unit_mm, 2 * half + par_u + 1)
                    for g in range(GROUPS):
                        for par in range(2):
                            src = acc[par_u][HD * g:HD * g + HD, :].rearrange("d (m a) -> d a m", a=2)
                            ins = act.activation(c_src[HD * par:HD * par + HD, a, g, :], src[:, par, :], ACT.Copy)
                    ins.then_inc(c_src_done, 1)
                    if a == 0:
                        split_hi(*kv(7), kv_widths[7])
                split_hi(*kv(8))
                half, par = kv(6)
                act.wait_ge(unit_mm, 2 * half + par + 1)
                act.activation(g_th[:, :], acc[par][0:3 * HEADS, :], ACT.Tanh, scale=0.5)\
                    .then_inc(g_th_done, 1)
                for a in range(2):
                    act.wait_ge(c_hid_mm, 2 * l + a + 1)
                    act.activation(c_th[:, a, :], turned[a][:, 0:GROUPS * N_PAD], ACT.Tanh, scale=0.5)\
                        .then_inc(c_th_done, 1)
                act.wait_ge(f_step, 6 * l + 2)
                act.activation(f_b[:, :], f_b[:, :], ACT.Exp, scale=-1.0).then_inc(f_exp, 1)
                act.wait_ge(f_exp, 3 * l + 1)
                act.activation(f_b[:, :], f_b[:, :], ACT.Ln, bias=1.0).then_inc(f_exp, 1)
                act.wait_ge(f_step, 6 * l + 5)
                act.activation(f_hi[:, :], f_b[:, :], ACT.Copy).then_inc(f_exp, 1)

                bodies(act, l, body)

                def merge_tile(e):
                    half = half0 + U_MERGE // 2 + 2 * e
                    for par in range(2):
                        split_hi(half + par, 1 - par)
                        act.wait_ge(unit_mm, 2 * half + par + 1)
                        act.activation(m_th[:, par, :], acc[par][:, :], ACT.Tanh, scale=0.5)\
                            .then_inc(m_th_done, 1)
                    split_hi(half + 1, 1)
                    split_hi(half + 2, 0)
                    act.wait_ge(m_sum_done, KT * l + e + 1)
                    act.activation(m_hi[:, bass.ds(e, 1), :], m_sum[:, 0:1, :], ACT.Copy, scale=0.5)\
                        .then_inc(m_hi_done, 1)

                with act.Fori(0, KT) as e:
                    merge_tile(e)
                with act.Fori(0, KT // 2 - 1) as j:
                    split_hi(half0 + U_OUT // 2 + j, 1)
                    split_hi(half0 + U_OUT // 2 + j + 1, 0)
                split_hi(half0 + U_OUT // 2 + KT // 2 - 1, 1)
            norm(DEPTH, final=True)
            for n in range(2 * QT):
                if n % 2:
                    act.wait_ge(o_turned, n + 1)
                    act.activation(o_nat[:, n // 2, 512:1024], turned[1][:, :], ACT.Copy).then_inc(o_copied[1], 1)

        @block.vector
        def _(dve):
            def split_lo(half, par, width=P):
                dve.wait_ge(w_hi_done, 2 * half + par + 1)
                dve.tensor_tensor(w_lo[:, par, :, 0:width], w_raw[:, par, :, 0:width],
                                  w_hi[:, par, :, 0:width], ALU.subtract).then_inc(w_lo_done, 1)

            def norm(n, between=None, final=False):
                dve.wait_ge(sq_used, KT * (n + 1))
                dve.tensor_scalar(rstd[:, :], misc[:, :], 1.0 / D, EPS, ALU.mult, ALU.add).then_inc(var_done, 1)
                if between is not None:
                    between()
                dve.wait_ge(std_done, n + 1)
                dve.reciprocal(rstd[:, :], rstd[:, :]).then_inc(rstd_done, 1)
                dve.wait_ge(rstd_done, n + 1)

                def raw(k):
                    if k >= 2 and not final:
                        dve.wait_ge(h_lo_done, KT * n + k - 1)
                    to = o_t[:, k, :] if final else h_raw[:, k % 2, :]
                    gain = gains[:, DEPTH, k:k + 1] if final else gains[:, bass.ds(n, 1), k]
                    dve.scalar_tensor_tensor(to, xT[:, k, :], gain, rstd[:, :],
                                             ALU.mult, ALU.mult).then_inc(h_raw_done, 1)

                def remainder(k):
                    dve.wait_ge(h_hi_done, KT * n + k + 1)
                    dve.tensor_tensor(h_lo[:, k, :], h_raw[:, k % 2, :], h_hi[:, k, :],
                                      ALU.subtract).then_inc(h_lo_done, 1)

                for k in range(KT):
                    raw(k)
                    if k and not final:
                        remainder(k - 1)
                if not final:
                    remainder(KT - 1)

            def rope_sum(c):
                dve.wait_ge(swapped, 64 * (c + 1))
                dve.tensor_tensor(q_swap[:, :], q_swap[:, :], sinT[:, :], ALU.mult).then_inc(sin_done, 1)
                dve.wait_ge(sin_done, c + 1)
                dve.wait_ge(cos_done, c + 1)
                dve.tensor_tensor(q_rope[:, :], q_rope[:, :], q_swap[:, :], ALU.add).then_inc(rope_done, 1)

            def part_lo_of(src, parts):
                dve.wait_ge(part_hi_done, parts + 1)
                dve.tensor_tensor(part_lo[:, :], src, part_hi[:, :], ALU.subtract).then_inc(part_lo_done, 1)

            def v_rest(n, to, hi):
                dve.wait_ge(v_hi_done, n + 1)
                dve.tensor_tensor(to, misc[:, :].rearrange("p (k s d) -> p s k d", k=QT, s=2), hi,
                                  ALU.subtract).then_inc(v_lo_done, 1)

            def z_silu_of(half, par, r, b):
                dve.wait_ge(z_th_done, r + 1)
                dve.scalar_tensor_tensor(z_silu[:, b, :], z_tanh[:, :], 1.0, acc[par][:, :],
                                         ALU.add, ALU.mult).then_inc(z_done, 1)

            def body(l, att, proj):
                plan = Body(att, proj)
                todo = {}

                def at(slot, what):
                    todo.setdefault(slot, []).append(what)

                if proj is not None:
                    for slot, units in plan.begin.items():
                        for u in units:
                            at(slot, lambda nxt=proj.unit(u + 1): split_lo(*nxt))
                    if proj.nsa:
                        c, n = l * 10 + 2 + proj.i, l * 26 + 2 + proj.i
                        at(plan.at_end(0, 4), lambda: rope_sum(c))
                        at(plan.at_end(0, 5), lambda: part_lo_of(q_rope[:, :], n))
                        at(plan.at_end(1, 1), lambda: z_silu_of(*proj.unit(1), proj.r, proj.b))
                    else:
                        n, v = l * 26 + 10 + 2 * proj.i, l * 10 + 2 + proj.i
                        at(plan.at_end(0, 1), lambda: part_lo_of(acc[0][:, :], n))
                        at(plan.at_end(1, 1), lambda: part_lo_of(acc[1][:, :], n + 1))
                        at(plan.at_end(2, 2), lambda: v_rest(v, v_lo[:, proj.b, :, :, HD:2 * HD],
                                                             v_hi[:, proj.b, :, :, HD:2 * HD]))
                        at(plan.at_end(3, 1), lambda: z_silu_of(*proj.unit(3), proj.r, proj.b))

                def max_step(s):
                    t, qt, ring = att.s0 + s, s % QT, s % SM_RING
                    width = P * (qt + 1)
                    dve.wait_ge(s_mm, t + 1)
                    if s >= SM_RING:
                        dve.wait_ge(s_turned, t - SM_RING + 1)
                    apart(dve)
                    dve.tensor_tensor_reduce(prob[:, ring, 0:width], scores[s % 2][:, 0:width],
                                             causal[:, T - width:T], -SCALE, BIG, ALU.add, ALU.min,
                                             row_max[:, ring:ring + 1]).then_inc(s_max, 1)

                def scale_step(s):
                    t, qt, ring = att.s0 + s, s % QT, s % SM_RING
                    h, _, _, branch = att.atts()[s // QT]
                    p = prob[:, ring, 0:P * (qt + 1)]
                    dve.wait_ge(s_exp, t + 1)
                    dve.reciprocal(row_inv[:, ring:ring + 1], row_sum[:, ring:ring + 1]).then_inc(s_inv, 1)
                    dve.wait_ge(s_inv, t + 1)
                    if branch is None:
                        ins = dve.tensor_scalar(p, p, row_inv[:, ring:ring + 1], None, ALU.mult)
                    else:
                        gate = gates[:, qt, bass.ds(2 * att.i + HEADS * branch + h, 1)]
                        ins = dve.tensor_scalar(p, p, row_inv[:, ring:ring + 1], gate, ALU.mult, ALU.mult)
                    ins.then_inc(s_scaled, 1)

                def lo_step(s):
                    a, qt = divmod(s, QT)
                    dve.wait_ge(pt_hi_done, att.s0 + s + 1)
                    dve.tensor_tensor(pt_tiles(pt_lo, a, qt), turned_tiles(s, qt), pt_tiles(pt_hi, a, qt),
                                      ALU.subtract).then_inc(pt_lo_done, 1)

                if att is not None and att.nsa:
                    m = att.l * PAIRS + att.i

                    def cmp_top():
                        dve.wait_ge(cmp_s, m + 1)
                        flat = misc[:, 0:2 * QT * N_PAD].rearrange("p (a n) -> p a n", n=N_PAD)
                        mask = cmp_mask[:, :, :, :].rearrange("p q h n -> p (q h) n")
                        dve.tensor_tensor(pc[:, :, :], flat, mask, ALU.add).then_inc(cmp_dve, 1)
                        dve.wait_ge(cmp_dve, 7 * m + 1)
                        dve.tensor_reduce(pc_max[:, :], pc[:, :, :], AX_X, ALU.max).then_inc(cmp_dve, 1)
                        dve.wait_ge(cmp_dve, 7 * m + 2)
                        dve.tensor_tensor(pc[:, :, :], pc[:, :, :],
                                          pc_max[:, :].unsqueeze(2).broadcast_to([P, 2 * QT, N_PAD]),
                                          ALU.subtract).then_inc(cmp_dve, 1)

                    def cmp_norm():
                        dve.wait_ge(cmp_exp, m + 1)
                        dve.tensor_reduce(pc_sum[:, :], pc[:, :, :], AX_X, ALU.add).then_inc(cmp_dve, 1)
                        dve.wait_ge(cmp_dve, 7 * m + 4)
                        dve.reciprocal(pc_inv[:, :], pc_sum[:, :]).then_inc(cmp_dve, 1)
                        dve.wait_ge(cmp_dve, 7 * m + 5)
                        inv = pc_inv[:, :].rearrange("p (q h) -> p q h", h=2)
                        dve.tensor_tensor(inv, inv, gates[:, :, bass.ds(2 * att.i, 2)],
                                          ALU.mult).then_inc(cmp_dve, 1)
                        dve.wait_ge(cmp_dve, 7 * m + 6)
                        dve.tensor_tensor(pc[:, :, :], pc[:, :, :],
                                          pc_inv[:, :].unsqueeze(2).broadcast_to([P, 2 * QT, N_PAD]),
                                          ALU.mult).then_inc(cmp_dve, 1)

                    at(1, cmp_top)
                    at(3, cmp_norm)

                last = max([plan.slots] + [k + 1 for k in todo])
                for s in range(last):
                    if 1 <= s <= plan.steps:
                        scale_step(s - 1)
                    if s < plan.steps:
                        max_step(s)
                    if 2 <= s < plan.steps + 2:
                        lo_step(s - 2)
                    for what in todo.get(s, []):
                        what()
                if att is not None:
                    dve.wait_ge(pv_mm, att.a0 + plan.steps // QT)
                    dve.wait_ge(z_done, att.r + 2)
                    dve.scalar_tensor_tensor(y_raw[:, :], o_pair[:, :], 0.5, z_silu[:, att.b, :],
                                             ALU.mult, ALU.mult).then_inc(y_mul, 1)
                    dve.wait_ge(y_hi_done, att.r + 1)
                    dve.tensor_tensor(y_lo[:, :], y_raw[:, :], y_hi[:, :], ALU.subtract).then_inc(y_lo_done, 1)

            dve.memset(row_inv[:, 0:1], 0.0).then_inc(w_lo_done, 2)
            dve.memset(row_inv[:, 1:2], 0.0).then_inc(z_done, 1)
            dve.memset(row_inv[:, 2:3], 0.0).then_inc(y_mul, 1)
            dve.memset(row_inv[:, 3:4], 0.0).then_inc(m_part, 2)
            dve.wait_ge(consts, N_CONSTS)
            dve.wait_ge(consts_dma, 16 * (2 + DEPTH + 2))
            dve.tensor_copy(sel[:, :, :], sel_f[:, :, :]).then_inc(sel_done, 1)
            for k in range(KT):
                dve.wait_ge(x_turned, k + 1)
                dve.tensor_copy(xT[:, k, :], turned[k % 2][:, :]).then_inc(x_done, 1)

            with dve.Fori(0, DEPTH) as l:
                half0 = l * (U_ALL // 2)

                def kv(n):
                    return half0 + n // 2, n % 2

                norm(l, between=lambda: split_lo(*kv(0), kv_widths[0]))
                split_lo(*kv(1), kv_widths[1])
                split_lo(*kv(2), kv_widths[2])
                rope_sum(l * 10)
                part_lo_of(q_rope[:, :], l * 26)
                split_lo(*kv(3), kv_widths[3])
                split_lo(*kv(4), kv_widths[4])
                rope_sum(l * 10 + 1)
                part_lo_of(q_rope[:, :], l * 26 + 1)
                split_lo(*kv(5), kv_widths[5])
                v_rest(l * 10, v_lo[:, :, 0, :, HD:2 * HD], v_hi[:, :, 0, :, HD:2 * HD])
                split_lo(*kv(6), kv_widths[6])
                v_rest(l * 10 + 1, v_lo[:, :, 1, :, HD:2 * HD], v_hi[:, :, 1, :, HD:2 * HD])
                dve.wait_ge(c_landed, 160 * (l + 1))
                for a in range(2):
                    dve.wait_ge(c_src_done, 2 * l + a + 1)
                    for j in range(CJ):
                        src = c_src[:, a, :, j:j + 8 * (N_CMP - 1) + 1:8]
                        ins = dve.tensor_scalar(c_blk[:, a, j, :, 0:N_CMP], src, c_pe[:, a, j:j + 1], None, ALU.add)
                    ins.then_inc(c_blk_done, 1)
                    if a == 0:
                        split_lo(*kv(7), kv_widths[7])
                split_lo(*kv(8))
                dve.wait_ge(unit_mm, 2 * half0 + 8)
                dve.tensor_scalar(f_a[:, :], acc[1][0:HEADS, :], b_f[:, bass.ds(l, 1)], None,
                                  ALU.add).then_inc(f_step, 1)
                dve.wait_ge(f_step, 6 * l + 1)
                dve.scalar_tensor_tensor(f_b[:, :], f_a[:, :], -1.0, f_a[:, :],
                                         ALU.mult, ALU.max).then_inc(f_step, 1)
                dve.wait_ge(g_turned, l + 1)
                dve.tensor_scalar(gates[:, :, :], misc[:, 0:QT * 3 * HEADS].rearrange("p (q c) -> p q c", q=QT),
                                  0.5, 0.5, ALU.mult, ALU.add).then_inc(gates_done, 1)
                dve.wait_ge(gates_done, 2 * l + 1)
                dve.tensor_scalar(gates[:, 0, 0:HEADS], gates[:, 0, 0:HEADS], past_first[:, 0:1], None,
                                  ALU.mult).then_inc(gates_done, 1)
                for a in range(2):
                    dve.wait_ge(c_th_done, 2 * l + a + 1)
                    dve.scalar_tensor_tensor(c_hid[:, a, :], c_th[:, a, :], 1.0, turned[a][:, 0:GROUPS * N_PAD],
                                             ALU.add, ALU.mult).then_inc(c_hid_done, 1)
                dve.wait_ge(f_exp, 3 * l + 2)
                dve.scalar_tensor_tensor(f_a[:, :], f_a[:, :], 0.0, f_b[:, :],
                                         ALU.min, ALU.subtract).then_inc(f_step, 1)
                dve.wait_ge(f_step, 6 * l + 3)
                dve.tensor_tensor_scan(f_b[:, :], ones[0:HEADS, 0:1].broadcast_to([HEADS, T]), f_a[:, :], 0.0,
                                       ALU.mult, ALU.add).then_inc(f_step, 1)
                dve.wait_ge(f_step, 6 * l + 4)
                dve.tensor_scalar(f_b[:, :], f_b[:, :], -1.0 / SCALE, None, ALU.mult).then_inc(f_step, 1)
                dve.wait_ge(f_exp, 3 * l + 3)
                dve.tensor_tensor(f_lo[:, :], f_b[:, :], f_hi[:, :], ALU.subtract).then_inc(f_step, 1)
                dve.wait_ge(pads, 2)
                dve.wait_ge(c_out_mm, 2 * l + 1)
                ck = scores[0][0:HD, 0:GROUPS * N_PAD].rearrange("d (g n) -> d g n", g=GROUPS)
                for h in range(2):
                    dve.tensor_scalar(kcb[HD * h:HD * h + HD, :, N_PAD * h:N_PAD * h + N_PAD], ck, 0.5, None,
                                      ALU.mult).then_inc(cb_ready, 1)
                dve.wait_ge(c_out_mm, 2 * l + 2)
                cv = scores[1][0:N_PAD, 0:GROUPS * HD].rearrange("n (g d) -> n g d", g=GROUPS)
                for h in range(2):
                    dve.tensor_scalar(vcb[N_PAD * h:N_PAD * h + N_PAD, :, HD * h:HD * h + HD], cv, 0.5, None,
                                      ALU.mult).then_inc(cb_ready, 1)
                dve.wait_ge(gates_done, 2 * l + 2)

                bodies(dve, l, body)

                with dve.Fori(0, KT) as e:
                    half = half0 + U_MERGE // 2 + 2 * e
                    split_lo(half, 1)
                    split_lo(half + 1, 0)
                    split_lo(half + 1, 1)
                    for n in range(2):
                        if n == 1:
                            split_lo(half + 2, 0)
                        dve.wait_ge(m_th_done, 2 * KT * l + 2 * e + n + 1)
                        dve.wait_ge(unit_mm, 2 * half + 3 + n)
                        dve.scalar_tensor_tensor(m_sum[:, n, :], m_th[:, n, :], 1.0, acc[n][:, :],
                                                 ALU.add, ALU.mult).then_inc(m_part, 1)
                    dve.wait_ge(m_part, 2 * KT * l + 2 * e + 4)
                    dve.tensor_tensor(m_sum[:, 0, :], m_sum[:, 0, :], m_sum[:, 1, :], ALU.add).then_inc(m_sum_done, 1)
                    dve.wait_ge(m_hi_done, KT * l + e + 1)
                    dve.scalar_tensor_tensor(m_lo[:, bass.ds(e, 1), :], m_sum[:, 0:1, :], 0.5,
                                             m_hi[:, bass.ds(e, 1), :], ALU.mult, ALU.subtract
                                             ).then_inc(m_lo_done, 1)

                def residual(j, par):
                    dve.wait_ge(unit_mm, 2 * (half0 + U_OUT // 2 + j) + par + 1)
                    tile = xT[:, bass.ds(2 * j + par, 1), :]
                    dve.tensor_tensor(tile, tile, acc[par][:, :].unsqueeze(1), ALU.add)\
                        .then_inc(x_done, 1)

                with dve.Fori(0, KT // 2 - 1) as j:
                    split_lo(half0 + U_OUT // 2 + j, 1)
                    residual(j, 0)
                    split_lo(half0 + U_OUT // 2 + j + 1, 0)
                    residual(j, 1)
                split_lo(half0 + U_OUT // 2 + KT // 2 - 1, 1)
                residual(KT // 2 - 1, 0)
                residual(KT // 2 - 1, 1)
            norm(DEPTH, final=True)
            for n in range(0, 2 * QT, 2):
                dve.wait_ge(o_turned, n + 1)
                dve.tensor_copy(o_nat[:, n // 2, 0:512], turned[0][:, :]).then_inc(o_copied[0], 1)

        @block.tensor
        def _(pe):
            def norm(n):
                for k in range(KT):
                    pe.wait_ge(sq_done, KT * n + k + 1)
                    pe.matmul(misc[:, :], ones[:, :], squares[:, k % 2, :], start=(k == 0),
                              stop=(k == KT - 1)).then_inc(sq_used, 1)

            def unit_piece(first, last, half, par, width=P, hi=None, lo=None, each_k=None, free=None):
                for n in range(first, last):
                    k, which = divmod(n, 3)
                    if n == 0:
                        pe.wait_ge(w_lo_done, 2 * half + par + 3)
                        if free is not None:
                            pe.wait_ge(*free)
                    if each_k is not None and which == 0:
                        pe.wait_ge(*each_k(k))
                    w = w_lo if which == 2 else w_hi
                    rhs = (lo if which == 1 else hi)[:, k, :] if hi is not None else \
                        (h_lo if which == 1 else h_hi)[:, k, :]
                    ins = pe.matmul(acc[par][0:width, :], w[:, par, k, 0:width], rhs,
                                    start=(n == 0), stop=(n == 23))
                    if n == 23:
                        ins.then_inc(unit_mm, 1)

            def bank_read(l, pair, part):
                if pair.nsa and pair.first:
                    return (g_th_done, l + 1) if part == 0 else (f_step, 6 * l + 1)
                if part == 0 and (pair.nsa or pair.first):
                    return raw_done, l * 10 + 2 + (pair.i if pair.nsa else PAIRS)
                if part == 0:
                    return v_raw_done, l * 10 + 2 + pair.i
                if part == 1:
                    return z_done, pair.r + 1
                return part_lo_done, l * 26 + 10 + 2 * pair.i + part - 1

            def turn_v(n):
                pe.wait_ge(v_raw_done, n + 1)
                for kt in range(QT):
                    ins = pe.transpose(misc[:, P * kt:P * kt + P], q_raw[:, P * kt:P * kt + P], ident[:, :])
                ins.then_inc(v_turned, 1)

            def body(l, att, proj):
                plan = Body(att, proj)
                extra = {}
                if proj is not None and not proj.nsa:
                    v = l * 10 + 2 + proj.i

                    def turn():
                        if not att.nsa:
                            pe.wait_ge(v_lo_done, v)
                        turn_v(v)

                    extra.setdefault(plan.at_end(2, 2), []).append(turn)

                def score_step(s):
                    a, qt = divmod(s, QT)
                    h, b, stream, branch = att.atts()[a]
                    n, cols = key_cols(qt), slice(P * qt, P * qt + P)
                    if s >= 2:
                        pe.wait_ge(s_max, att.s0 + s - 1)
                    to = scores[s % 2][:, 0:n]
                    pe.matmul(to, q_st[:, att.b, h, cols], kk_hi[:, b, stream, 0:n], start=True, stop=False)
                    ins = pe.matmul(to, q_st[:, att.b, h, cols], kk_lo[:, b, stream, 0:n], start=False,
                                    stop=branch is not None)
                    if branch is None:
                        ins = pe.matmul(to, sel[:, h, :], f_row[:, b, 0:n], start=False, stop=True)
                    ins.then_inc(s_mm, 1)

                def turn_step(s):
                    qt = s % QT
                    pe.wait_ge(s_scaled, att.s0 + s + 1)
                    if s >= 2:
                        pe.wait_ge(pt_lo_done, att.s0 + s - 1)
                    for kt in range(qt + 1):
                        ins = pe.transpose(turned[s % 2][:, P * kt:P * kt + P],
                                           prob[:, s % SM_RING, P * kt:P * kt + P], ident[:, :])
                    ins.then_inc(s_turned, 1)

                def value_step(a):
                    h, b, stream, branch = att.atts()[a]
                    n_atts = plan.steps // QT
                    pe.wait_ge(pt_lo_done, att.s0 + QT * (a + 1))
                    if a == 0:
                        if not att.nsa:
                            pe.wait_ge(y_mul, att.r + 1)
                        pe.wait_ge(v_lo_done, l * 10 + 2 + (0 if att.nsa else att.i + 1))
                    cols = slice(HD - HD * h, HD - HD * h + P)
                    for kt in range(QT):
                        q0 = min(P * kt, T - 2 * P)
                        src = slice(384 * kt + q0, 384 * kt + T)
                        for m, (v, pt) in enumerate(((v_hi, pt_hi), (v_hi, pt_lo), (v_lo, pt_hi))):
                            ins = pe.matmul(o_pair[:, q0:T], v[:, b, stream, kt, cols], pt[:, a % 2, src],
                                            start=(a == 0 and kt == 0 and m == 0 and not att.nsa),
                                            stop=(a == n_atts - 1 and kt == QT - 1 and m == 2))
                    ins.then_inc(pv_mm, 1)

                def cmp_scores():
                    pe.wait_ge(raw_done, l * 10 + 2 + att.i + 1)
                    pe.wait_ge(cb_ready, 4 * (l + 1))
                    for qt in range(QT):
                        ins = pe.matmul(misc[:, 64 * qt:64 * qt + 64], q_raw[:, P * qt:P * qt + P],
                                        kcb[:, att.g, :], start=True, stop=True)
                    ins.then_inc(cmp_s, 1)

                def cmp_turn():
                    pe.wait_ge(cmp_dve, 7 * (att.l * PAIRS + att.i) + 7)
                    apart(pe)
                    for qt in range(QT):
                        ins = pe.transpose(misc[0:2 * N_PAD, P * qt:P * qt + P],
                                           pc[:, 2 * qt:2 * qt + 2, :].rearrange("p h n -> p (h n)"), ident[:, :])
                    ins.then_inc(cmp_turned, 1)

                def cmp_values():
                    pe.wait_ge(cmp_pt, att.l * PAIRS + att.i + 1)
                    pe.wait_ge(y_mul, att.r + 1)
                    pe.matmul(o_pair[:, :], vcb[:, att.g, :], pc_t[:, :], start=True, stop=False)

                if att is not None:
                    pe.wait_ge(q_stacked, 64 * (att.r + 1))
                    pe.wait_ge(k_stacked, 128 * (l * 10 + 2 + (0 if att.nsa else att.i + 1)))
                    if not att.nsa:
                        pe.wait_ge(f_landed, 16 * (att.l * PAIRS + att.i + 1))
                    for a in range(plan.steps // QT):
                        extra.setdefault(QT * a + 6, []).append(lambda a=a: value_step(a))
                    if att.nsa:
                        extra.setdefault(0, []).insert(0, cmp_scores)
                        extra.setdefault(4, []).insert(0, cmp_turn)
                        extra.setdefault(5, []).insert(0, cmp_values)

                done = 0
                for s in range(max([plan.slots] + [k + 1 for k in extra])):
                    if s < plan.steps:
                        score_step(s)
                    want = plan.cum[s] if s < plan.slots else done
                    while done < want:
                        u = done // 24
                        stop = min(want, 24 * u + 24)
                        unit_piece(done - 24 * u, stop - 24 * u, *proj.unit(u),
                                   free=bank_read(l, proj, u))
                        done = stop
                    if 2 <= s < plan.steps + 2:
                        turn_step(s - 2)
                    for what in extra.get(s, []):
                        what()

            pe.wait_ge(consts, N_CONSTS)
            pe.wait_ge(x_landed, 16)
            for k in range(KT):
                if k >= 2:
                    pe.wait_ge(x_done, k - 1)
                for i in range(QT):
                    ins = pe.transpose(turned[k % 2][:, P * i:P * i + P], x_nat[:, i, P * k:P * k + P], ident[:, :])
                ins.then_inc(x_turned, 1)
            pe.wait_ge(sel_done, 1)
            with pe.Fori(0, DEPTH) as l:
                half0 = l * (U_ALL // 2)

                readers = [None, None, (raw_done, l * 10 + 1), (raw_done, l * 10 + 2),
                           (v_raw_done, l * 10 + 1), (v_raw_done, l * 10 + 2),
                           (c_src_done, 2 * l + 1), (c_src_done, 2 * l + 2)]

                def kv(n, **more):
                    unit_piece(0, 24, half0 + n // 2, n % 2, kv_widths[n], free=readers[n], **more)

                norm(l)
                kv(0, each_k=lambda k: (h_lo_done, KT * l + k + 1))
                kv(1)
                kv(2)
                kv(3)
                turn_v(l * 10)
                kv(4)
                pe.wait_ge(v_lo_done, l * 10 + 1)
                turn_v(l * 10 + 1)
                kv(5)
                kv(6)
                kv(7)
                pe.wait_ge(g_th_done, l + 1)
                pe.wait_ge(v_lo_done, l * 10 + 2)
                apart(pe)
                for i in range(QT):
                    ins = pe.transpose(misc[:, 48 * i:48 * i + 48], g_th[:, P * i:P * i + P],
                                       ident[0:3 * HEADS, 0:3 * HEADS])
                ins.then_inc(g_turned, 1)
                pe.wait_ge(pads, 2 + 7 * l + 5)
                pe.wait_ge(c_landed, 160 * (l + 1))
                for a in range(2):
                    pe.wait_ge(c_blk_done, 2 * l + a + 1)
                    for j in range(CJ):
                        ins = pe.matmul(turned[a][:, 0:GROUPS * N_PAD], c_w1[:, a, j, :],
                                        c_blk[:, a, j, :, :].rearrange("p g n -> p (g n)"),
                                        start=(j == 0), stop=(j == CJ - 1))
                    ins.then_inc(c_hid_mm, 1)
                pe.wait_ge(c_hid_done, 2 * l + 1)
                pe.matmul(scores[0][0:HD, 0:64], c_w2[:, 0, :], c_hid[:, 0, :], start=True,
                          stop=True).then_inc(c_out_mm, 1)
                pe.wait_ge(c_hid_done, 2 * l + 2)
                for g in range(GROUPS):
                    ins = pe.matmul(scores[1][0:N_PAD, HD * g:HD * g + HD], c_hid[:, 1, N_PAD * g:N_PAD * g + N_PAD],
                                    c_w2[:, 1, :], start=True, stop=True)
                ins.then_inc(c_out_mm, 1)

                bodies(pe, l, body)

                pe.wait_ge(v_raw_done, l * 10 + 10)
                pe.wait_ge(z_done, 2 * PAIRS * (l + 1) + 1)
                apart(pe)
                with pe.Fori(0, KT) as e:
                    half = half0 + U_MERGE // 2 + 2 * e
                    for n in range(2):
                        unit_piece(0, 24, half, n, free=(m_part, 2 * KT * l + 2 * e + n + 1))
                    for mixer in range(2):
                        pe.wait_ge(y_loaded[mixer], 32 * (l + 1))
                        unit_piece(0, 24, half + 1, mixer, hi=yt_hi[:, mixer], lo=yt_lo[:, mixer],
                                   free=(m_th_done, 2 * KT * l + 2 * e + mixer + 1))
                pe.wait_ge(m_lo_done, KT * (l + 1))
                apart(pe)
                with pe.Fori(0, KT // 2) as j:
                    for par in range(2):
                        unit_piece(0, 24, half0 + U_OUT // 2 + j, par, hi=m_hi, lo=m_lo,
                                   free=(x_done, KT * (l + 1) + 2 * j + par - 1))
            norm(DEPTH)
            pe.wait_ge(h_raw_done, KT * (DEPTH + 1))
            for n in range(2 * QT):
                if n >= 2:
                    pe.wait_ge(o_copied[n % 2], n // 2)
                for c in range(4):
                    k = 4 * (n % 2) + c
                    ins = pe.transpose(turned[n % 2][:, P * c:P * c + P],
                                       o_t[:, k, P * (n // 2):P * (n // 2) + P], ident[:, :])
                ins.then_inc(o_turned, 1)


_INS = ["x", "norm_g", "w_in", "b_forget", "cmp_pe_k", "cmp_w1_k", "cmp_w2_k", "cmp_pe_v", "cmp_w1_v",
        "cmp_w2_v", "w_proj_nsa", "w_proj_fox", "w_out", "final_g"]


def rope_tables():
    inv = np.float32(10000.0) ** (-np.arange(0, HD, 2, dtype=np.float32) / np.float32(HD))
    ang = (np.arange(T, dtype=np.float32)[None, :] * inv[:, None]).astype(np.float32)
    cos, sin = np.cos(ang), np.sin(ang)
    return (np.concatenate([cos] * 4).astype(np.float32),
            np.concatenate([-sin, sin] * 2).astype(np.float32))


def kernel(**inputs):
    import concourse.bacc as _bacc
    from concourse.bass_utils import run_bass_kernel_spmd as _run

    nc = _bacc.Bacc("TRN2", target_bir_lowering=False, num_devices=1)
    arrays, args = {}, []
    for name in _INS:
        a = np.ascontiguousarray(inputs[name])
        arrays[f"in_{name}_dram"] = a
        args.append(nc.dram_tensor(f"in_{name}_dram", a.shape, mybir.dt.from_np(a.dtype), kind="ExternalInput").ap())
    for name, a in zip(("rope_cos", "rope_sin"), rope_tables()):
        arrays[f"in_{name}_dram"] = a
        args.append(nc.dram_tensor(f"in_{name}_dram", a.shape, mybir.dt.from_np(a.dtype), kind="ExternalInput").ap())
    args.append(nc.dram_tensor("out_0_dram", (1, T, D), F32, kind="ExternalOutput").ap())
    bass_trunk(nc, *args)
    r = _run(nc, [arrays], core_ids=[0])
    return r.results[0]["out_0_dram"]
```

```python
from contextlib import ExitStack

import numpy as np

import concourse.bass as bass
from concourse import mybir

F32 = mybir.dt.float32
F32R = mybir.dt.float32r
ALU = mybir.AluOpType
ACT = mybir.ActivationFunctionType
AX_X = mybir.AxisListType.X

P = 128
T = 512
D = 1024
DEPTH = 2
HD = 64
HEADS = 16
PAIRS = HEADS // 2
GROUPS = 2
KT = D // P
QT = T // P
CMP_BLOCK, CMP_STRIDE = 32, 16
N_CMP = (T - CMP_BLOCK) // CMP_STRIDE + 1
N_PAD = 32
CJ = CMP_BLOCK // 2
NEG = -1.0e30
BIG = 3.0e38
SCALE = HD ** -0.5
EPS = 1e-6

C_QA = 0
C_KV = C_QA + D
C_G = C_KV + 3 * 2 * GROUPS * HD
C_ZA = C_G + 3 * HEADS
C_QB = C_ZA + D
C_KB = C_QB + D
C_VB = C_KB + D
C_F = C_VB + D
C_ZB = C_F + HEADS
C_RA = C_ZB + D
C_RB = C_RA + D
IN_COLS = C_RB + D
KV_UNITS = [(C_KV + 2 * P, P), (C_KV + 4 * P, P), (C_KV + 3 * P, P), (C_KV + 5 * P, P),
            (C_KV, P), (C_KV + P, P), (C_G, 3 * HEADS), (C_F, HEADS)]

U_NSA, U_FOX, U_MERGE, U_OUT, U_ALL = 8, 24, 56, 88, 96
S_FOX, S_ALL = 4 * 4 * PAIRS, 4 * 4 * PAIRS + 4 * 2 * PAIRS
A_FOX, A_ALL = 4 * PAIRS, 6 * PAIRS
SM_RING = 4
LAG_SCALE, LAG_TURN, LAG_PT, LAG_PV = 1, 2, 3, 4
PT_COLS = 3 * 384 + T


def spread(total, busy):
    level = 0.0
    while sum(max(0.0, level - b) for b in busy) < total:
        level += 0.05
    cum, done = [], 0.0
    for b in busy:
        done += max(0.0, level - b)
        cum.append(min(total, int(done)))
    cum[-1] = total
    return cum


class Body:

    def __init__(self, att, proj):
        self.att, self.proj = att, proj
        self.steps = 0 if att is None else (16 if att.nsa else 8)
        self.slots = self.steps + LAG_PT if att is not None else (8 if proj.nsa else 16)
        n = 0 if proj is None else (2 if proj.nsa else 4)
        busy = [0.0] * self.slots
        for s in range(self.steps):
            q = s % QT
            busy[max(0, s - 1)] += (1.0, 1.0, 1.5, 2.0)[q] * (1 if att.nsa else 1.5)
            busy[s + LAG_TURN] += 0.5 * (q + 1)
        for a in range(self.steps // QT):
            busy[min(self.slots - 1, QT * a + QT - 1 + LAG_PV)] += 9.0
        self.cum = spread(24 * n, busy)
        self.begin, self.end = {}, {}
        for u in range(n):
            first = next(s for s in range(self.slots) if self.cum[s] > 24 * u)
            last = next(s for s in range(self.slots) if self.cum[s] >= 24 * u + 24)
            self.begin.setdefault(first, []).append(u)
            self.end[u] = last
        self.n_units = n

    def at_end(self, part, lag):
        return min(self.end[part] + lag, self.slots + lag)


class Pair:

    def __init__(self, nsa, l, i, parity, group=0, first=False):
        self.first = first
        self.nsa, self.l, self.i, self.b, self.g = nsa, l, i, parity, group
        if nsa:
            self.half = l * (U_ALL // 2) + U_NSA // 2 + i
            self.s0 = l * S_ALL + 16 * i
            self.a0 = l * A_ALL + 4 * i
            self.r = l * (2 * PAIRS) + i
        else:
            self.half = l * (U_ALL // 2) + U_FOX // 2 + 2 * i
            self.s0 = l * S_ALL + S_FOX + 8 * i
            self.a0 = l * A_ALL + A_FOX + 2 * i
            self.r = l * (2 * PAIRS) + PAIRS + i

    def unit(self, part):
        return self.half + part // 2, part % 2

    def atts(self):
        if self.nsa:
            return [(h, self.g, s, 1 + s) for h in range(2) for s in range(2)]
        return [(h, self.b, h, None) for h in (1, 0)]


def bass_trunk(nc, x, norm_g, w_in, b_forget, pe_k, w1_k, w2_k, pe_v, w1_v, w2_v, w_nsa, w_fox,
               w_out, final_g, rope_c, rope_s, out):
    ctx = ExitStack()
    with ctx:
        scope = [ctx]

        def sb(name, shape, dt=F32):
            return scope[-1].enter_context(nc.sbuf_tensor(name, shape, dt))

        def psum(name, shape):
            return ctx.enter_context(nc.psum_tensor(name, shape, F32))

        def sem(name):
            return ctx.enter_context(nc.semaphore(name))

        h_hi = sb("h_hi", [P, KT, T], F32R)
        h_lo = sb("h_lo", [P, KT, T], F32R)
        w_raw = sb("w_raw", [P, 2, KT, P])
        w_hi = sb("w_hi", [P, 2, KT, P], F32R)
        w_lo = sb("w_lo", [P, 2, KT, P], F32R)
        cosT = sb("cosT", [P, T])
        sinT = sb("sinT", [P, T])
        causal = sb("causal", [P, T])
        cmp_mask = sb("cmp_mask", [P, QT, 2, N_PAD])
        ident = sb("ident", [P, P])
        ones = sb("ones", [P, P])
        sel_f = sb("sel_f", [36, 2, P])
        sel = sb("sel", [36, 2, P], F32R)
        past_first = sb("past_first", [P, 1])
        gains = sb("gains", [P, DEPTH + 1, KT])
        b_f = sb("b_f", [HEADS, DEPTH])
        gates = sb("gates", [P, QT, 3 * HEADS])
        kcb = sb("kcb", [P, GROUPS, 2 * N_PAD])
        vcb = sb("vcb", [2 * N_PAD, GROUPS, P])
        pool_note = sb("pool_note", [P, 1])
        row_max = sb("row_max", [P, SM_RING])
        row_sum = sb("row_sum", [P, SM_RING])
        row_inv = sb("row_inv", [P, SM_RING])
        with ExitStack() as own_place:
            scope.append(own_place)
            y_all = [sb(f"y_all{n}", [P, PAIRS, T]) for n in range(2)]
            scope.pop()
        with ExitStack() as own_place:
            scope.append(own_place)
            m_hi = sb("m_hi", [P, KT, T], F32R)
            m_lo = sb("m_lo", [P, KT, T], F32R)
            scope.pop()
        sb("place_of_y_and_m", [P, 2, KT, T])

        with ExitStack() as own_place:
            scope.append(own_place)
            xT = sb("xT", [P, KT, T])
            scope.pop()
        with ExitStack() as own:
            scope.append(own)
            v_hi = sb("v_hi", [P, 2, 2, QT, 2 * HD], F32R)
            v_lo = sb("v_lo", [P, 2, 2, QT, 2 * HD], F32R)
            pt_hi = sb("pt_hi", [P, 2, PT_COLS], F32R)
            pt_lo = sb("pt_lo", [P, 2, PT_COLS], F32R)
            prob = sb("prob", [P, SM_RING, T])
            q_st = sb("q_st", [P, 2, 2, T], F32R)
            kk_hi = sb("kk_hi", [P, 2, 2, T], F32R)
            kk_lo = sb("kk_lo", [P, 2, 2, T], F32R)
            f_row = sb("f_row", [36, T], F32R)
            q_raw = sb("q_raw", [P, T])
            q_swap = sb("q_swap", [P, T])
            q_rope = sb("q_rope", [P, T])
            z_silu = sb("z_silu", [P, 2, T])
            pc = sb("pc", [P, 2 * QT, N_PAD])
            pc_t = sb("pc_t", [2 * N_PAD, T])
            pc_max = sb("pc_max", [P, 2 * QT])
            pc_sum = sb("pc_sum", [P, 2 * QT])
            pc_inv = sb("pc_inv", [P, 2 * QT])
            scope.pop()
        with ExitStack() as own:
            scope.append(own)
            sb("place_of_x_squares", [P, KT, T])
            squares = sb("squares", [P, 2, T])
            rstd = sb("rstd", [P, T])
            h_raw = sb("h_raw", [P, 2, T])
            c_w1 = sb("c_w1", [P, 2, CJ, P])
            c_w2 = sb("c_w2", [P, 2, HD])
            c_pe = sb("c_pe", [P, 2, CJ])
            c_src = sb("c_src", [P, 2, GROUPS, T // 2])
            c_blk = sb("c_blk", [P, 2, CJ, GROUPS, N_PAD])
            c_th = sb("c_th", [P, 2, GROUPS * N_PAD])
            c_hid = sb("c_hid", [P, 2, GROUPS * N_PAD])
            scope.pop()
        with ExitStack() as own:
            scope.append(own)
            sb("place_of_x_g_th", [P, KT, T])
            g_th = sb("g_th", [3 * HEADS, T])
            f_a = sb("f_a", [HEADS, T])
            f_b = sb("f_b", [HEADS, T])
            f_hi = sb("f_hi", [HEADS, T], F32R)
            f_lo = sb("f_lo", [HEADS, T], F32R)
            scope.pop()
        with ExitStack() as own:
            scope.append(own)
            sb("place_of_x_yt_hi", [P, KT, T])
            yt_hi = sb("yt_hi", [P, 2, KT, T], F32R)
            yt_lo = sb("yt_lo", [P, 2, KT, T], F32R)
            m_th = sb("m_th", [P, 2, T])
            m_sum = sb("m_sum", [P, 2, T])
            scope.pop()
        with ExitStack() as own:
            scope.append(own)
            sb("place_of_x_clear", [P, KT, T])
            sb("place_of_norm", [P, 5, T])
            o_t = sb("o_t", [P, KT, T])
            o_nat = sb("o_nat", [P, QT, D])
            x_nat = sb("x_nat", [P, QT, D])
            scope.pop()

        x_dram = nc.dram_tensor("x_scratch", [P, KT, T], F32, kind="Internal").ap()
        f_dram = nc.dram_tensor("f_scratch", [HEADS, 2, T], F32R, kind="Internal").ap()

        acc = [psum(f"acc{n}", [P, T]) for n in range(2)]
        scores = [psum(f"scores{n}", [P, T]) for n in range(2)]
        turned = [psum(f"turned{n}", [P, T]) for n in range(2)]
        o_pair = psum("o_pair", [P, T])
        misc = psum("misc", [P, T])

        consts = sem("consts")
        consts_dma = sem("consts_dma")
        x_landed = sem("x_landed")
        x_turned = sem("x_turned")
        x_done = sem("x_done")
        x_saved = sem("x_saved")
        x_back = sem("x_back")
        w_landed = [sem(f"w_landed{n}") for n in range(2)]
        w_hi_done = sem("w_hi_done")
        w_lo_done = sem("w_lo_done")
        unit_mm = sem("unit_mm")
        sq_done = sem("sq_done")
        sq_used = sem("sq_used")
        var_done = sem("var_done")
        std_done = sem("std_done")
        rstd_done = sem("rstd_done")
        h_raw_done = sem("h_raw_done")
        h_hi_done = sem("h_hi_done")
        h_lo_done = sem("h_lo_done")
        pads = sem("pads")
        raw_done = sem("raw_done")
        swap_done = sem("swap_done")
        rope_parts = sem("rope_parts")
        rope_done = sem("rope_done")
        part_hi_done = sem("part_hi_done")
        part_lo_done = sem("part_lo_done")
        v_raw_done = sem("v_raw_done")
        v_turned = sem("v_turned")
        v_hi_done = sem("v_hi_done")
        v_lo_done = sem("v_lo_done")
        c_landed = sem("c_landed")
        c_src_done = sem("c_src_done")
        c_blk_done = sem("c_blk_done")
        c_hid_mm = sem("c_hid_mm")
        c_th_done = sem("c_th_done")
        c_hid_done = sem("c_hid_done")
        c_out_mm = sem("c_out_mm")
        cb_ready = sem("cb_ready")
        g_th_done = sem("g_th_done")
        g_turned = sem("g_turned")
        gates_done = sem("gates_done")
        f_step = sem("f_step")
        f_exp = sem("f_exp")
        f_saved = sem("f_saved")
        f_landed = sem("f_landed")
        s_mm = sem("s_mm")
        s_max = sem("s_max")
        s_exp = sem("s_exp")
        s_inv = sem("s_inv")
        s_scaled = sem("s_scaled")
        s_turned = sem("s_turned")
        pt_hi_done = sem("pt_hi_done")
        pt_lo_done = sem("pt_lo_done")
        pv_mm = sem("pv_mm")
        cmp_s = sem("cmp_s")
        cmp_dve = sem("cmp_dve")
        cmp_exp = sem("cmp_exp")
        cmp_turned = sem("cmp_turned")
        cmp_pt = sem("cmp_pt")
        z_th_done = sem("z_th_done")
        z_done = sem("z_done")
        sel_done = sem("sel_done")
        y_mul = sem("y_mul")
        yt_hi_done = sem("yt_hi_done")
        yt_lo_done = sem("yt_lo_done")
        m_th_done = sem("m_th_done")
        m_part = sem("m_part")
        m_sum_done = sem("m_sum_done")
        m_hi_done = sem("m_hi_done")
        m_lo_done = sem("m_lo_done")
        o_turned = sem("o_turned")
        o_copied = [sem(f"o_copied{n}") for n in range(2)]
        o_stored = sem("o_stored")

        w_view = w_in.rearrange("l (k p) c -> p l k c", p=P)
        wn_view = w_nsa.rearrange("l (k p) c -> p l k c", p=P)
        wf_view = w_fox.rearrange("l (k p) c -> p l k c", p=P)
        wo_view = w_out.rearrange("l (k p) c -> p l k c", p=P)

        kv_widths = [w for _, w in KV_UNITS]
        N_CONSTS = 14

        def apart(eng):
            eng.nop(nofuse=True)

        def key_cols(qt):
            return max(P * (qt + 1), 2 * P)

        def bodies(eng, l, body):
            body(l, None, Pair(True, l, 0, 0, first=True))
            with eng.Fori(0, 2) as j:
                body(l, Pair(True, l, 2 * j, 0, 0), Pair(True, l, 2 * j + 1, 1))
                body(l, Pair(True, l, 2 * j + 1, 1, 0), Pair(True, l, 2 * j + 2, 0))
            for i in range(4, 7):
                body(l, Pair(True, l, i, i % 2, 1), Pair(True, l, i + 1, (i + 1) % 2))
            body(l, Pair(True, l, 7, 1, 1), Pair(False, l, 0, 0, first=True))
            with eng.Fori(0, 3) as j:
                body(l, Pair(False, l, 2 * j, 0), Pair(False, l, 2 * j + 1, 1))
                body(l, Pair(False, l, 2 * j + 1, 1), Pair(False, l, 2 * j + 2, 0))
            body(l, Pair(False, l, 6, 0), Pair(False, l, 7, 1))
            body(l, Pair(False, l, 7, 1), None)

        def own(h):
            return slice(HD * h, HD * h + HD)

        def other(h):
            return own(1 - h)

        def pt_tiles(pt, a, qt):
            first = P * qt
            return pt[:, a % 2, first:first + 384 * qt + P] if qt == 0 else \
                strided(pt, a % 2, first, qt + 1)

        def strided(pt, half, first, n):
            whole = pt[:, half, first:first + 384 * (n - 1) + P]
            ap = pt[:, half, first:first + 384 * n] if first + 384 * n <= PT_COLS else None
            if ap is not None:
                return ap.rearrange("p (k c) -> p k c", k=n)[:, :, 0:P]
            early = first - 256
            return pt[:, half, early:early + 384 * n].rearrange("p (k c) -> p k c", k=n)[:, :, 256:384]

        def turned_tiles(s, qt):
            bank = turned[s % 2][:, 0:P * (qt + 1)]
            return bank if qt == 0 else bank.rearrange("p (k c) -> p k c", k=qt + 1)

        block = ctx.enter_context(nc.Block())

        @block.sync
        def _(sp):
            def load(src, l, col, width, half, par, first=False):
                sp.wait_ge(w_lo_done, 2 * half + par + 1)
                sp.dma_start(w_raw[:, par:par + 1, :, 0:width],
                             src[:, bass.ds(l, 1), :, bass.ds(col, width)]).then_inc(w_landed[par], 16)

            sp.dma_start(x_nat[:, :, :], x[0].rearrange("(i p) d -> p i d", p=P)).then_inc(x_landed, 16)
            with sp.Fori(0, DEPTH) as l:
                base = l * (U_ALL // 2)
                for n, (col, width) in enumerate(KV_UNITS):
                    load(w_view, l, col, width, base + n // 2, n % 2)
                with sp.Fori(0, PAIRS) as i:
                    half = base + U_NSA // 2 + i
                    load(w_view, l, C_QA + P * i, P, half, 0)
                    load(w_view, l, C_ZA + P * i, P, half, 1)
                with sp.Fori(0, PAIRS) as i:
                    half = base + U_FOX // 2 + 2 * i
                    load(w_view, l, C_QB + P * i, P, half, 0)
                    load(w_view, l, C_KB + P * i, P, half, 1)
                    load(w_view, l, C_VB + P * i, P, half + 1, 0)
                    load(w_view, l, C_ZB + P * i, P, half + 1, 1)
                with sp.Fori(0, KT) as e:
                    half = base + U_MERGE // 2 + 2 * e
                    load(w_view, l, C_RA + P * e, P, half, 0)
                    load(w_view, l, C_RB + P * e, P, half, 1)
                    load(wn_view, l, P * e, P, half + 1, 0)
                    load(wf_view, l, P * e, P, half + 1, 1)
                with sp.Fori(0, KT // 2) as j:
                    half = base + U_OUT // 2 + j
                    load(wo_view, l, 2 * P * j, P, half, 0)
                    load(wo_view, l, 2 * P * j + P, P, half, 1)
            for i in range(QT):
                for n in range(2):
                    sp.wait_ge(o_copied[n], i + 1)
                sp.dma_start(out[0, i * P:(i + 1) * P, :], o_nat[:, i, :]).then_inc(o_stored, 16)
            sp.wait_ge(o_stored, 16 * QT)

        @block.gpsimd
        def _(pool):
            pool.memset(ident[:, :], 0.0).then_inc(consts, 1)
            pool.memset(ones[:, :], 1.0).then_inc(consts, 1)
            pool.memset(causal[:, :], 0.0).then_inc(consts, 1)
            pool.memset(cmp_mask[:, :, :, :], 0.0).then_inc(consts, 1)
            pool.memset(sel_f[:, :, :], 1.0).then_inc(consts, 1)
            pool.memset(past_first[:, :], 1.0).then_inc(consts, 1)
            pool.wait_ge(consts, 6)
            pool.affine_select(out=ident[:, :], in_=ident[:, :], compare_op=ALU.not_equal, fill=1.0,
                               base=0, pattern=[[-1, P]], channel_multiplier=1).then_inc(consts, 1)
            tri = causal[:, T - P:T]
            pool.affine_select(out=tri, in_=tri, compare_op=ALU.is_ge, fill=NEG, base=0,
                               pattern=[[-1, P]], channel_multiplier=1).then_inc(consts, 1)
            pool.affine_select(out=cmp_mask[:, :, :, :], in_=cmp_mask[:, :, :, :], compare_op=ALU.is_ge,
                               fill=NEG, base=1 - CMP_BLOCK,
                               pattern=[[P, QT], [0, 2], [-CMP_STRIDE, N_PAD]],
                               channel_multiplier=1).then_inc(consts, 1)
            for b in range(2):
                rows = sel_f[32 * b:32 * b + 4]
                pool.wait_ge(consts, 9 + 2 * b)
                pool.affine_select(out=rows[:, 0, :], in_=rows[:, 0, :], compare_op=ALU.is_ge, fill=0.0,
                                   base=1, pattern=[[0, P]], channel_multiplier=-1).then_inc(consts, 1)
                pool.affine_select(out=rows[:, 1, :], in_=rows[:, 1, :], compare_op=ALU.is_ge, fill=0.0,
                                   base=-2, pattern=[[0, P]], channel_multiplier=1).then_inc(consts, 1)
            pool.wait_ge(consts, 13)
            pool.affine_select(out=past_first[:, :], in_=past_first[:, :], compare_op=ALU.is_ge, fill=0.0,
                               base=1 - CMP_BLOCK, pattern=[[0, 1]],
                               channel_multiplier=1).then_inc(consts, 1)
            pool.memset(kcb[:, :, :], 0.0).then_inc(pads, 1)
            pool.memset(vcb[:, :, :], 0.0).then_inc(pads, 1)

            def rotate(l, n):
                c = l * 10 + n
                pool.wait_ge(raw_done, c + 1)
                apart(pool)
                if not (isinstance(n, int) and n == 0):
                    pool.wait_ge(part_lo_done, l * 26 + n)
                    apart(pool)
                pool.tensor_tensor(q_rope[:, :], q_raw[:, :], cosT[:, :], ALU.mult).then_inc(rope_parts, 1)
                pool.wait_ge(swap_done, c + 1)
                apart(pool)
                pool.tensor_tensor(q_swap[:, :], q_swap[:, :], sinT[:, :], ALU.mult).then_inc(rope_parts, 1)
                pool.wait_ge(rope_parts, 2 * (c + 1))
                apart(pool)
                pool.tensor_tensor(q_rope[:, :], q_rope[:, :], q_swap[:, :], ALU.add).then_inc(rope_done, 1)

            def body(l, att, proj):
                if proj is not None and proj.nsa:
                    rotate(l, 2 + proj.i)
                elif proj is not None:
                    pool.wait_ge(f_saved, 32 * (l + 1))
                    pool.wait_ge(s_mm, att.s0 + 1)
                    apart(pool)
                    pool.dma_start(f_row[32 * proj.b:32 * proj.b + 4, :],
                                   f_dram[bass.ds(2 * proj.i, 2)].rearrange("h a t -> (h a) t")
                                   ).then_inc(f_landed, 16)

            with pool.Fori(0, DEPTH) as l:
                pool.wait_ge(x_done, KT * (l + 1))
                apart(pool)
                pool.dma_start(x_dram, xT[:, :, :]).then_inc(x_saved, 16)
                pool.wait_ge(h_lo_done, KT * (l + 1))
                apart(pool)
                pool.wait_ge(x_saved, 16 * (l + 1))
                apart(pool)
                for v in (v_hi, v_lo):
                    flat = v[:, :, :, :, :].rearrange("p b s k c -> p (b s k) c")
                    pool.memset(flat[:, :, 0:HD].bitcast(F32), 0.0).then_inc(pads, 1)
                pool.memset(c_blk[:, :, :, :, N_CMP:N_PAD].rearrange("p a j g n -> p (a j g) n"),
                            0.0).then_inc(pads, 1)
                for s in range(2):
                    rotate(l, s)
                pool.wait_ge(f_step, 6 * (l + 1))
                apart(pool)
                pool.dma_start(f_dram[:, 0, :], f_hi[:, :]).then_inc(f_saved, 16)
                pool.dma_start(f_dram[:, 1, :], f_lo[:, :]).then_inc(f_saved, 16)
                pool.wait_ge(f_saved, 32 * (l + 1))
                pool.wait_ge(c_out_mm, 2 * (l + 1))
                apart(pool)
                for pt in (pt_hi, pt_lo):
                    pool.memset(pt[:, :, 3 * 384 + 2 * P:3 * 384 + 3 * P].bitcast(F32), 0.0).then_inc(pads, 1)
                bodies(pool, l, body)
                pool.wait_ge(y_mul, 2 * PAIRS * (l + 1) + 2)
                apart(pool)
                pool.dma_start(xT[:, :, :], x_dram).then_inc(x_back, 16)

        @block.scalar
        def _(act):
            def split_hi(half, par, width=P, wait=True):
                act.wait_ge(w_landed[par], 16 * (half + 1))
                if wait:
                    act.wait_ge(unit_mm, 2 * half + par - 1)
                act.activation(w_hi[:, par, :, 0:width], w_raw[:, par, :, 0:width],
                               ACT.Copy).then_inc(w_hi_done, 1)

            def norm(n, between=None, final=False):
                for k in range(KT):
                    act.wait_ge(x_done, KT * n + k + 1)
                    if k >= 2:
                        act.wait_ge(sq_used, KT * n + k - 1)
                    act.activation(squares[:, k % 2, :], xT[:, k, :], ACT.Square).then_inc(sq_done, 1)
                if between is not None:
                    between()
                act.wait_ge(var_done, n + 1)
                act.activation(rstd[:, :], rstd[:, :], ACT.Sqrt).then_inc(std_done, 1)
                if final:
                    return
                for k in range(KT):
                    act.wait_ge(h_raw_done, KT * n + k + 1)
                    act.activation(h_hi[:, k, :], h_raw[:, k % 2, :], ACT.Copy).then_inc(h_hi_done, 1)

            def raw_copy(half, par, c, waits, c_prev=True):
                act.wait_ge(unit_mm, 2 * half + par + 1)
                for s, value in waits:
                    act.wait_ge(s, value)
                act.activation(q_raw[:, :], acc[par][:, :], ACT.Copy).then_inc(raw_done, 1)
                if c_prev:
                    act.wait_ge(rope_done, c)
                for n in range(4):
                    to = 32 * (n ^ 1)
                    ins = act.activation(q_swap[to:to + 32, :], acc[par][32 * n:32 * n + 32, :], ACT.Copy)
                ins.then_inc(swap_done, 1)

            def q_round(src, b, waits):
                for s, value in waits:
                    act.wait_ge(s, value)
                for h in range(2):
                    ins = act.activation(q_st[own(h), b, h, :], src[own(h), :], ACT.Copy)
                ins.then_inc(part_hi_done, 1)

            def k_round(src, places, waits):
                for s, value in waits:
                    act.wait_ge(s, value)
                for h, (b, stream) in enumerate(places):
                    for rows in (own(h), other(h)):
                        ins = act.activation(kk_hi[rows, b, stream, :], src[own(h), :], ACT.Copy)
                ins.then_inc(part_hi_done, 1)

            def v_copy(half, par, waits):
                act.wait_ge(unit_mm, 2 * half + par + 1)
                for s, value in waits:
                    act.wait_ge(s, value)
                act.activation(q_raw[:, :], acc[par][:, :], ACT.Copy).then_inc(v_raw_done, 1)

            def v_round(n, to):
                act.wait_ge(v_turned, n + 1)
                act.activation(to, misc[:, :].rearrange("p (k s d) -> p s k d", k=QT, s=2),
                               ACT.Copy).then_inc(v_hi_done, 1)

            def z_tanh_of(half, par, r, b):
                act.wait_ge(unit_mm, 2 * half + par + 1)
                act.wait_ge(y_mul, r + 1)
                act.activation(z_silu[:, b, :], acc[par][:, :], ACT.Tanh, scale=0.5).then_inc(z_th_done, 1)

            def body(l, att, proj):
                plan = Body(att, proj)
                todo = {}

                def at(slot, what):
                    todo.setdefault(slot, []).append(what)

                if proj is not None:
                    for slot, units in plan.begin.items():
                        for u in units:
                            nxt = proj.unit(u + 1)
                            at(slot, lambda nxt=nxt: split_hi(*nxt))
                    if proj.nsa:
                        c = l * 10 + 2 + proj.i
                        first = att is None
                        raw_waits = [(v_turned, l * 10 + 2)] if first else [(cmp_s, att.l * PAIRS + att.i + 1)]
                        q_waits = [(rope_done, c + 1)] + ([] if first else [(s_mm, att.s0 + 1)])
                        at(plan.at_end(0, 1), lambda: raw_copy(*proj.unit(0), c, raw_waits))
                        at(plan.at_end(0, 6), lambda: q_round(q_rope, proj.b, q_waits))
                        at(plan.at_end(1, 1), lambda: z_tanh_of(*proj.unit(1), proj.r, proj.b))
                    else:
                        n = l * 10 + 2 + proj.i
                        q_waits = [(unit_mm, 2 * proj.half + 1), (s_mm, att.s0 + 1)]
                        k_waits = [(unit_mm, 2 * proj.half + 2)]
                        places = [(proj.b, 0), (proj.b, 1)]
                        v_waits = [(cmp_s, PAIRS * (l + 1))] if att.nsa else [(v_turned, n)]
                        at(plan.at_end(0, 1), lambda: q_round(acc[0], proj.b, q_waits))
                        at(plan.at_end(1, 1), lambda: k_round(acc[1], places, k_waits))
                        at(plan.at_end(2, 1), lambda: v_copy(*proj.unit(2), v_waits))
                        at(plan.at_end(2, 2), lambda: v_round(n, v_hi[:, proj.b, :, :, HD:2 * HD]))
                        at(plan.at_end(3, 1), lambda: z_tanh_of(*proj.unit(3), proj.r, proj.b))

                def exp_step(s):
                    t = att.s0 + s
                    ring, width = s % SM_RING, P * (s % QT + 1)
                    act.wait_ge(s_max, t + 1)
                    act.activation(prob[:, ring, 0:width], prob[:, ring, 0:width], ACT.Exp,
                                   bias=row_max[:, ring:ring + 1], scale=-1.0,
                                   accum_out=row_sum[:, ring:ring + 1]).then_inc(s_exp, 1)

                def hi_step(s):
                    a, qt = divmod(s, QT)
                    act.wait_ge(s_turned, att.s0 + s + 1)
                    if qt == 0 and a >= 2:
                        act.wait_ge(pv_mm, att.a0 + a - 1)
                    act.activation(pt_tiles(pt_hi, a, qt), turned_tiles(s, qt), ACT.Copy)\
                        .then_inc(pt_hi_done, 1)

                if att is not None and att.nsa:
                    m = att.l * PAIRS + att.i

                    def cmp_exponent():
                        act.wait_ge(cmp_dve, 7 * m + 3)
                        act.activation(pc[:, :, :], pc[:, :, :], ACT.Exp, scale=SCALE).then_inc(cmp_exp, 1)

                    def cmp_copy():
                        act.wait_ge(cmp_turned, m + 1)
                        act.activation(pc_t[:, :], misc[0:2 * N_PAD, :], ACT.Copy).then_inc(cmp_pt, 1)

                    at(2, cmp_exponent)
                    at(4, cmp_copy)

                last = max([plan.slots] + [k + 1 for k in todo])
                for s in range(last):
                    if s < plan.steps:
                        exp_step(s)
                    if 2 <= s < plan.steps + 2:
                        hi_step(s - 2)
                    for what in todo.get(s, []):
                        what()

            for n, (to, src) in enumerate(((cosT[:, :], rope_c), (sinT[:, :], rope_s))):
                act.dma_start(to, src).then_inc(consts_dma, 16)
            with nc.allow_non_contiguous_dma(reason="a few kB of per-channel constants"):
                for l in range(DEPTH):
                    act.dma_start(gains[:, l, :], norm_g[l].rearrange("(k p) -> p k", p=P)).then_inc(consts_dma, 16)
                act.dma_start(gains[:, DEPTH, :], final_g.rearrange("(k p) -> p k", p=P)).then_inc(consts_dma, 16)
                act.dma_start(b_f[:, :], b_forget.rearrange("l h -> h l")).then_inc(consts_dma, 16)

            with act.Fori(0, DEPTH) as l:
                half0 = l * (U_ALL // 2)
                norm(l, between=lambda: split_hi(half0, 0, kv_widths[0], wait=False))
                for a, w1, w2, pe in ((0, w1_k, w2_k, pe_k), (1, w1_v, w2_v, pe_v)):
                    for j in (slice(0, CJ // 2), slice(CJ // 2, CJ)):
                        act.dma_start(c_w1[:, a:a + 1, j, :],
                                      w1.rearrange("l (j p) h -> p l j h", p=P)[:, bass.ds(l, 1), j]
                                      ).then_inc(c_landed, 16)
                    act.dma_start(c_w2[:, a:a + 1, :],
                                  w2.rearrange("l h d -> h l d")[:, bass.ds(l, 1)]).then_inc(c_landed, 16)
                    with nc.allow_non_contiguous_dma(reason="8 kB of position vectors, transposed"):
                        for par in range(2):
                            act.dma_start(c_pe[HD * par:HD * par + HD, a:a + 1, :],
                                          pe.rearrange("l (j a) d -> a d l j", a=2)[par][:, bass.ds(l, 1)]
                                          ).then_inc(c_landed, 16)

                def kv(n):
                    return half0 + n // 2, n % 2

                split_hi(*kv(1), kv_widths[1], wait=False)
                split_hi(*kv(2), kv_widths[2])
                raw_copy(*kv(0), l * 10, [], c_prev=False)
                split_hi(*kv(3), kv_widths[3])
                k_round(q_rope, [(0, 0), (1, 0)], [(rope_done, l * 10 + 1)])
                raw_copy(*kv(1), l * 10 + 1, [(rope_done, l * 10 + 1)])
                split_hi(*kv(4), kv_widths[4])
                k_round(q_rope, [(0, 1), (1, 1)], [(rope_done, l * 10 + 2)])
                v_copy(*kv(2), [(rope_done, l * 10 + 2), (x_saved, 16 * (l + 1))])
                split_hi(*kv(5), kv_widths[5])
                v_round(l * 10, v_hi[:, :, 0, :, HD:2 * HD])
                v_copy(*kv(3), [(v_turned, l * 10 + 1)])
                split_hi(*kv(6), kv_widths[6])
                v_round(l * 10 + 1, v_hi[:, :, 1, :, HD:2 * HD])
                for a in range(2):
                    half, par_u = kv(4 + a)
                    act.wait_ge(unit_mm, 2 * half + par_u + 1)
                    for g in range(GROUPS):
                        for par in range(2):
                            src = acc[par_u][HD * g:HD * g + HD, :].rearrange("d (m a) -> d a m", a=2)
                            ins = act.activation(c_src[HD * par:HD * par + HD, a, g, :], src[:, par, :], ACT.Copy)
                    ins.then_inc(c_src_done, 1)
                    if a == 0:
                        split_hi(*kv(7), kv_widths[7])
                split_hi(*kv(8))
                half, par = kv(6)
                act.wait_ge(unit_mm, 2 * half + par + 1)
                act.activation(g_th[:, :], acc[par][0:3 * HEADS, :], ACT.Tanh, scale=0.5)\
                    .then_inc(g_th_done, 1)
                for a in range(2):
                    act.wait_ge(c_hid_mm, 2 * l + a + 1)
                    act.activation(c_th[:, a, :], turned[a][:, 0:GROUPS * N_PAD], ACT.Tanh, scale=0.5)\
                        .then_inc(c_th_done, 1)
                act.wait_ge(f_step, 6 * l + 2)
                act.activation(f_b[:, :], f_b[:, :], ACT.Exp, scale=-1.0).then_inc(f_exp, 1)
                act.wait_ge(f_exp, 3 * l + 1)
                act.activation(f_b[:, :], f_b[:, :], ACT.Ln, bias=1.0).then_inc(f_exp, 1)
                act.wait_ge(f_step, 6 * l + 5)
                act.activation(f_hi[:, :], f_b[:, :], ACT.Copy).then_inc(f_exp, 1)

                bodies(act, l, body)

                act.wait_ge(y_mul, 2 * PAIRS * (l + 1) + 2)
                for mixer in range(2):
                    for k in range(0, KT, 2):
                        act.activation(yt_hi[:, mixer, k:k + 2, :], y_all[mixer][:, k:k + 2, :],
                                       ACT.Copy).then_inc(yt_hi_done, 1)

                def merge_tile(e):
                    half = half0 + U_MERGE // 2 + 2 * e
                    for par in range(2):
                        split_hi(half + par, 1 - par)
                        act.wait_ge(unit_mm, 2 * half + par + 1)
                        act.activation(m_th[:, par, :], acc[par][:, :], ACT.Tanh, scale=0.5)\
                            .then_inc(m_th_done, 1)
                    split_hi(half + 1, 1)
                    split_hi(half + 2, 0)
                    act.wait_ge(m_sum_done, KT * l + e + 1)
                    act.activation(m_hi[:, bass.ds(e, 1), :], m_sum[:, 0:1, :], ACT.Copy, scale=0.5)\
                        .then_inc(m_hi_done, 1)

                with act.Fori(0, KT) as e:
                    merge_tile(e)
                with act.Fori(0, KT // 2 - 1) as j:
                    split_hi(half0 + U_OUT // 2 + j, 1)
                    split_hi(half0 + U_OUT // 2 + j + 1, 0)
                split_hi(half0 + U_OUT // 2 + KT // 2 - 1, 1)
            norm(DEPTH, final=True)
            for n in range(2 * QT):
                if n % 2:
                    act.wait_ge(o_turned, n + 1)
                    act.activation(o_nat[:, n // 2, 512:1024], turned[1][:, :], ACT.Copy).then_inc(o_copied[1], 1)

        @block.vector
        def _(dve):
            def split_lo(half, par, width=P):
                dve.wait_ge(w_hi_done, 2 * half + par + 1)
                dve.tensor_tensor(w_lo[:, par, :, 0:width], w_raw[:, par, :, 0:width],
                                  w_hi[:, par, :, 0:width], ALU.subtract).then_inc(w_lo_done, 1)

            def norm(n, between=None, final=False):
                dve.wait_ge(sq_used, KT * (n + 1))
                dve.tensor_scalar(rstd[:, :], misc[:, :], 1.0 / D, EPS, ALU.mult, ALU.add).then_inc(var_done, 1)
                if between is not None:
                    between()
                dve.wait_ge(std_done, n + 1)
                dve.reciprocal(rstd[:, :], rstd[:, :]).then_inc(rstd_done, 1)
                dve.wait_ge(rstd_done, n + 1)

                def raw(k):
                    if k >= 2 and not final:
                        dve.wait_ge(h_lo_done, KT * n + k - 1)
                    to = o_t[:, k, :] if final else h_raw[:, k % 2, :]
                    gain = gains[:, DEPTH, k:k + 1] if final else gains[:, bass.ds(n, 1), k]
                    dve.scalar_tensor_tensor(to, xT[:, k, :], gain, rstd[:, :],
                                             ALU.mult, ALU.mult).then_inc(h_raw_done, 1)

                def remainder(k):
                    dve.wait_ge(h_hi_done, KT * n + k + 1)
                    dve.tensor_tensor(h_lo[:, k, :], h_raw[:, k % 2, :], h_hi[:, k, :],
                                      ALU.subtract).then_inc(h_lo_done, 1)

                for k in range(KT):
                    raw(k)
                    if k and not final:
                        remainder(k - 1)
                if not final:
                    remainder(KT - 1)

            def q_rest(src, b, parts):
                dve.wait_ge(part_hi_done, parts + 1)
                for h in range(2):
                    ins = dve.tensor_tensor(q_st[other(h), b, h, :], src[own(h), :], q_st[own(h), b, h, :],
                                            ALU.subtract)
                ins.then_inc(part_lo_done, 1)

            def k_rest(src, places, parts, both):
                dve.wait_ge(part_hi_done, parts + 1)
                for h, (b, stream) in enumerate(places):
                    for rows in (own(h), other(h))[:2 if both else 1]:
                        ins = dve.tensor_tensor(kk_lo[rows, b, stream, :], src[own(h), :],
                                                kk_hi[own(h), b, stream, :], ALU.subtract)
                ins.then_inc(part_lo_done, 1)

            def v_rest(n, to, hi):
                dve.wait_ge(v_hi_done, n + 1)
                dve.tensor_tensor(to, misc[:, :].rearrange("p (k s d) -> p s k d", k=QT, s=2), hi,
                                  ALU.subtract).then_inc(v_lo_done, 1)

            def z_silu_of(half, par, r, b):
                dve.wait_ge(z_th_done, r + 1)
                dve.scalar_tensor_tensor(z_silu[:, b, :], z_silu[:, b, :], 1.0, acc[par][:, :],
                                         ALU.add, ALU.mult).then_inc(z_done, 1)

            def body(l, att, proj):
                plan = Body(att, proj)
                todo = {}

                def at(slot, what):
                    todo.setdefault(slot, []).append(what)

                if proj is not None:
                    for slot, units in plan.begin.items():
                        for u in units:
                            at(slot + 1, lambda nxt=proj.unit(u + 1): split_lo(*nxt))
                    if proj.nsa:
                        c, n = l * 10 + 2 + proj.i, l * 26 + 2 + proj.i
                        at(plan.at_end(0, 7), lambda: q_rest(q_rope, proj.b, n))
                        at(plan.at_end(1, 1), lambda: z_silu_of(*proj.unit(1), proj.r, proj.b))
                    else:
                        n, v = l * 26 + 10 + 2 * proj.i, l * 10 + 2 + proj.i
                        places = [(proj.b, 0), (proj.b, 1)]
                        at(plan.at_end(0, 1), lambda: q_rest(acc[0], proj.b, n))
                        at(plan.at_end(1, 1), lambda: k_rest(acc[1], places, n + 1, False))
                        at(plan.at_end(2, 2), lambda: v_rest(v, v_lo[:, proj.b, :, :, HD:2 * HD],
                                                             v_hi[:, proj.b, :, :, HD:2 * HD]))
                        at(plan.at_end(3, 1), lambda: z_silu_of(*proj.unit(3), proj.r, proj.b))

                def max_step(s):
                    t, qt, ring = att.s0 + s, s % QT, s % SM_RING
                    width = P * (qt + 1)
                    dve.wait_ge(s_mm, t + 1)
                    if s >= SM_RING:
                        dve.wait_ge(s_turned, t - SM_RING + 1)
                    apart(dve)
                    dve.tensor_tensor_reduce(prob[:, ring, 0:width], scores[s % 2][:, 0:width],
                                             causal[:, T - width:T], -SCALE, BIG, ALU.add, ALU.min,
                                             row_max[:, ring:ring + 1]).then_inc(s_max, 1)

                def invert_step(s):
                    dve.wait_ge(s_exp, att.s0 + s + 1)
                    ring = s % SM_RING
                    dve.reciprocal(row_inv[:, ring:ring + 1], row_sum[:, ring:ring + 1]).then_inc(s_inv, 1)

                def scale_step(s):
                    t, qt, ring = att.s0 + s, s % QT, s % SM_RING
                    h, _, _, branch = att.atts()[s // QT]
                    p = prob[:, ring, 0:P * (qt + 1)]
                    dve.wait_ge(s_inv, t + 1)
                    if branch is None:
                        ins = dve.tensor_scalar(p, p, row_inv[:, ring:ring + 1], None, ALU.mult)
                    else:
                        gate = gates[:, qt, bass.ds(2 * att.i + HEADS * branch + h, 1)]
                        ins = dve.tensor_scalar(p, p, row_inv[:, ring:ring + 1], gate, ALU.mult, ALU.mult)
                    ins.then_inc(s_scaled, 1)

                def lo_step(s):
                    a, qt = divmod(s, QT)
                    dve.wait_ge(pt_hi_done, att.s0 + s + 1)
                    dve.tensor_tensor(pt_tiles(pt_lo, a, qt), turned_tiles(s, qt), pt_tiles(pt_hi, a, qt),
                                      ALU.subtract).then_inc(pt_lo_done, 1)

                if att is not None and att.nsa:
                    m = att.l * PAIRS + att.i

                    def cmp_top():
                        dve.wait_ge(cmp_s, m + 1)
                        flat = misc[:, 0:2 * QT * N_PAD].rearrange("p (a n) -> p a n", n=N_PAD)
                        mask = cmp_mask[:, :, :, :].rearrange("p q h n -> p (q h) n")
                        dve.tensor_tensor(pc[:, :, :], flat, mask, ALU.add).then_inc(cmp_dve, 1)
                        dve.wait_ge(cmp_dve, 7 * m + 1)
                        dve.tensor_reduce(pc_max[:, :], pc[:, :, :], AX_X, ALU.max).then_inc(cmp_dve, 1)
                        dve.wait_ge(cmp_dve, 7 * m + 2)
                        dve.tensor_tensor(pc[:, :, :], pc[:, :, :],
                                          pc_max[:, :].unsqueeze(2).broadcast_to([P, 2 * QT, N_PAD]),
                                          ALU.subtract).then_inc(cmp_dve, 1)

                    def cmp_norm():
                        dve.wait_ge(cmp_exp, m + 1)
                        dve.tensor_reduce(pc_sum[:, :], pc[:, :, :], AX_X, ALU.add).then_inc(cmp_dve, 1)
                        dve.wait_ge(cmp_dve, 7 * m + 4)
                        dve.reciprocal(pc_inv[:, :], pc_sum[:, :]).then_inc(cmp_dve, 1)
                        dve.wait_ge(cmp_dve, 7 * m + 5)
                        inv = pc_inv[:, :].rearrange("p (q h) -> p q h", h=2)
                        dve.tensor_tensor(inv, inv, gates[:, :, bass.ds(2 * att.i, 2)],
                                          ALU.mult).then_inc(cmp_dve, 1)
                        dve.wait_ge(cmp_dve, 7 * m + 6)
                        dve.tensor_tensor(pc[:, :, :], pc[:, :, :],
                                          pc_inv[:, :].unsqueeze(2).broadcast_to([P, 2 * QT, N_PAD]),
                                          ALU.mult).then_inc(cmp_dve, 1)

                    at(1, cmp_top)
                    at(3, cmp_norm)

                last = max([plan.slots] + [k + 1 for k in todo])
                for s in range(last):
                    if LAG_SCALE <= s < plan.steps + LAG_SCALE:
                        invert_step(s - LAG_SCALE)
                    if s < plan.steps:
                        max_step(s)
                    if LAG_SCALE <= s < plan.steps + LAG_SCALE:
                        scale_step(s - LAG_SCALE)
                    if LAG_PT <= s < plan.steps + LAG_PT:
                        lo_step(s - LAG_PT)
                    for what in todo.get(s, []):
                        what()
                if att is not None:
                    dve.wait_ge(pv_mm, att.a0 + plan.steps // QT)
                    dve.wait_ge(z_done, att.r + 2)
                    y = y_all[0 if att.nsa else 1][:, bass.ds(att.i, 1), :]
                    dve.scalar_tensor_tensor(y, o_pair[:, :].unsqueeze(1), 0.5, z_silu[:, att.b:att.b + 1, :],
                                             ALU.mult, ALU.mult).then_inc(y_mul, 1)

            dve.memset(row_inv[:, 0:1], 0.0).then_inc(w_lo_done, 2)
            dve.memset(row_inv[:, 1:2], 0.0).then_inc(z_done, 1)
            dve.memset(row_inv[:, 2:3], 0.0).then_inc(y_mul, 2)
            dve.memset(row_inv[:, 3:4], 0.0).then_inc(m_part, 2)
            dve.wait_ge(consts, N_CONSTS)
            dve.wait_ge(consts_dma, 16 * (2 + DEPTH + 2))
            dve.tensor_copy(sel[:, :, :], sel_f[:, :, :]).then_inc(sel_done, 1)
            for k in range(KT):
                dve.wait_ge(x_turned, k + 1)
                dve.tensor_copy(xT[:, k, :], turned[k % 2][:, :]).then_inc(x_done, 1)

            with dve.Fori(0, DEPTH) as l:
                half0 = l * (U_ALL // 2)

                def kv(n):
                    return half0 + n // 2, n % 2

                norm(l, between=lambda: split_lo(*kv(0), kv_widths[0]))
                split_lo(*kv(1), kv_widths[1])
                split_lo(*kv(2), kv_widths[2])
                k_rest(q_rope, [(0, 0), (1, 0)], l * 26, True)
                split_lo(*kv(3), kv_widths[3])
                split_lo(*kv(4), kv_widths[4])
                k_rest(q_rope, [(0, 1), (1, 1)], l * 26 + 1, True)
                split_lo(*kv(5), kv_widths[5])
                v_rest(l * 10, v_lo[:, :, 0, :, HD:2 * HD], v_hi[:, :, 0, :, HD:2 * HD])
                split_lo(*kv(6), kv_widths[6])
                v_rest(l * 10 + 1, v_lo[:, :, 1, :, HD:2 * HD], v_hi[:, :, 1, :, HD:2 * HD])
                dve.wait_ge(c_landed, 160 * (l + 1))
                for a in range(2):
                    dve.wait_ge(c_src_done, 2 * l + a + 1)
                    for j in range(CJ):
                        src = c_src[:, a, :, j:j + 8 * (N_CMP - 1) + 1:8]
                        ins = dve.tensor_scalar(c_blk[:, a, j, :, 0:N_CMP], src, c_pe[:, a, j:j + 1], None, ALU.add)
                    ins.then_inc(c_blk_done, 1)
                    if a == 0:
                        split_lo(*kv(7), kv_widths[7])
                split_lo(*kv(8))
                dve.wait_ge(unit_mm, 2 * half0 + 8)
                dve.tensor_scalar(f_a[:, :], acc[1][0:HEADS, :], b_f[:, bass.ds(l, 1)], None,
                                  ALU.add).then_inc(f_step, 1)
                dve.wait_ge(f_step, 6 * l + 1)
                dve.scalar_tensor_tensor(f_b[:, :], f_a[:, :], -1.0, f_a[:, :],
                                         ALU.mult, ALU.max).then_inc(f_step, 1)
                dve.wait_ge(g_turned, l + 1)
                dve.tensor_scalar(gates[:, :, :], misc[:, 0:QT * 3 * HEADS].rearrange("p (q c) -> p q c", q=QT),
                                  0.5, 0.5, ALU.mult, ALU.add).then_inc(gates_done, 1)
                dve.wait_ge(gates_done, 2 * l + 1)
                dve.tensor_scalar(gates[:, 0, 0:HEADS], gates[:, 0, 0:HEADS], past_first[:, 0:1], None,
                                  ALU.mult).then_inc(gates_done, 1)
                for a in range(2):
                    dve.wait_ge(c_th_done, 2 * l + a + 1)
                    dve.scalar_tensor_tensor(c_hid[:, a, :], c_th[:, a, :], 1.0, turned[a][:, 0:GROUPS * N_PAD],
                                             ALU.add, ALU.mult).then_inc(c_hid_done, 1)
                dve.wait_ge(f_exp, 3 * l + 2)
                dve.scalar_tensor_tensor(f_a[:, :], f_a[:, :], 0.0, f_b[:, :],
                                         ALU.min, ALU.subtract).then_inc(f_step, 1)
                dve.wait_ge(f_step, 6 * l + 3)
                dve.tensor_tensor_scan(f_b[:, :], ones[0:HEADS, 0:1].broadcast_to([HEADS, T]), f_a[:, :], 0.0,
                                       ALU.mult, ALU.add).then_inc(f_step, 1)
                dve.wait_ge(f_step, 6 * l + 4)
                dve.tensor_scalar(f_b[:, :], f_b[:, :], -1.0 / SCALE, None, ALU.mult).then_inc(f_step, 1)
                dve.wait_ge(f_exp, 3 * l + 3)
                dve.tensor_tensor(f_lo[:, :], f_b[:, :], f_hi[:, :], ALU.subtract).then_inc(f_step, 1)
                dve.wait_ge(pads, 2)
                dve.wait_ge(c_out_mm, 2 * l + 1)
                ck = scores[0][0:HD, 0:GROUPS * N_PAD].rearrange("d (g n) -> d g n", g=GROUPS)
                for h in range(2):
                    dve.tensor_scalar(kcb[HD * h:HD * h + HD, :, N_PAD * h:N_PAD * h + N_PAD], ck, 0.5, None,
                                      ALU.mult).then_inc(cb_ready, 1)
                dve.wait_ge(c_out_mm, 2 * l + 2)
                cv = scores[1][0:N_PAD, 0:GROUPS * HD].rearrange("n (g d) -> n g d", g=GROUPS)
                for h in range(2):
                    dve.tensor_scalar(vcb[N_PAD * h:N_PAD * h + N_PAD, :, HD * h:HD * h + HD], cv, 0.5, None,
                                      ALU.mult).then_inc(cb_ready, 1)
                dve.wait_ge(gates_done, 2 * l + 2)

                bodies(dve, l, body)

                for mixer in range(2):
                    for k in range(0, KT, 2):
                        dve.wait_ge(yt_hi_done, KT * l + KT // 2 * mixer + k // 2 + 1)
                        dve.tensor_tensor(yt_lo[:, mixer, k:k + 2, :], y_all[mixer][:, k:k + 2, :],
                                          yt_hi[:, mixer, k:k + 2, :], ALU.subtract).then_inc(yt_lo_done, 1)

                with dve.Fori(0, KT) as e:
                    half = half0 + U_MERGE // 2 + 2 * e
                    split_lo(half, 1)
                    split_lo(half + 1, 0)
                    split_lo(half + 1, 1)
                    for n in range(2):
                        if n == 1:
                            split_lo(half + 2, 0)
                        dve.wait_ge(m_th_done, 2 * KT * l + 2 * e + n + 1)
                        dve.wait_ge(unit_mm, 2 * half + 3 + n)
                        dve.scalar_tensor_tensor(m_sum[:, n, :], m_th[:, n, :], 1.0, acc[n][:, :],
                                                 ALU.add, ALU.mult).then_inc(m_part, 1)
                    dve.wait_ge(m_part, 2 * KT * l + 2 * e + 4)
                    dve.tensor_tensor(m_sum[:, 0, :], m_sum[:, 0, :], m_sum[:, 1, :], ALU.add).then_inc(m_sum_done, 1)
                    dve.wait_ge(m_hi_done, KT * l + e + 1)
                    dve.scalar_tensor_tensor(m_lo[:, bass.ds(e, 1), :], m_sum[:, 0:1, :], 0.5,
                                             m_hi[:, bass.ds(e, 1), :], ALU.mult, ALU.subtract
                                             ).then_inc(m_lo_done, 1)

                def residual(j, par):
                    dve.wait_ge(unit_mm, 2 * (half0 + U_OUT // 2 + j) + par + 1)
                    tile = xT[:, bass.ds(2 * j + par, 1), :]
                    dve.tensor_tensor(tile, tile, acc[par][:, :].unsqueeze(1), ALU.add)\
                        .then_inc(x_done, 1)

                dve.wait_ge(x_back, 16 * (l + 1))
                apart(dve)
                with dve.Fori(0, KT // 2 - 1) as j:
                    split_lo(half0 + U_OUT // 2 + j, 1)
                    residual(j, 0)
                    split_lo(half0 + U_OUT // 2 + j + 1, 0)
                    residual(j, 1)
                split_lo(half0 + U_OUT // 2 + KT // 2 - 1, 1)
                residual(KT // 2 - 1, 0)
                residual(KT // 2 - 1, 1)
            norm(DEPTH, final=True)
            for n in range(0, 2 * QT, 2):
                dve.wait_ge(o_turned, n + 1)
                dve.tensor_copy(o_nat[:, n // 2, 0:512], turned[0][:, :]).then_inc(o_copied[0], 1)

        @block.tensor
        def _(pe):
            def norm(n):
                for k in range(KT):
                    pe.wait_ge(sq_done, KT * n + k + 1)
                    pe.matmul(misc[:, :], ones[:, :], squares[:, k % 2, :], start=(k == 0),
                              stop=(k == KT - 1)).then_inc(sq_used, 1)

            def unit_piece(first, last, half, par, width=P, hi=None, lo=None, each_k=None, free=None):
                for n in range(first, last):
                    k, which = divmod(n, 3)
                    if n == 0:
                        pe.wait_ge(w_lo_done, 2 * half + par + 3)
                        if free is not None:
                            pe.wait_ge(*free)
                    if each_k is not None and which == 0:
                        pe.wait_ge(*each_k(k))
                    w = w_lo if which == 2 else w_hi
                    rhs = (lo if which == 1 else hi)[:, k, :] if hi is not None else \
                        (h_lo if which == 1 else h_hi)[:, k, :]
                    ins = pe.matmul(acc[par][0:width, :], w[:, par, k, 0:width], rhs,
                                    start=(n == 0), stop=(n == 23))
                    if n == 23:
                        ins.then_inc(unit_mm, 1)

            def bank_read(l, pair, part):
                if pair.nsa and pair.first:
                    return (g_th_done, l + 1) if part == 0 else (f_step, 6 * l + 1)
                if part == 0 and (pair.nsa or pair.first):
                    return swap_done, l * 10 + 2 + (pair.i if pair.nsa else PAIRS)
                if part == 0:
                    return v_raw_done, l * 10 + 2 + pair.i
                if part == 1:
                    return z_done, pair.r + 1
                return part_lo_done, l * 26 + 10 + 2 * pair.i + part - 1

            def turn_v(n):
                pe.wait_ge(v_raw_done, n + 1)
                for kt in range(QT):
                    ins = pe.transpose(misc[:, P * kt:P * kt + P], q_raw[:, P * kt:P * kt + P], ident[:, :])
                ins.then_inc(v_turned, 1)

            def body(l, att, proj):
                plan = Body(att, proj)
                extra = {}
                if proj is not None and not proj.nsa:
                    v = l * 10 + 2 + proj.i

                    def turn():
                        if not att.nsa:
                            pe.wait_ge(v_lo_done, v)
                        turn_v(v)

                    extra.setdefault(plan.at_end(2, 2), []).append(turn)

                def score_step(s):
                    a, qt = divmod(s, QT)
                    h, b, stream, branch = att.atts()[a]
                    n, cols = key_cols(qt), slice(P * qt, P * qt + P)
                    if s >= 2:
                        pe.wait_ge(s_max, att.s0 + s - 1)
                    to = scores[s % 2][:, 0:n]
                    pe.matmul(to, q_st[:, att.b, h, cols], kk_hi[:, b, stream, 0:n], start=True, stop=False)
                    ins = pe.matmul(to, q_st[own(h), att.b, h, cols], kk_lo[own(h), b, stream, 0:n], start=False,
                                    stop=branch is not None)
                    if branch is None:
                        rows = slice(32 * b, 32 * b + 4)
                        ins = pe.matmul(to, sel[rows, h, :], f_row[rows, 0:n], start=False, stop=True)
                    ins.then_inc(s_mm, 1)

                def turn_step(s):
                    qt = s % QT
                    pe.wait_ge(s_scaled, att.s0 + s + 1)
                    if s >= 2:
                        pe.wait_ge(pt_lo_done, att.s0 + s - 1)
                    for kt in range(qt + 1):
                        ins = pe.transpose(turned[s % 2][:, P * kt:P * kt + P],
                                           prob[:, s % SM_RING, P * kt:P * kt + P], ident[:, :])
                    ins.then_inc(s_turned, 1)

                def value_step(a):
                    pe.wait_ge(pt_lo_done, att.s0 + QT * (a + 1))
                    if a == 0:
                        if not att.nsa:
                            pe.wait_ge(y_mul, att.r + 2)
                        pe.wait_ge(v_lo_done, l * 10 + 2 + (0 if att.nsa else att.i + 1))
                    terms = [(a, kt, m) for kt in range(QT) for m in range(3)]
                    if not att.nsa:
                        terms = terms[:-1] if a == 0 else terms + [(0, QT - 1, 2)]
                    for a_of, kt, m in terms:
                        h, b, stream, _ = att.atts()[a_of]
                        v, pt = ((v_hi, pt_hi), (v_hi, pt_lo), (v_lo, pt_hi))[m]
                        q0, width = min(P * kt, T - 2 * P), (HD, P)[h]
                        ins = pe.matmul(o_pair[0:width, q0:T], v[:, b, stream, kt, 2 * HD - width:2 * HD],
                                        pt[:, a_of % 2, 384 * kt + q0:384 * kt + T],
                                        start=not att.nsa and (a_of, kt, m) == (0, 0, 0),
                                        stop=(a_of, kt, m) == terms[-1] and a == plan.steps // QT - 1)
                    ins.then_inc(pv_mm, 1)

                def cmp_scores():
                    pe.wait_ge(raw_done, l * 10 + 2 + att.i + 1)
                    pe.wait_ge(cb_ready, 4 * (l + 1))
                    for qt in range(QT):
                        ins = pe.matmul(misc[:, 64 * qt:64 * qt + 64], q_raw[:, P * qt:P * qt + P],
                                        kcb[:, att.g, :], start=True, stop=True)
                    ins.then_inc(cmp_s, 1)

                def cmp_turn():
                    pe.wait_ge(cmp_dve, 7 * (att.l * PAIRS + att.i) + 7)
                    apart(pe)
                    for qt in range(QT):
                        ins = pe.transpose(misc[0:2 * N_PAD, P * qt:P * qt + P],
                                           pc[:, 2 * qt:2 * qt + 2, :].rearrange("p h n -> p (h n)"), ident[:, :])
                    ins.then_inc(cmp_turned, 1)

                def cmp_values():
                    pe.wait_ge(cmp_pt, att.l * PAIRS + att.i + 1)
                    pe.wait_ge(y_mul, att.r + 2)
                    pe.matmul(o_pair[:, :], vcb[:, att.g, :], pc_t[:, :], start=True, stop=False)

                if att is not None:
                    pe.wait_ge(part_lo_done, l * 26 + (3 + att.i if att.nsa else 12 + 2 * att.i))
                    if not att.nsa:
                        pe.wait_ge(f_landed, 16 * (att.l * PAIRS + att.i + 1))
                    for a in range(plan.steps // QT):
                        extra.setdefault(QT * a + QT - 1 + LAG_PV, []).append(lambda a=a: value_step(a))
                    if att.nsa:
                        extra.setdefault(0, []).insert(0, cmp_scores)
                        extra.setdefault(4, []).insert(0, cmp_turn)
                        extra.setdefault(5, []).insert(0, cmp_values)

                done = 0
                for s in range(max([plan.slots] + [k + 1 for k in extra])):
                    for step in ([0, 1] if s == 0 else [s + 1]):
                        if step < plan.steps:
                            score_step(step)
                    if LAG_TURN <= s < plan.steps + LAG_TURN:
                        turn_step(s - LAG_TURN)
                    want = plan.cum[s] if s < plan.slots else done
                    while done < want:
                        u = done // 24
                        stop = min(want, 24 * u + 24)
                        unit_piece(done - 24 * u, stop - 24 * u, *proj.unit(u),
                                   free=bank_read(l, proj, u))
                        done = stop
                    for what in extra.get(s, []):
                        what()

            pe.wait_ge(consts, N_CONSTS)
            pe.wait_ge(x_landed, 16)
            for k in range(KT):
                if k >= 2:
                    pe.wait_ge(x_done, k - 1)
                for i in range(QT):
                    ins = pe.transpose(turned[k % 2][:, P * i:P * i + P], x_nat[:, i, P * k:P * k + P], ident[:, :])
                ins.then_inc(x_turned, 1)
            pe.wait_ge(sel_done, 1)
            with pe.Fori(0, DEPTH) as l:
                half0 = l * (U_ALL // 2)

                readers = [None, None, (swap_done, l * 10 + 1), (swap_done, l * 10 + 2),
                           (v_raw_done, l * 10 + 1), (v_raw_done, l * 10 + 2),
                           (c_src_done, 2 * l + 1), (c_src_done, 2 * l + 2)]

                def kv(n, **more):
                    unit_piece(0, 24, half0 + n // 2, n % 2, kv_widths[n], free=readers[n], **more)

                norm(l)
                kv(0, each_k=lambda k: (h_lo_done, KT * l + k + 1))
                kv(1)
                kv(2)
                kv(3)
                turn_v(l * 10)
                kv(4)
                pe.wait_ge(v_lo_done, l * 10 + 1)
                turn_v(l * 10 + 1)
                kv(5)
                kv(6)
                kv(7)
                pe.wait_ge(g_th_done, l + 1)
                pe.wait_ge(v_lo_done, l * 10 + 2)
                apart(pe)
                for i in range(QT):
                    ins = pe.transpose(misc[:, 48 * i:48 * i + 48], g_th[:, P * i:P * i + P],
                                       ident[0:3 * HEADS, 0:3 * HEADS])
                ins.then_inc(g_turned, 1)
                pe.wait_ge(pads, 2 + 5 * l + 3)
                pe.wait_ge(c_landed, 160 * (l + 1))
                for a in range(2):
                    pe.wait_ge(c_blk_done, 2 * l + a + 1)
                    for j in range(CJ):
                        ins = pe.matmul(turned[a][:, 0:GROUPS * N_PAD], c_w1[:, a, j, :],
                                        c_blk[:, a, j, :, :].rearrange("p g n -> p (g n)"),
                                        start=(j == 0), stop=(j == CJ - 1))
                    ins.then_inc(c_hid_mm, 1)
                pe.wait_ge(c_hid_done, 2 * l + 1)
                pe.matmul(scores[0][0:HD, 0:64], c_w2[:, 0, :], c_hid[:, 0, :], start=True,
                          stop=True).then_inc(c_out_mm, 1)
                pe.wait_ge(c_hid_done, 2 * l + 2)
                for g in range(GROUPS):
                    ins = pe.matmul(scores[1][0:N_PAD, HD * g:HD * g + HD], c_hid[:, 1, N_PAD * g:N_PAD * g + N_PAD],
                                    c_w2[:, 1, :], start=True, stop=True)
                ins.then_inc(c_out_mm, 1)

                pe.wait_ge(pads, 2 + 5 * l + 5)
                apart(pe)
                bodies(pe, l, body)

                pe.wait_ge(v_raw_done, l * 10 + 10)
                pe.wait_ge(z_done, 2 * PAIRS * (l + 1) + 1)
                apart(pe)
                with pe.Fori(0, KT) as e:
                    half = half0 + U_MERGE // 2 + 2 * e
                    for n in range(2):
                        unit_piece(0, 24, half, n, free=(m_part, 2 * KT * l + 2 * e + n + 1))
                    for mixer in range(2):
                        pe.wait_ge(yt_lo_done, KT * l + KT // 2 * (mixer + 1))
                        unit_piece(0, 24, half + 1, mixer, hi=yt_hi[:, mixer], lo=yt_lo[:, mixer],
                                   free=(m_th_done, 2 * KT * l + 2 * e + mixer + 1))
                pe.wait_ge(m_lo_done, KT * (l + 1))
                apart(pe)
                with pe.Fori(0, KT // 2) as j:
                    for par in range(2):
                        unit_piece(0, 24, half0 + U_OUT // 2 + j, par, hi=m_hi, lo=m_lo,
                                   free=(x_done, KT * (l + 1) + 2 * j + par - 1))
            norm(DEPTH)
            pe.wait_ge(h_raw_done, KT * (DEPTH + 1))
            for n in range(2 * QT):
                if n >= 2:
                    pe.wait_ge(o_copied[n % 2], n // 2)
                for c in range(4):
                    k = 4 * (n % 2) + c
                    ins = pe.transpose(turned[n % 2][:, P * c:P * c + P],
                                       o_t[:, k, P * (n // 2):P * (n // 2) + P], ident[:, :])
                ins.then_inc(o_turned, 1)


_INS = ["x", "norm_g", "w_in", "b_forget", "cmp_pe_k", "cmp_w1_k", "cmp_w2_k", "cmp_pe_v", "cmp_w1_v",
        "cmp_w2_v", "w_proj_nsa", "w_proj_fox", "w_out", "final_g"]


def rope_tables():
    inv = np.float32(10000.0) ** (-np.arange(0, HD, 2, dtype=np.float32) / np.float32(HD))
    ang = (np.arange(T, dtype=np.float32)[None, :] * inv[:, None]).astype(np.float32)
    cos, sin = np.cos(ang), np.sin(ang)
    return (np.concatenate([cos] * 4).astype(np.float32),
            np.concatenate([-sin, sin] * 2).astype(np.float32))


def kernel(**inputs):
    import concourse.bacc as _bacc
    from concourse.bass_utils import run_bass_kernel_spmd as _run

    nc = _bacc.Bacc("TRN2", target_bir_lowering=False, num_devices=1)
    arrays, args = {}, []
    for name in _INS:
        a = np.ascontiguousarray(inputs[name])
        arrays[f"in_{name}_dram"] = a
        args.append(nc.dram_tensor(f"in_{name}_dram", a.shape, mybir.dt.from_np(a.dtype), kind="ExternalInput").ap())
    for name, a in zip(("rope_cos", "rope_sin"), rope_tables()):
        arrays[f"in_{name}_dram"] = a
        args.append(nc.dram_tensor(f"in_{name}_dram", a.shape, mybir.dt.from_np(a.dtype), kind="ExternalInput").ap())
    args.append(nc.dram_tensor("out_0_dram", (1, T, D), F32, kind="ExternalOutput").ap())
    bass_trunk(nc, *args)
    r = _run(nc, [arrays], core_ids=[0])
    return r.results[0]["out_0_dram"]
```

```python
from contextlib import ExitStack

import numpy as np

import concourse.bass as bass
from concourse import mybir

F32 = mybir.dt.float32
F32R = mybir.dt.float32r
ALU = mybir.AluOpType
ACT = mybir.ActivationFunctionType
AX_X = mybir.AxisListType.X

P = 128
T = 512
D = 1024
DEPTH = 2
HD = 64
HEADS = 16
PAIRS = HEADS // 2
GROUPS = 2
KT = D // P
QT = T // P
CMP_BLOCK, CMP_STRIDE = 32, 16
N_CMP = (T - CMP_BLOCK) // CMP_STRIDE + 1
N_PAD = 32
CJ = CMP_BLOCK // 2
NEG = -1.0e30
BIG = 3.0e38
SCALE = HD ** -0.5
EPS = 1e-6

C_QA = 0
C_KV = C_QA + D
C_G = C_KV + 3 * 2 * GROUPS * HD
C_ZA = C_G + 3 * HEADS
C_QB = C_ZA + D
C_KB = C_QB + D
C_VB = C_KB + D
C_F = C_VB + D
C_ZB = C_F + HEADS
C_RA = C_ZB + D
C_RB = C_RA + D
IN_COLS = C_RB + D
KV_UNITS = [(C_KV, P), (C_KV + P, P), (C_G, 3 * HEADS), (C_F, HEADS),
            (C_KV + 2 * P, P), (C_KV + 4 * P, P), (C_KV + 3 * P, P), (C_QA, P), (C_KV + 5 * P, P), (C_ZA, P)]

U_NSA, U_FOX, U_MERGE, U_OUT, U_ALL = 8, 24, 56, 88, 96
S_FOX, S_ALL = 4 * 4 * PAIRS, 4 * 4 * PAIRS + 4 * 2 * PAIRS
A_FOX, A_ALL = 4 * PAIRS, 6 * PAIRS
SM_RING = 4
H_RING = 4
LAG_SCALE, LAG_TURN, LAG_PT, LAG_PV = 1, 2, 3, 4
PT_COLS = 3 * 384 + T


def spread(total, busy):
    level = 0.0
    while sum(max(0.0, level - b) for b in busy) < total:
        level += 0.05
    cum, done = [], 0.0
    for b in busy:
        done += max(0.0, level - b)
        cum.append(min(total, int(done)))
    cum[-1] = total
    return cum


class Body:

    def __init__(self, prev, att, proj):
        self.prev, self.att, self.proj = prev, att, proj
        self.steps = att.steps
        self.slots = self.steps + (LAG_PV if proj.gates else 0)
        n = 2 if proj.nsa or proj.gates else 4
        busy = [0.0] * self.slots
        for s in range(self.slots):
            for lag, costs in ((-1, (1.0, 1.0, 1.5, 2.0) if att.nsa else (1.5, 1.5, 2.3, 3.0)),
                               (LAG_TURN, (1.25, 1.25, 1.25, 1.25)), (LAG_PV, (0.0, 0.0, 0.0, 9.0))):
                if s - lag < self.steps or not proj.gates:
                    busy[s] += costs[(s - lag) % QT]
        self.cum = spread(24 * n, busy)
        self.begin, self.end = {}, {}
        for u in range(n):
            first = next(s for s in range(self.slots) if self.cum[s] > 24 * u)
            last = next(s for s in range(self.slots) if self.cum[s] >= 24 * u + 24)
            self.begin.setdefault(first, []).append(u)
            self.end[u] = last

    def step(self, s):
        if s < 0:
            return None if self.prev is None else (self.prev, self.prev.steps + s)
        if s < self.steps:
            return self.att, s
        return None if self.proj.gates else (self.proj, s - self.steps)

    def at_end(self, part, lag):
        return min(self.end[part] + lag, self.slots + lag)


class FirstGates:
    nsa, gates = False, True

    def __init__(self, l):
        self.half = l * (U_ALL // 2) + U_MERGE // 2

    def unit(self, part):
        return self.half + part // 2, part % 2


class Pair:

    gates = False

    def __init__(self, nsa, l, i, parity, group=0, first=False):
        self.first = first
        self.steps = 16 if nsa else 8
        self.nsa, self.l, self.i, self.b, self.g = nsa, l, i, parity, group
        if nsa:
            self.half = l * (U_ALL // 2) + U_NSA // 2 + i
            self.s0 = l * S_ALL + 16 * i
            self.a0 = l * A_ALL + 4 * i
            self.r = l * (2 * PAIRS) + i
        else:
            self.half = l * (U_ALL // 2) + U_FOX // 2 + 2 * i
            self.s0 = l * S_ALL + S_FOX + 8 * i
            self.a0 = l * A_ALL + A_FOX + 2 * i
            self.r = l * (2 * PAIRS) + PAIRS + i

    def unit(self, part):
        return self.half + part // 2, part % 2

    def atts(self):
        if self.nsa:
            return [(h, self.g, s, 1 + s) for h in range(2) for s in range(2)]
        return [(h, self.b, h, None) for h in (1, 0)]


def bass_trunk(nc, x, norm_g, w_in, b_forget, pe_k, w1_k, w2_k, pe_v, w1_v, w2_v, w_nsa, w_fox,
               w_out, final_g, rope_c, rope_s, out):
    ctx = ExitStack()
    with ctx:
        scope = [ctx]

        def sb(name, shape, dt=F32):
            return scope[-1].enter_context(nc.sbuf_tensor(name, shape, dt))

        def psum(name, shape):
            return ctx.enter_context(nc.psum_tensor(name, shape, F32))

        def sem(name):
            return ctx.enter_context(nc.semaphore(name))

        h_hi = sb("h_hi", [P, KT, T], F32R)
        h_lo = sb("h_lo", [P, KT, T], F32R)
        w_raw = sb("w_raw", [P, 2, KT, P])
        w_hi = sb("w_hi", [P, 2, KT, P], F32R)
        w_lo = sb("w_lo", [P, 2, KT, P], F32R)
        cosT = sb("cosT", [P, T])
        sinT = sb("sinT", [P, T])
        causal = sb("causal", [P, T])
        cmp_mask = sb("cmp_mask", [P, QT, 2, N_PAD])
        ident = sb("ident", [P, P])
        ones = sb("ones", [P, P])
        sel_f = sb("sel_f", [36, 2, P])
        sel = sb("sel", [36, 2, P], F32R)
        past_first = sb("past_first", [P, 1])
        gains = sb("gains", [P, DEPTH + 1, KT])
        b_f = sb("b_f", [HEADS, DEPTH])
        gates = sb("gates", [P, QT, 3 * HEADS])
        kcb = sb("kcb", [P, GROUPS, 2 * N_PAD])
        vcb = sb("vcb", [2 * N_PAD, GROUPS, P])
        row_max = sb("row_max", [P, SM_RING])
        row_sum = sb("row_sum", [P, SM_RING])
        row_inv = sb("row_inv", [P, SM_RING])
        with ExitStack() as own_place:
            scope.append(own_place)
            y_all = [sb(f"y_all{n}", [P, PAIRS, T]) for n in range(2)]
            scope.pop()
        with ExitStack() as own_place:
            scope.append(own_place)
            m_hi = sb("m_hi", [P, KT, T], F32R)
            m_lo = sb("m_lo", [P, KT, T], F32R)
            scope.pop()
        with ExitStack() as own_place:
            scope.append(own_place)
            h_raw = sb("h_raw", [P, H_RING, T])
            g_th = sb("g_th", [3 * HEADS, T])
            f_a = sb("f_a", [HEADS, T])
            f_b = sb("f_b", [HEADS, T])
            f_hi = sb("f_hi", [HEADS, T], F32R)
            f_lo = sb("f_lo", [HEADS, T], F32R)
            scope.pop()
        sb("place_of_y_and_m", [P, 2, KT, T])

        with ExitStack() as own_place:
            scope.append(own_place)
            xT = sb("xT", [P, KT, T])
            scope.pop()
        with ExitStack() as own:
            scope.append(own)
            v_hi = sb("v_hi", [P, 2, 2, QT, 2 * HD], F32R)
            v_lo = sb("v_lo", [P, 2, 2, QT, 2 * HD], F32R)
            pt_hi = sb("pt_hi", [P, 2, PT_COLS], F32R)
            pt_lo = sb("pt_lo", [P, 2, PT_COLS], F32R)
            prob = sb("prob", [P, SM_RING, T])
            q_st = sb("q_st", [P, 2, 2, T], F32R)
            kk_hi = sb("kk_hi", [P, 2, 2, T], F32R)
            kk_lo = sb("kk_lo", [P, 2, 2, T], F32R)
            f_row = sb("f_row", [36, T], F32R)
            q_raw = sb("q_raw", [P, T])
            q_swap = sb("q_swap", [P, T])
            q_rope = sb("q_rope", [P, T])
            z_silu = sb("z_silu", [P, 2, T])
            pc = sb("pc", [P, 2 * QT, N_PAD])
            pc_t = sb("pc_t", [2 * N_PAD, T])
            pc_max = sb("pc_max", [P, 2 * QT])
            pc_sum = sb("pc_sum", [P, 2 * QT])
            pc_inv = sb("pc_inv", [P, 2 * QT])
            scope.pop()
        with ExitStack() as own:
            scope.append(own)
            sb("xT_under_norm", [P, KT, T])
            squares = sb("squares", [P, 2, T])
            sq_sum = sb("sq_sum", [P, T])
            rstd = sb("rstd", [P, T])
            c_w1 = sb("c_w1", [P, 2, CJ, P])
            c_w2 = sb("c_w2", [P, 2, HD])
            c_pe = sb("c_pe", [P, 2, CJ])
            c_src = sb("c_src", [P, 2, GROUPS, T // 2])
            c_blk = sb("c_blk", [P, 2, CJ, GROUPS, N_PAD])
            c_th = sb("c_th", [P, 2, GROUPS * N_PAD])
            c_hid = sb("c_hid", [P, 2, GROUPS * N_PAD])
            scope.pop()
        with ExitStack() as own:
            scope.append(own)
            sb("xT_under_merge", [P, KT, T])
            yt_hi = sb("yt_hi", [P, 2, KT, T], F32R)
            yt_lo = sb("yt_lo", [P, 2, KT, T], F32R)
            m_th = sb("m_th", [P, 2, T])
            m_sum = sb("m_sum", [P, 2, T])
            scope.pop()
        with ExitStack() as own:
            scope.append(own)
            sb("xT_under_ends", [P, KT, T])
            sb("norm_under_ends", [P, 4, T])
            o_t = sb("o_t", [P, KT, T])
            o_nat = sb("o_nat", [P, QT, D])
            x_nat = sb("x_nat", [P, QT, D])
            scope.pop()

        x_dram = nc.dram_tensor("x_scratch", [P, KT, T], F32, kind="Internal").ap()
        f_dram = nc.dram_tensor("f_scratch", [HEADS, 2, T], F32R, kind="Internal").ap()

        acc = [psum(f"acc{n}", [P, T]) for n in range(2)]
        scores = [psum(f"scores{n}", [P, T]) for n in range(2)]
        turned = [psum(f"turned{n}", [P, T]) for n in range(2)]
        o_pair = psum("o_pair", [P, T])
        misc = psum("misc", [P, T])

        consts = sem("consts")
        consts_dma = sem("consts_dma")
        rope_landed = sem("rope_landed")
        x_landed = [sem(f"x_landed{n}") for n in range(2)]
        x_turned = sem("x_turned")
        x_done = sem("x_done")
        x_saved = sem("x_saved")
        x_back = sem("x_back")
        w_landed = [sem(f"w_landed{n}") for n in range(2)]
        w_hi_done = sem("w_hi_done")
        w_lo_done = sem("w_lo_done")
        unit_mm = sem("unit_mm")
        sq_done = sem("sq_done")
        sq_added = sem("sq_added")
        sq_summed = sem("sq_summed")
        var_done = sem("var_done")
        std_done = sem("std_done")
        rstd_done = sem("rstd_done")
        h_raw_done = sem("h_raw_done")
        h_hi_done = sem("h_hi_done")
        h_lo_done = [sem("h_lo_even"), sem("h_lo_odd")]
        pads = sem("pads")
        raw_done = sem("raw_done")
        swap_done = sem("swap_done")
        rope_parts = sem("rope_parts")
        rope_done = sem("rope_done")
        part_hi_done = sem("part_hi_done")
        part_lo_done = sem("part_lo_done")
        v_raw_done = sem("v_raw_done")
        v_turned = sem("v_turned")
        v_hi_done = sem("v_hi_done")
        v_lo_done = sem("v_lo_done")
        c_landed = sem("c_landed")
        c_src_done = sem("c_src_done")
        c_blk_done = sem("c_blk_done")
        c_hid_mm = sem("c_hid_mm")
        c_th_done = sem("c_th_done")
        c_hid_done = sem("c_hid_done")
        c_out_mm = sem("c_out_mm")
        cb_ready = sem("cb_ready")
        g_th_done = sem("g_th_done")
        g_turned = sem("g_turned")
        gates_done = sem("gates_done")
        f_step = sem("f_step")
        f_exp = sem("f_exp")
        f_saved = sem("f_saved")
        f_landed = sem("f_landed")
        s_mm = sem("s_mm")
        s_max = sem("s_max")
        s_exp = sem("s_exp")
        s_inv = sem("s_inv")
        s_scaled = sem("s_scaled")
        s_turned = sem("s_turned")
        pt_hi_done = sem("pt_hi_done")
        pt_lo_done = sem("pt_lo_done")
        pv_mm = sem("pv_mm")
        cmp_s = sem("cmp_s")
        cmp_dve = sem("cmp_dve")
        cmp_pool = sem("cmp_pool")
        cmp_exp = sem("cmp_exp")
        cmp_turned = sem("cmp_turned")
        cmp_pt = sem("cmp_pt")
        z_th_done = sem("z_th_done")
        z_done = sem("z_done")
        sel_done = sem("sel_done")
        y_mul = sem("y_mul")
        yt_hi_done = sem("yt_hi_done")
        yt_lo_done = sem("yt_lo_done")
        m_th_done = sem("m_th_done")
        m_part = sem("m_part")
        m_sum_done = sem("m_sum_done")
        m_hi_done = sem("m_hi_done")
        m_lo_done = sem("m_lo_done")
        o_turned = sem("o_turned")
        o_copied = [sem(f"o_copied{n}") for n in range(2)]
        o_stored = sem("o_stored")

        w_view = w_in.rearrange("l (k p) c -> p l k c", p=P)
        wn_view = w_nsa.rearrange("l (k p) c -> p l k c", p=P)
        wf_view = w_fox.rearrange("l (k p) c -> p l k c", p=P)
        wo_view = w_out.rearrange("l (k p) c -> p l k c", p=P)

        kv_widths = [w for _, w in KV_UNITS]
        N_CONSTS = 14

        def apart(eng):
            eng.nop(nofuse=True)

        def key_cols(qt):
            return max(P * (qt + 1), 2 * P)

        def bodies(eng, l, body):
            def nsa(i):
                return Pair(True, l, i, i % 2, i // (PAIRS // GROUPS))

            def fox(i, parity, first=False):
                return Pair(False, l, i, parity, first=first)

            body(l, None, nsa(0), nsa(1))
            for i in range(1, PAIRS - 1):
                body(l, nsa(i - 1), nsa(i), nsa(i + 1))
            body(l, nsa(PAIRS - 2), nsa(PAIRS - 1), fox(0, 0, first=True))
            body(l, nsa(PAIRS - 1), fox(0, 0), fox(1, 1))
            with eng.Fori(0, PAIRS // 2 - 1) as j:
                body(l, fox(2 * j, 0), fox(2 * j + 1, 1), fox(2 * j + 2, 0))
                body(l, fox(2 * j + 1, 1), fox(2 * j + 2, 0), fox(2 * j + 3, 1))
            body(l, fox(PAIRS - 2, 0), fox(PAIRS - 1, 1), FirstGates(l))

        def own(h):
            return slice(HD * h, HD * h + HD)

        def other(h):
            return own(1 - h)

        def h_remainder(eng, n, k):
            eng.wait_ge(h_hi_done, KT * n + k + 1)
            apart(eng)
            eng.tensor_tensor(h_lo[:, k, :], h_raw[:, k % H_RING, :], h_hi[:, k, :],
                              ALU.subtract).then_inc(h_lo_done[k % 2], 1)

        def pt_tiles(pt, a, qt):
            first = P * qt
            return pt[:, a % 2, first:first + 384 * qt + P] if qt == 0 else \
                strided(pt, a % 2, first, qt + 1)

        def strided(pt, half, first, n):
            ap = pt[:, half, first:first + 384 * n] if first + 384 * n <= PT_COLS else None
            if ap is not None:
                return ap.rearrange("p (k c) -> p k c", k=n)[:, :, 0:P]
            early = first - 256
            return pt[:, half, early:early + 384 * n].rearrange("p (k c) -> p k c", k=n)[:, :, 256:384]

        def turned_tiles(s, qt):
            bank = turned[s % 2][:, 0:P * (qt + 1)]
            return bank if qt == 0 else bank.rearrange("p (k c) -> p k c", k=qt + 1)

        block = ctx.enter_context(nc.Block())

        @block.sync
        def _(sp):
            def load(src, l, col, width, half, par):
                sp.wait_ge(w_lo_done, 2 * half + par + 1)
                apart(sp)
                sp.dma_start(w_raw[:, par:par + 1, :, 0:width],
                             src[:, bass.ds(l, 1), :, bass.ds(col, width)]).then_inc(w_landed[par], 16)

            def load_compression(l):
                for a, w1, w2, pe in ((0, w1_k, w2_k, pe_k), (1, w1_v, w2_v, pe_v)):
                    for j in (slice(0, CJ // 2), slice(CJ // 2, CJ)):
                        sp.dma_start(c_w1[:, a:a + 1, j, :],
                                     w1.rearrange("l (j p) h -> p l j h", p=P)[:, bass.ds(l, 1), j]
                                     ).then_inc(c_landed, 16)
                    sp.dma_start(c_w2[:, a:a + 1, :],
                                 w2.rearrange("l h d -> h l d")[:, bass.ds(l, 1)]).then_inc(c_landed, 16)
                    with nc.allow_non_contiguous_dma(reason="8 kB of position vectors, transposed"):
                        for par in range(2):
                            sp.dma_start(c_pe[HD * par:HD * par + HD, a:a + 1, :],
                                         pe.rearrange("l (j a) d -> a d l j", a=2)[par][:, bass.ds(l, 1)]
                                         ).then_inc(c_landed, 16)

            for n in range(2):
                cols = slice(D // 2 * n, D // 2 * n + D // 2)
                sp.dma_start(x_nat[:, :, cols], x[0].rearrange("(i p) d -> p i d", p=P)[:, :, cols]
                             ).then_inc(x_landed[n], 16)
            with sp.Fori(0, DEPTH) as l:
                base = l * (U_ALL // 2)
                for n, (col, width) in enumerate(KV_UNITS):
                    load(w_view, l, col, width, base + n // 2, n % 2)
                    if n == 1:
                        load_compression(l)
                with sp.Fori(1, PAIRS) as i:
                    half = base + U_NSA // 2 + i
                    load(w_view, l, C_QA + P * i, P, half, 0)
                    load(w_view, l, C_ZA + P * i, P, half, 1)
                with sp.Fori(0, PAIRS) as i:
                    half = base + U_FOX // 2 + 2 * i
                    load(w_view, l, C_QB + P * i, P, half, 0)
                    load(w_view, l, C_KB + P * i, P, half, 1)
                    load(w_view, l, C_VB + P * i, P, half + 1, 0)
                    load(w_view, l, C_ZB + P * i, P, half + 1, 1)
                with sp.Fori(0, KT) as e:
                    half = base + U_MERGE // 2 + 2 * e
                    load(w_view, l, C_RA + P * e, P, half, 0)
                    load(w_view, l, C_RB + P * e, P, half, 1)
                    load(wn_view, l, P * e, P, half + 1, 0)
                    load(wf_view, l, P * e, P, half + 1, 1)
                with sp.Fori(0, KT // 2) as j:
                    half = base + U_OUT // 2 + j
                    load(wo_view, l, 2 * P * j, P, half, 0)
                    load(wo_view, l, 2 * P * j + P, P, half, 1)
            for m in range(2 * QT):
                half, i = divmod(m, QT)
                cols = slice(D // 2 * half, D // 2 * half + D // 2)
                sp.wait_ge(o_copied[m % 2], m // 2 + 1)
                sp.dma_start(out[0, i * P:(i + 1) * P, cols], o_nat[:, i, cols]).then_inc(o_stored, 16)
            sp.wait_ge(o_stored, 16 * 2 * QT)

        @block.gpsimd
        def _(pool):
            pool.memset(ident[:, :], 0.0).then_inc(consts, 1)
            pool.memset(ones[:, :], 1.0).then_inc(consts, 1)
            pool.memset(causal[:, :], 0.0).then_inc(consts, 1)
            pool.memset(cmp_mask[:, :, :, :], 0.0).then_inc(consts, 1)
            pool.memset(sel_f[:, :, :], 1.0).then_inc(consts, 1)
            pool.memset(past_first[:, :], 1.0).then_inc(consts, 1)
            pool.wait_ge(consts, 6)
            pool.affine_select(out=ident[:, :], in_=ident[:, :], compare_op=ALU.not_equal, fill=1.0,
                               base=0, pattern=[[-1, P]], channel_multiplier=1).then_inc(consts, 1)
            tri = causal[:, T - P:T]
            pool.affine_select(out=tri, in_=tri, compare_op=ALU.is_ge, fill=NEG, base=0,
                               pattern=[[-1, P]], channel_multiplier=1).then_inc(consts, 1)
            pool.affine_select(out=cmp_mask[:, :, :, :], in_=cmp_mask[:, :, :, :], compare_op=ALU.is_ge,
                               fill=NEG, base=1 - CMP_BLOCK,
                               pattern=[[P, QT], [0, 2], [-CMP_STRIDE, N_PAD]],
                               channel_multiplier=1).then_inc(consts, 1)
            for b in range(2):
                rows = sel_f[32 * b:32 * b + 4]
                pool.wait_ge(consts, 9 + 2 * b)
                pool.affine_select(out=rows[:, 0, :], in_=rows[:, 0, :], compare_op=ALU.is_ge, fill=0.0,
                                   base=1, pattern=[[0, P]], channel_multiplier=-1).then_inc(consts, 1)
                pool.affine_select(out=rows[:, 1, :], in_=rows[:, 1, :], compare_op=ALU.is_ge, fill=0.0,
                                   base=-2, pattern=[[0, P]], channel_multiplier=1).then_inc(consts, 1)
            pool.wait_ge(consts, 13)
            pool.affine_select(out=past_first[:, :], in_=past_first[:, :], compare_op=ALU.is_ge, fill=0.0,
                               base=1 - CMP_BLOCK, pattern=[[0, 1]],
                               channel_multiplier=1).then_inc(consts, 1)
            pool.memset(kcb[:, :, :], 0.0).then_inc(pads, 1)
            pool.memset(vcb[:, :, :], 0.0).then_inc(pads, 1)

            def rotate(l, n):
                c = l * 10 + n
                pool.wait_ge(raw_done, c + 1)
                apart(pool)
                if not (isinstance(n, int) and n == 0):
                    pool.wait_ge(part_lo_done, l * 26 + n)
                    apart(pool)
                pool.tensor_tensor(q_rope[:, :], q_raw[:, :], cosT[:, :], ALU.mult).then_inc(rope_parts, 1)
                pool.wait_ge(swap_done, c + 1)
                apart(pool)
                pool.tensor_tensor(q_swap[:, :], q_swap[:, :], sinT[:, :], ALU.mult).then_inc(rope_parts, 1)
                pool.wait_ge(rope_parts, 2 * (c + 1))
                apart(pool)
                pool.tensor_tensor(q_rope[:, :], q_rope[:, :], q_swap[:, :], ALU.add).then_inc(rope_done, 1)

            def compressed_softmax(m, i):
                wide = [P, 2 * QT, N_PAD]
                pool.wait_ge(cmp_dve, 4 * m + 2)
                apart(pool)
                pool.tensor_tensor(pc[:, :, :], pc[:, :, :], pc_max[:, :].unsqueeze(2).broadcast_to(wide),
                                   ALU.subtract).then_inc(cmp_pool, 1)
                pool.wait_ge(cmp_dve, 4 * m + 4)
                apart(pool)
                inv = pc_inv[:, :].rearrange("p (q h) -> p q h", h=2)
                pool.tensor_tensor(inv, inv, gates[:, :, bass.ds(2 * i, 2)], ALU.mult).then_inc(cmp_pool, 1)
                pool.wait_ge(cmp_pool, 3 * m + 2)
                apart(pool)
                pool.tensor_tensor(pc[:, :, :], pc[:, :, :], pc_inv[:, :].unsqueeze(2).broadcast_to(wide),
                                   ALU.mult).then_inc(cmp_pool, 1)

            def body(l, prev, att, proj):
                if att.nsa:
                    compressed_softmax(att.l * PAIRS + att.i, att.i)
                if proj.nsa:
                    rotate(l, 2 + proj.i)
                elif not proj.gates:
                    pool.wait_ge(f_saved, 32 * (l + 1))
                    pool.wait_ge(s_mm, att.s0 + 1)
                    apart(pool)
                    pool.dma_start(f_row[32 * proj.b:32 * proj.b + 4, :],
                                   f_dram[bass.ds(2 * proj.i, 2)].rearrange("h a t -> (h a) t")
                                   ).then_inc(f_landed, 16)

            pool.wait_ge(rope_landed, 32)
            with pool.Fori(0, DEPTH) as l:
                pool.wait_ge(x_done, KT * (l + 1))
                apart(pool)
                pool.dma_start(x_dram, xT[:, :, :]).then_inc(x_saved, 16)
                for k in range(1, KT, 2):
                    h_remainder(pool, l, k)
                pool.wait_ge(h_lo_done[0], KT // 2 * (l + 1))
                apart(pool)
                pool.wait_ge(x_saved, 16 * (l + 1))
                apart(pool)
                for v in (v_hi, v_lo):
                    flat = v[:, :, :, :, :].rearrange("p b s k c -> p (b s k) c")
                    pool.memset(flat[:, :, 0:HD].bitcast(F32), 0.0).then_inc(pads, 1)
                pool.memset(c_blk[:, :, :, :, N_CMP:N_PAD].rearrange("p a j g n -> p (a j g) n"),
                            0.0).then_inc(pads, 1)
                for s in range(2):
                    rotate(l, s)
                rotate(l, 2)
                pool.wait_ge(c_out_mm, 2 * (l + 1))
                apart(pool)
                for pt in (pt_hi, pt_lo):
                    pool.memset(pt[:, :, 3 * 384 + 2 * P:3 * 384 + 3 * P].bitcast(F32), 0.0).then_inc(pads, 1)
                pool.wait_ge(f_step, 6 * (l + 1))
                apart(pool)
                pool.dma_start(f_dram[:, 0, :], f_hi[:, :]).then_inc(f_saved, 16)
                pool.dma_start(f_dram[:, 1, :], f_lo[:, :]).then_inc(f_saved, 16)
                pool.wait_ge(f_saved, 32 * (l + 1))
                apart(pool)
                bodies(pool, l, body)
                pool.wait_ge(y_mul, 2 * PAIRS * (l + 1) + 2)
                apart(pool)
                pool.dma_start(xT[:, :, :], x_dram).then_inc(x_back, 16)

        @block.scalar
        def _(act):
            def split_hi(half, par, width=P, wait=True):
                act.wait_ge(w_landed[par], 16 * (half + 1))
                if wait:
                    act.wait_ge(unit_mm, 2 * half + par - 1)
                act.activation(w_hi[:, par, :, 0:width], w_raw[:, par, :, 0:width],
                               ACT.Copy).then_inc(w_hi_done, 1)

            def square(n, k, par):
                act.wait_ge(x_done, KT * n + k + 1)
                if not (isinstance(k, int) and k < 2):
                    act.wait_ge(sq_added, (KT - 1) * n + k - 1)
                act.activation(squares[:, par:par + 1, :], xT[:, bass.ds(k, 1), :],
                               ACT.Square).then_inc(sq_done, 1)

            def norm(n, between=None, final=False):
                if between is not None:
                    between()
                act.wait_ge(var_done, n + 1)
                act.activation(rstd[:, :], rstd[:, :], ACT.Sqrt).then_inc(std_done, 1)
                if final:
                    return
                for k in range(KT):
                    act.wait_ge(h_raw_done, KT * n + k + 1)
                    act.activation(h_hi[:, k, :], h_raw[:, k % H_RING, :], ACT.Copy).then_inc(h_hi_done, 1)

            def raw_copy(half, par, c, waits):
                act.wait_ge(unit_mm, 2 * half + par + 1)
                for s, value in waits:
                    act.wait_ge(s, value)
                act.activation(q_raw[:, :], acc[par][:, :], ACT.Copy).then_inc(raw_done, 1)

            def swap_copy(half, par, c, places=range(4), c_prev=True):
                if c_prev and 0 in places:
                    act.wait_ge(rope_done, c)
                for n in places:
                    to = 32 * (n ^ 1)
                    ins = act.activation(q_swap[to:to + 32, :], acc[par][32 * n:32 * n + 32, :], ACT.Copy)
                if 3 in places:
                    ins.then_inc(swap_done, 1)

            def q_round(src, b, waits, heads=(0, 1)):
                for s, value in waits:
                    act.wait_ge(s, value)
                for h in heads:
                    ins = act.activation(q_st[own(h), b, h, :], src[own(h), :], ACT.Copy)
                if 1 in heads:
                    ins.then_inc(part_hi_done, 1)

            def k_round(src, places, waits):
                for s, value in waits:
                    act.wait_ge(s, value)
                for h, (b, stream) in enumerate(places):
                    for rows in (own(h), other(h)):
                        ins = act.activation(kk_hi[rows, b, stream, :], src[own(h), :], ACT.Copy)
                ins.then_inc(part_hi_done, 1)

            def v_copy(half, par, to, waits):
                act.wait_ge(unit_mm, 2 * half + par + 1)
                for s, value in waits:
                    act.wait_ge(s, value)
                act.activation(to, acc[par][:, :], ACT.Copy).then_inc(v_raw_done, 1)

            def v_round(n, to):
                act.wait_ge(v_turned, n + 1)
                act.activation(to, misc[:, :].rearrange("p (k s d) -> p s k d", k=QT, s=2),
                               ACT.Copy).then_inc(v_hi_done, 1)

            def z_tanh_of(half, par, r, b):
                act.wait_ge(unit_mm, 2 * half + par + 1)
                act.wait_ge(y_mul, r + 1)
                act.activation(z_silu[:, b, :], acc[par][:, :], ACT.Tanh, scale=0.5).then_inc(z_th_done, 1)

            def body(l, prev, att, proj):
                plan = Body(prev, att, proj)
                todo = {}

                def at(slot, what):
                    todo.setdefault(slot, []).append(what)

                for slot, units in plan.begin.items():
                    for u in units:
                        nxt = proj.unit(u + 1)
                        at(slot, lambda nxt=nxt: split_hi(*nxt))
                if not proj.gates:
                    if proj.nsa:
                        c = l * 10 + 2 + proj.i
                        raw_waits = [(cmp_s, att.l * PAIRS + att.i + 1)]
                        q_waits = [(rope_done, c + 1), (s_mm, att.s0 + 1)]
                        at(plan.at_end(0, 1), lambda: raw_copy(*proj.unit(0), c, raw_waits))
                        at(plan.at_end(0, 2), lambda: swap_copy(*proj.unit(0), c, (0, 1)))
                        at(plan.at_end(0, 3), lambda: swap_copy(*proj.unit(0), c, (2, 3)))
                        at(plan.at_end(0, 6), lambda: q_round(q_rope, proj.b, q_waits, (0,)))
                        at(plan.at_end(0, 7), lambda: q_round(q_rope, proj.b, [], (1,)))
                        at(plan.at_end(1, 1), lambda: z_tanh_of(*proj.unit(1), proj.r, proj.b))
                    else:
                        n = l * 10 + 2 + proj.i
                        q_waits = [(unit_mm, 2 * proj.half + 1), (s_mm, att.s0 + 1)]
                        k_waits = [(unit_mm, 2 * proj.half + 2)]
                        places = [(proj.b, 0), (proj.b, 1)]
                        v_waits = [(cmp_s, PAIRS * (l + 1))] if att.nsa else [(v_turned, n)]
                        at(plan.at_end(0, 1), lambda: q_round(acc[0], proj.b, q_waits))
                        at(plan.at_end(1, 1), lambda: k_round(acc[1], places, k_waits))
                        at(plan.at_end(2, 1), lambda: v_copy(*proj.unit(2), q_raw[:, :], v_waits))
                        at(plan.at_end(2, 2), lambda: v_round(n, v_hi[:, proj.b, :, :, HD:2 * HD]))
                        at(plan.at_end(3, 1), lambda: z_tanh_of(*proj.unit(3), proj.r, proj.b))

                def exp_step(pair, s):
                    t = pair.s0 + s
                    ring, width = s % SM_RING, P * (s % QT + 1)
                    act.wait_ge(s_max, t + 1)
                    act.activation(prob[:, ring, 0:width], prob[:, ring, 0:width], ACT.Exp,
                                   bias=row_max[:, ring:ring + 1], scale=-1.0,
                                   accum_out=row_sum[:, ring:ring + 1]).then_inc(s_exp, 1)

                def hi_step(pair, s):
                    a, qt = divmod(s, QT)
                    act.wait_ge(s_turned, pair.s0 + s + 1)
                    if qt == 0 and not (prev is None and a < 2):
                        act.wait_ge(pv_mm, pair.a0 + a - 1)
                    act.activation(pt_tiles(pt_hi, a, qt), turned_tiles(s, qt), ACT.Copy)\
                        .then_inc(pt_hi_done, 1)

                if att.nsa:
                    m = att.l * PAIRS + att.i

                    def cmp_exponent():
                        act.wait_ge(cmp_pool, 3 * m + 1)
                        act.activation(pc[:, :, :], pc[:, :, :], ACT.Exp, scale=SCALE).then_inc(cmp_exp, 1)

                    def cmp_copy():
                        act.wait_ge(cmp_turned, m + 1)
                        act.activation(pc_t[:, :], misc[0:2 * N_PAD, :], ACT.Copy).then_inc(cmp_pt, 1)

                    at(3, cmp_exponent)
                    at(5, cmp_copy)

                last = max([plan.slots] + [k + 1 for k in todo])
                for s in range(last):
                    if s < plan.steps:
                        exp_step(att, s)
                    if s < plan.slots and s - LAG_TURN < plan.steps and plan.step(s - LAG_TURN):
                        hi_step(*plan.step(s - LAG_TURN))
                    for what in todo.get(s, []):
                        what()

            with nc.allow_non_contiguous_dma(reason="a few kB of per-channel constants"):
                for l in range(DEPTH):
                    act.dma_start(gains[:, l, :], norm_g[l].rearrange("(k p) -> p k", p=P)).then_inc(consts_dma, 16)
                act.dma_start(gains[:, DEPTH, :], final_g.rearrange("(k p) -> p k", p=P)).then_inc(consts_dma, 16)
                act.dma_start(b_f[:, :], b_forget.rearrange("l h -> h l")).then_inc(consts_dma, 16)
            for k in range(KT):
                square(0, k, k % 2)
                if k == KT // 2:
                    for to, src in ((cosT[:, :], rope_c), (sinT[:, :], rope_s)):
                        act.dma_start(to, src).then_inc(rope_landed, 16)
            with act.Fori(0, DEPTH) as l:
                half0 = l * (U_ALL // 2)
                norm(l, between=lambda: split_hi(half0, 0, kv_widths[0], wait=False))
                def kv(n):
                    return half0 + n // 2, n % 2

                def compression_source(a):
                    half, par_u = kv(a)
                    act.wait_ge(unit_mm, 2 * half + par_u + 1)
                    for g in range(GROUPS):
                        for par in range(2):
                            src = acc[par_u][own(g), :].rearrange("d (m a) -> d a m", a=2)
                            ins = act.activation(c_src[own(par), a, g, :], src[:, par, :], ACT.Copy)
                    ins.then_inc(c_src_done, 1)

                def compression_tanh(a):
                    act.wait_ge(c_hid_mm, 2 * l + a + 1)
                    act.activation(c_th[:, a, :], turned[a][:, 0:GROUPS * N_PAD], ACT.Tanh, scale=0.5)\
                        .then_inc(c_th_done, 1)

                split_hi(*kv(1), kv_widths[1], wait=False)
                split_hi(*kv(2), kv_widths[2])
                compression_source(0)
                split_hi(*kv(3), kv_widths[3])
                compression_source(1)
                split_hi(*kv(4), kv_widths[4])
                half, par = kv(2)
                act.wait_ge(unit_mm, 2 * half + par + 1)
                act.activation(g_th[:, :], acc[par][0:3 * HEADS, :], ACT.Tanh, scale=0.5)\
                    .then_inc(g_th_done, 1)
                split_hi(*kv(5), kv_widths[5])
                act.wait_ge(f_step, 6 * l + 2)
                act.activation(f_b[:, :], f_b[:, :], ACT.Exp, scale=-1.0).then_inc(f_exp, 1)
                compression_tanh(0)
                split_hi(*kv(6), kv_widths[6])
                raw_copy(*kv(4), l * 10, [])
                swap_copy(*kv(4), l * 10, c_prev=False)
                compression_tanh(1)
                split_hi(*kv(7), kv_widths[7])
                k_round(q_rope, [(0, 0), (1, 0)], [(rope_done, l * 10 + 1)])
                raw_copy(*kv(5), l * 10 + 1, [(rope_done, l * 10 + 1)])
                swap_copy(*kv(5), l * 10 + 1)
                act.wait_ge(f_exp, 3 * l + 1)
                act.activation(f_b[:, :], f_b[:, :], ACT.Ln, bias=1.0).then_inc(f_exp, 1)
                split_hi(*kv(8))
                v_copy(*kv(6), z_silu[:, 0, :], [])
                k_round(q_rope, [(0, 1), (1, 1)], [(rope_done, l * 10 + 2)])
                split_hi(*kv(9))
                raw_copy(*kv(7), l * 10 + 2, [(rope_done, l * 10 + 2)])
                swap_copy(*kv(7), l * 10 + 2)
                act.wait_ge(f_step, 6 * l + 5)
                act.activation(f_hi[:, :], f_b[:, :], ACT.Copy).then_inc(f_exp, 1)
                act.wait_ge(x_saved, 16 * (l + 1))
                v_round(l * 10, v_hi[:, :, 0, :, HD:2 * HD])
                split_hi(*kv(10))
                v_copy(*kv(8), z_silu[:, 1, :], [])
                q_round(q_rope, 0, [(rope_done, l * 10 + 3)])
                z_tanh_of(*kv(9), 2 * PAIRS * l, 0)
                v_round(l * 10 + 1, v_hi[:, :, 1, :, HD:2 * HD])

                bodies(act, l, body)

                def gate_tanh(half, par):
                    act.wait_ge(unit_mm, 2 * half + par + 1)
                    act.activation(m_th[:, par, :], acc[par][:, :], ACT.Tanh, scale=0.5)\
                        .then_inc(m_th_done, 1)

                def merge_rest(half, e):
                    split_hi(half + 2, 0)
                    act.wait_ge(m_sum_done, KT * l + e + 1)
                    act.activation(m_hi[:, bass.ds(e, 1), :], m_sum[:, 0:1, :], ACT.Copy, scale=0.5)\
                        .then_inc(m_hi_done, 1)

                half = half0 + U_MERGE // 2
                act.wait_ge(y_mul, 2 * PAIRS * (l + 1) + 2)
                for mixer in range(2):
                    gate_tanh(half, mixer)
                    for k in range(0, KT, 2):
                        act.activation(yt_hi[:, mixer, k:k + 2, :], y_all[mixer][:, k:k + 2, :],
                                       ACT.Copy).then_inc(yt_hi_done, 1)
                    if mixer == 0:
                        split_hi(half + 1, 1)
                merge_rest(half, 0)
                with act.Fori(1, KT) as e:
                    half = half0 + U_MERGE // 2 + 2 * e
                    for par in range(2):
                        split_hi(half + par, 1 - par)
                        gate_tanh(half, par)
                    split_hi(half + 1, 1)
                    merge_rest(half, e)
                out0 = half0 + U_OUT // 2
                split_hi(out0, 1)
                split_hi(out0 + 1, 0)
                square(l + 1, 0, 0)
                with act.Fori(1, KT // 2 - 1) as j:
                    split_hi(out0 + j, 1)
                    square(l + 1, 2 * j - 1, 1)
                    split_hi(out0 + j + 1, 0)
                    square(l + 1, 2 * j, 0)
                split_hi(out0 + KT // 2 - 1, 1)
                for k in range(KT - 3, KT):
                    square(l + 1, k, k % 2)
            norm(DEPTH, final=True)
            for m in range(1, 2 * QT, 2):
                half, i = divmod(m, QT)
                act.wait_ge(o_turned, m + 1)
                act.activation(o_nat[:, i, D // 2 * half:D // 2 * half + D // 2], turned[1][:, :],
                               ACT.Copy).then_inc(o_copied[1], 1)

        @block.vector
        def _(dve):
            def split_lo(half, par, width=P):
                dve.wait_ge(w_hi_done, 2 * half + par + 1)
                dve.tensor_tensor(w_lo[:, par, :, 0:width], w_raw[:, par, :, 0:width],
                                  w_hi[:, par, :, 0:width], ALU.subtract).then_inc(w_lo_done, 1)

            def add_squares(n, k, par):
                dve.wait_ge(sq_done, KT * n + k + 1)
                if isinstance(k, int) and k == 0:
                    ins = dve.tensor_copy(sq_sum[:, :], squares[:, par, :])
                else:
                    dve.wait_ge(sq_added, (KT - 1) * n + k)
                    apart(dve)
                    ins = dve.tensor_tensor(sq_sum[:, :], sq_sum[:, :], squares[:, par, :], ALU.add)
                ins.then_inc(sq_added, 1)

            def norm(n, between=None, final=False):
                dve.wait_ge(sq_summed, n + 1)
                dve.tensor_scalar(rstd[:, :], misc[:, :], 1.0 / D, EPS, ALU.mult, ALU.add).then_inc(var_done, 1)
                if between is not None:
                    between()
                dve.wait_ge(std_done, n + 1)
                dve.reciprocal(rstd[:, :], rstd[:, :]).then_inc(rstd_done, 1)
                dve.wait_ge(rstd_done, n + 1)

                def raw(k):
                    if k >= H_RING and not final:
                        dve.wait_ge(h_lo_done[k % 2], KT // 2 * n + (k - H_RING) // 2 + 1)
                    to = o_t[:, k, :] if final else h_raw[:, k % H_RING, :]
                    gain = gains[:, DEPTH, k:k + 1] if final else gains[:, bass.ds(n, 1), k]
                    dve.scalar_tensor_tensor(to, xT[:, k, :], gain, rstd[:, :],
                                             ALU.mult, ALU.mult).then_inc(h_raw_done, 1)

                for k in range(KT):
                    raw(k)
                    if k % 2 and k > 1 and not final:
                        h_remainder(dve, n, k - 3)
                if not final:
                    h_remainder(dve, n, KT - 2)

            def q_rest(src, b, parts):
                dve.wait_ge(part_hi_done, parts + 1)
                for h in range(2):
                    ins = dve.tensor_tensor(q_st[other(h), b, h, :], src[own(h), :], q_st[own(h), b, h, :],
                                            ALU.subtract)
                ins.then_inc(part_lo_done, 1)

            def k_rest(src, places, parts, both):
                dve.wait_ge(part_hi_done, parts + 1)
                for h, (b, stream) in enumerate(places):
                    for rows in (own(h), other(h))[:2 if both else 1]:
                        ins = dve.tensor_tensor(kk_lo[rows, b, stream, :], src[own(h), :],
                                                kk_hi[own(h), b, stream, :], ALU.subtract)
                ins.then_inc(part_lo_done, 1)

            def v_rest(n, to, hi):
                dve.wait_ge(v_hi_done, n + 1)
                dve.tensor_tensor(to, misc[:, :].rearrange("p (k s d) -> p s k d", k=QT, s=2), hi,
                                  ALU.subtract).then_inc(v_lo_done, 1)

            def z_silu_of(half, par, r, b):
                dve.wait_ge(z_th_done, r + 1)
                dve.scalar_tensor_tensor(z_silu[:, b, :], z_silu[:, b, :], 1.0, acc[par][:, :],
                                         ALU.add, ALU.mult).then_inc(z_done, 1)

            def body(l, prev, att, proj):
                plan = Body(prev, att, proj)
                todo = {}

                def at(slot, what):
                    todo.setdefault(slot, []).append(what)

                for slot, units in plan.begin.items():
                    for u in units:
                        at(slot + 1, lambda nxt=proj.unit(u + 1): split_lo(*nxt))
                if not proj.gates:
                    if proj.nsa:
                        c, n = l * 10 + 2 + proj.i, l * 26 + 2 + proj.i
                        at(plan.at_end(0, 8), lambda: q_rest(q_rope, proj.b, n))
                        at(plan.at_end(1, 1), lambda: z_silu_of(*proj.unit(1), proj.r, proj.b))
                    else:
                        n, v = l * 26 + 10 + 2 * proj.i, l * 10 + 2 + proj.i
                        places = [(proj.b, 0), (proj.b, 1)]
                        at(plan.at_end(0, 1), lambda: q_rest(acc[0], proj.b, n))
                        at(plan.at_end(1, 1), lambda: k_rest(acc[1], places, n + 1, False))
                        at(plan.at_end(2, 2), lambda: v_rest(v, v_lo[:, proj.b, :, :, HD:2 * HD],
                                                             v_hi[:, proj.b, :, :, HD:2 * HD]))
                        at(plan.at_end(3, 1), lambda: z_silu_of(*proj.unit(3), proj.r, proj.b))

                def max_step(pair, s):
                    t, qt, ring = pair.s0 + s, s % QT, s % SM_RING
                    width = P * (qt + 1)
                    dve.wait_ge(s_mm, t + 1)
                    if s >= SM_RING or prev is not None:
                        dve.wait_ge(s_turned, t - SM_RING + 1)
                    apart(dve)
                    dve.tensor_tensor_reduce(prob[:, ring, 0:width], scores[s % 2][:, 0:width],
                                             causal[:, T - width:T], -SCALE, BIG, ALU.add, ALU.min,
                                             row_max[:, ring:ring + 1]).then_inc(s_max, 1)

                def invert_step(pair, s):
                    dve.wait_ge(s_exp, pair.s0 + s + 1)
                    ring = s % SM_RING
                    dve.reciprocal(row_inv[:, ring:ring + 1], row_sum[:, ring:ring + 1]).then_inc(s_inv, 1)

                def scale_step(pair, s):
                    qt, ring = s % QT, s % SM_RING
                    h, _, _, branch = pair.atts()[s // QT]
                    p = prob[:, ring, 0:P * (qt + 1)]
                    dve.wait_ge(s_inv, pair.s0 + s + 1)
                    if branch is None:
                        ins = dve.tensor_scalar(p, p, row_inv[:, ring:ring + 1], None, ALU.mult)
                    else:
                        gate = gates[:, qt, bass.ds(2 * pair.i + HEADS * branch + h, 1)]
                        ins = dve.tensor_scalar(p, p, row_inv[:, ring:ring + 1], gate, ALU.mult, ALU.mult)
                    ins.then_inc(s_scaled, 1)

                def lo_step(pair, s):
                    a, qt = divmod(s, QT)
                    dve.wait_ge(pt_hi_done, pair.s0 + s + 1)
                    dve.tensor_tensor(pt_tiles(pt_lo, a, qt), turned_tiles(s, qt), pt_tiles(pt_hi, a, qt),
                                      ALU.subtract).then_inc(pt_lo_done, 1)

                def gate_output(pair):
                    dve.wait_ge(pv_mm, pair.a0 + pair.steps // QT)
                    dve.wait_ge(z_done, pair.r + 2)
                    y = y_all[0 if pair.nsa else 1][:, bass.ds(pair.i, 1), :]
                    dve.scalar_tensor_tensor(y, o_pair[:, :].unsqueeze(1), 0.5, z_silu[:, pair.b:pair.b + 1, :],
                                             ALU.mult, ALU.mult).then_inc(y_mul, 1)

                if prev is not None:
                    at(LAG_PV, lambda: gate_output(prev))
                if proj.gates:
                    at(plan.steps + LAG_PV, lambda: gate_output(att))

                if att.nsa:
                    m = att.l * PAIRS + att.i

                    def cmp_top():
                        dve.wait_ge(cmp_s, m + 1)
                        flat = misc[:, 0:2 * QT * N_PAD].rearrange("p (a n) -> p a n", n=N_PAD)
                        mask = cmp_mask[:, :, :, :].rearrange("p q h n -> p (q h) n")
                        dve.tensor_tensor(pc[:, :, :], flat, mask, ALU.add).then_inc(cmp_dve, 1)
                        dve.wait_ge(cmp_dve, 4 * m + 1)
                        dve.tensor_reduce(pc_max[:, :], pc[:, :, :], AX_X, ALU.max).then_inc(cmp_dve, 1)

                    def cmp_norm():
                        dve.wait_ge(cmp_exp, m + 1)
                        dve.tensor_reduce(pc_sum[:, :], pc[:, :, :], AX_X, ALU.add).then_inc(cmp_dve, 1)
                        dve.wait_ge(cmp_dve, 4 * m + 3)
                        dve.reciprocal(pc_inv[:, :], pc_sum[:, :]).then_inc(cmp_dve, 1)
                    at(2, cmp_top)
                    at(4, cmp_norm)

                last = max([plan.slots] + [k + 1 for k in todo])
                for s in range(last):
                    now = s < plan.slots

                    def step(lag):
                        return plan.step(s - lag) if now and s - lag < plan.steps else None

                    if step(LAG_SCALE):
                        invert_step(*step(LAG_SCALE))
                    if step(0):
                        max_step(*step(0))
                    if step(LAG_SCALE):
                        scale_step(*step(LAG_SCALE))
                    if step(LAG_PT):
                        lo_step(*step(LAG_PT))
                    for what in todo.get(s, []):
                        what()

            dve.memset(row_inv[:, 0:1], 0.0).then_inc(w_lo_done, 2)
            dve.memset(row_inv[:, 1:2], 0.0).then_inc(z_done, 1)
            dve.memset(row_inv[:, 2:3], 0.0).then_inc(y_mul, 2)
            dve.memset(row_inv[:, 3:4], 0.0).then_inc(m_part, 2)
            dve.wait_ge(consts, N_CONSTS)
            dve.tensor_copy(sel[:, :, :], sel_f[:, :, :]).then_inc(sel_done, 1)
            for k in range(KT):
                dve.wait_ge(x_turned, k + 1)
                dve.tensor_copy(xT[:, k, :], turned[k % 2][:, :]).then_inc(x_done, 1)
                if k:
                    add_squares(0, k - 1, (k - 1) % 2)
            dve.wait_ge(consts_dma, 16 * (DEPTH + 2))

            with dve.Fori(0, DEPTH) as l:
                half0 = l * (U_ALL // 2)

                def kv(n):
                    return half0 + n // 2, n % 2

                norm(l, between=lambda: split_lo(*kv(0), kv_widths[0]))
                def blocks(a):
                    dve.wait_ge(c_src_done, 2 * l + a + 1)
                    for j in range(CJ):
                        src = c_src[:, a, :, j:j + 8 * (N_CMP - 1) + 1:8]
                        ins = dve.tensor_scalar(c_blk[:, a, j, :, 0:N_CMP], src, c_pe[:, a, j:j + 1], None, ALU.add)
                    ins.then_inc(c_blk_done, 1)

                def hidden(a):
                    dve.wait_ge(c_th_done, 2 * l + a + 1)
                    dve.scalar_tensor_tensor(c_hid[:, a, :], c_th[:, a, :], 1.0, turned[a][:, 0:GROUPS * N_PAD],
                                             ALU.add, ALU.mult).then_inc(c_hid_done, 1)

                split_lo(*kv(1), kv_widths[1])
                split_lo(*kv(2), kv_widths[2])
                dve.wait_ge(c_landed, 160 * (l + 1))
                blocks(0)
                split_lo(*kv(3), kv_widths[3])
                blocks(1)
                split_lo(*kv(4), kv_widths[4])
                dve.wait_ge(unit_mm, 2 * half0 + 4)
                dve.tensor_scalar(f_a[:, :], acc[1][0:HEADS, :], b_f[:, bass.ds(l, 1)], None,
                                  ALU.add).then_inc(f_step, 1)
                dve.wait_ge(f_step, 6 * l + 1)
                dve.scalar_tensor_tensor(f_b[:, :], f_a[:, :], -1.0, f_a[:, :],
                                         ALU.mult, ALU.max).then_inc(f_step, 1)
                split_lo(*kv(5), kv_widths[5])
                dve.wait_ge(g_turned, l + 1)
                dve.tensor_scalar(gates[:, :, :], misc[:, 0:QT * 3 * HEADS].rearrange("p (q c) -> p q c", q=QT),
                                  0.5, 0.5, ALU.mult, ALU.add).then_inc(gates_done, 1)
                dve.wait_ge(gates_done, 2 * l + 1)
                dve.tensor_scalar(gates[:, 0, 0:HEADS], gates[:, 0, 0:HEADS], past_first[:, 0:1], None,
                                  ALU.mult).then_inc(gates_done, 1)
                hidden(0)
                split_lo(*kv(6), kv_widths[6])
                hidden(1)
                split_lo(*kv(7), kv_widths[7])
                k_rest(q_rope, [(0, 0), (1, 0)], l * 26, True)
                dve.wait_ge(f_exp, 3 * l + 2)
                dve.scalar_tensor_tensor(f_a[:, :], f_a[:, :], 0.0, f_b[:, :],
                                         ALU.min, ALU.subtract).then_inc(f_step, 1)
                dve.wait_ge(f_step, 6 * l + 3)
                dve.tensor_tensor_scan(f_b[:, :], ones[0:HEADS, 0:1].broadcast_to([HEADS, T]), f_a[:, :], 0.0,
                                       ALU.mult, ALU.add).then_inc(f_step, 1)
                dve.wait_ge(f_step, 6 * l + 4)
                dve.tensor_scalar(f_b[:, :], f_b[:, :], -1.0 / SCALE, None, ALU.mult).then_inc(f_step, 1)
                split_lo(*kv(8))
                dve.wait_ge(pads, 2)
                dve.wait_ge(c_out_mm, 2 * l + 1)
                ck = scores[0][0:HD, 0:GROUPS * N_PAD].rearrange("d (g n) -> d g n", g=GROUPS)
                for h in range(2):
                    dve.tensor_scalar(kcb[own(h), :, N_PAD * h:N_PAD * h + N_PAD], ck, 0.5, None,
                                      ALU.mult).then_inc(cb_ready, 1)
                dve.wait_ge(c_out_mm, 2 * l + 2)
                cv = scores[1][0:N_PAD, 0:GROUPS * HD].rearrange("n (g d) -> n g d", g=GROUPS)
                for h in range(2):
                    dve.tensor_scalar(vcb[N_PAD * h:N_PAD * h + N_PAD, :, HD * h:HD * h + HD], cv, 0.5, None,
                                      ALU.mult).then_inc(cb_ready, 1)
                k_rest(q_rope, [(0, 1), (1, 1)], l * 26 + 1, True)
                split_lo(*kv(9))
                dve.wait_ge(f_exp, 3 * l + 3)
                dve.tensor_tensor(f_lo[:, :], f_b[:, :], f_hi[:, :], ALU.subtract).then_inc(f_step, 1)
                v_rest(l * 10, v_lo[:, :, 0, :, HD:2 * HD], v_hi[:, :, 0, :, HD:2 * HD])
                split_lo(*kv(10))
                q_rest(q_rope, 0, l * 26 + 2)
                z_silu_of(*kv(9), 2 * PAIRS * l, 0)
                v_rest(l * 10 + 1, v_lo[:, :, 1, :, HD:2 * HD], v_hi[:, :, 1, :, HD:2 * HD])
                dve.wait_ge(gates_done, 2 * l + 2)

                apart(dve)
                bodies(dve, l, body)

                for mixer in range(2):
                    for k in range(0, KT, 2):
                        dve.wait_ge(yt_hi_done, KT * l + KT // 2 * mixer + k // 2 + 1)
                        dve.tensor_tensor(yt_lo[:, mixer, k:k + 2, :], y_all[mixer][:, k:k + 2, :],
                                          yt_hi[:, mixer, k:k + 2, :], ALU.subtract).then_inc(yt_lo_done, 1)
                    if mixer == 0:
                        split_lo(half0 + U_MERGE // 2 + 1, 1)

                def merge_sums(half, e):
                    for n in range(2):
                        if n == 1:
                            split_lo(half + 2, 0)
                        dve.wait_ge(m_th_done, 2 * KT * l + 2 * e + n + 1)
                        dve.wait_ge(unit_mm, 2 * half + 3 + n)
                        dve.scalar_tensor_tensor(m_sum[:, n, :], m_th[:, n, :], 1.0, acc[n][:, :],
                                                 ALU.add, ALU.mult).then_inc(m_part, 1)
                    dve.wait_ge(m_part, 2 * KT * l + 2 * e + 4)
                    dve.tensor_tensor(m_sum[:, 0, :], m_sum[:, 0, :], m_sum[:, 1, :], ALU.add).then_inc(m_sum_done, 1)
                    dve.wait_ge(m_hi_done, KT * l + e + 1)
                    dve.scalar_tensor_tensor(m_lo[:, bass.ds(e, 1), :], m_sum[:, 0:1, :], 0.5,
                                             m_hi[:, bass.ds(e, 1), :], ALU.mult, ALU.subtract
                                             ).then_inc(m_lo_done, 1)

                merge_sums(half0 + U_MERGE // 2, 0)
                with dve.Fori(1, KT) as e:
                    half = half0 + U_MERGE // 2 + 2 * e
                    split_lo(half, 1)
                    split_lo(half + 1, 0)
                    split_lo(half + 1, 1)
                    merge_sums(half, e)

                def residual(j, par):
                    dve.wait_ge(unit_mm, 2 * (half0 + U_OUT // 2 + j) + par + 1)
                    tile = xT[:, bass.ds(2 * j + par, 1), :]
                    dve.tensor_tensor(tile, tile, acc[par][:, :].unsqueeze(1), ALU.add)\
                        .then_inc(x_done, 1)

                dve.wait_ge(x_back, 16 * (l + 1))
                apart(dve)
                out0 = half0 + U_OUT // 2
                split_lo(out0, 1)
                residual(0, 0)
                split_lo(out0 + 1, 0)
                add_squares(l + 1, 0, 0)
                residual(0, 1)
                with dve.Fori(1, KT // 2 - 1) as j:
                    split_lo(out0 + j, 1)
                    add_squares(l + 1, 2 * j - 1, 1)
                    residual(j, 0)
                    split_lo(out0 + j + 1, 0)
                    add_squares(l + 1, 2 * j, 0)
                    residual(j, 1)
                split_lo(out0 + KT // 2 - 1, 1)
                add_squares(l + 1, KT - 3, 1)
                residual(KT // 2 - 1, 0)
                add_squares(l + 1, KT - 2, 0)
                residual(KT // 2 - 1, 1)
            norm(DEPTH, final=True)
            for m in range(0, 2 * QT, 2):
                half, i = divmod(m, QT)
                dve.wait_ge(o_turned, m + 1)
                dve.tensor_copy(o_nat[:, i, D // 2 * half:D // 2 * half + D // 2], turned[0][:, :]
                                ).then_inc(o_copied[0], 1)

        @block.tensor
        def _(pe):
            def sum_squares(n):
                pe.wait_ge(sq_added, (KT - 1) * (n + 1))
                pe.matmul(misc[:, :], ones[:, :], sq_sum[:, :], start=True, stop=False)
                pe.wait_ge(sq_done, KT * (n + 1))
                pe.matmul(misc[:, :], ones[:, :], squares[:, 1, :], start=False, stop=True).then_inc(sq_summed, 1)

            def unit_piece(first, last, half, par, width=P, hi=None, lo=None, each_k=None, free=None):
                for n in range(first, last):
                    k, which = divmod(n, 3)
                    if n == 0:
                        pe.wait_ge(w_lo_done, 2 * half + par + 3)
                        if free is not None:
                            pe.wait_ge(*free)
                    if each_k is not None and which == 0:
                        pe.wait_ge(*each_k(k))
                    w = w_lo if which == 2 else w_hi
                    rhs = (lo if which == 1 else hi)[:, k, :] if hi is not None else \
                        (h_lo if which == 1 else h_hi)[:, k, :]
                    ins = pe.matmul(acc[par][0:width, :], w[:, par, k, 0:width], rhs,
                                    start=(n == 0), stop=(n == 23))
                    if n == 23:
                        ins.then_inc(unit_mm, 1)

            def bank_read(l, pair, part):
                if pair.gates:
                    return (v_raw_done, l * 10 + 10) if part == 0 else (z_done, 2 * PAIRS * (l + 1) + 1)
                if part == 0 and (pair.nsa or pair.first):
                    return swap_done, l * 10 + 2 + (pair.i if pair.nsa else PAIRS)
                if part == 0:
                    return v_raw_done, l * 10 + 2 + pair.i
                if part == 1:
                    return z_done, pair.r + 1
                return part_lo_done, l * 26 + 10 + 2 * pair.i + part - 1

            def turn_v(n, src):
                pe.wait_ge(v_raw_done, n + 1)
                for kt in range(QT):
                    ins = pe.transpose(misc[:, P * kt:P * kt + P], src[:, P * kt:P * kt + P], ident[:, :])
                ins.then_inc(v_turned, 1)

            def body(l, prev, att, proj):
                plan = Body(prev, att, proj)
                extra = {}
                if not proj.nsa and not proj.gates:
                    v = l * 10 + 2 + proj.i

                    def turn():
                        if not att.nsa:
                            pe.wait_ge(v_lo_done, v)
                        turn_v(v, q_raw)

                    extra.setdefault(plan.at_end(2, 2), []).append(turn)

                def score_step(pair, s):
                    a, qt = divmod(s, QT)
                    h, b, stream, branch = pair.atts()[a]
                    n, cols = key_cols(qt), slice(P * qt, P * qt + P)
                    if s == 0:
                        pe.wait_ge(part_lo_done, l * 26 + (3 + pair.i if pair.nsa else 12 + 2 * pair.i))
                        if not pair.nsa:
                            pe.wait_ge(f_landed, 16 * (pair.l * PAIRS + pair.i + 1))
                    if s >= 2 or prev is not None or pair is not att:
                        pe.wait_ge(s_max, pair.s0 + s - 1)
                    to = scores[s % 2][:, 0:n]
                    pe.matmul(to, q_st[:, pair.b, h, cols], kk_hi[:, b, stream, 0:n], start=True, stop=False)
                    ins = pe.matmul(to, q_st[own(h), pair.b, h, cols], kk_lo[own(h), b, stream, 0:n], start=False,
                                    stop=branch is not None)
                    if branch is None:
                        rows = slice(32 * b, 32 * b + 4)
                        ins = pe.matmul(to, sel[rows, h, :], f_row[rows, 0:n], start=False, stop=True)
                    ins.then_inc(s_mm, 1)

                def turn_step(pair, s):
                    qt = s % QT
                    pe.wait_ge(s_scaled, pair.s0 + s + 1)
                    if s >= 2 or prev is not None:
                        pe.wait_ge(pt_lo_done, pair.s0 + s - 1)
                    for kt in range(qt + 1):
                        ins = pe.transpose(turned[s % 2][:, P * kt:P * kt + P],
                                           prob[:, s % SM_RING, P * kt:P * kt + P], ident[:, :])
                    ins.then_inc(s_turned, 1)

                def value_step(pair, a):
                    pe.wait_ge(pt_lo_done, pair.s0 + QT * (a + 1))
                    if a == 0:
                        if not pair.nsa:
                            pe.wait_ge(y_mul, pair.r + 2)
                        pe.wait_ge(v_lo_done, l * 10 + 2 + (0 if pair.nsa else pair.i + 1))
                    h, b, stream, _ = pair.atts()[a]
                    width = (HD, P)[h]
                    last = a == pair.steps // QT - 1
                    for kt in range(QT):
                        q0 = min(P * kt, T - 2 * P)
                        for m, (v, pt) in enumerate(((v_hi, pt_hi), (v_hi, pt_lo), (v_lo, pt_hi))):
                            ins = pe.matmul(o_pair[0:width, q0:T], v[:, b, stream, kt, 2 * HD - width:2 * HD],
                                            pt[:, a % 2, 384 * kt + q0:384 * kt + T],
                                            start=not pair.nsa and (a, kt, m) == (0, 0, 0),
                                            stop=pair.nsa and last and (kt, m) == (QT - 1, 2))
                    if last and not pair.nsa:
                        zeros = pt_hi[:, a % 2, 3 * 384 + 2 * P:3 * 384 + 3 * P]
                        ins = pe.matmul(o_pair[:, 0:P], v_hi[:, b, stream, 0, :], zeros, start=False, stop=True)
                    ins.then_inc(pv_mm, 1)

                def cmp_scores():
                    pe.wait_ge(raw_done, l * 10 + 2 + att.i + 1)
                    pe.wait_ge(cb_ready, 4 * (l + 1))
                    pe.wait_ge(v_lo_done, l * 10 + 2)
                    apart(pe)
                    for qt in range(QT):
                        ins = pe.matmul(misc[:, 64 * qt:64 * qt + 64], q_raw[:, P * qt:P * qt + P],
                                        kcb[:, att.g, :], start=True, stop=True)
                    ins.then_inc(cmp_s, 1)

                def cmp_turn():
                    pe.wait_ge(cmp_pool, 3 * (att.l * PAIRS + att.i) + 3)
                    apart(pe)
                    for qt in range(QT):
                        ins = pe.transpose(misc[0:2 * N_PAD, P * qt:P * qt + P],
                                           pc[:, 2 * qt:2 * qt + 2, :].rearrange("p h n -> p (h n)"), ident[:, :])
                    ins.then_inc(cmp_turned, 1)

                def cmp_values():
                    pe.wait_ge(cmp_pt, att.l * PAIRS + att.i + 1)
                    pe.wait_ge(y_mul, att.r + 2)
                    pe.matmul(o_pair[:, :], vcb[:, att.g, :], pc_t[:, :], start=True, stop=False)

                for s in range(plan.slots):
                    pair_step = plan.step(s - LAG_PV)
                    if s - LAG_PV < plan.steps and pair_step and pair_step[1] % QT == QT - 1:
                        extra.setdefault(s, []).append(
                            lambda which=pair_step: value_step(which[0], which[1] // QT))
                if att.nsa:
                    extra.setdefault(1, []).insert(0, cmp_scores)
                    extra.setdefault(5, []).insert(0, cmp_turn)
                    extra.setdefault(6, []).insert(0, cmp_values)
                if prev is None:
                    score_step(att, 0)

                done = 0
                for s in range(max([plan.slots] + [k + 1 for k in extra])):
                    if s < plan.slots and s - LAG_TURN < plan.steps and plan.step(s - LAG_TURN):
                        turn_step(*plan.step(s - LAG_TURN))
                    if s < plan.slots and plan.step(s + 1) and s < plan.steps:
                        score_step(*plan.step(s + 1))
                    want = plan.cum[s] if s < plan.slots else done
                    while done < want:
                        u = done // 24
                        stop = min(want, 24 * u + 24)
                        unit_piece(done - 24 * u, stop - 24 * u, *proj.unit(u),
                                   free=bank_read(l, proj, u))
                        done = stop
                    for what in extra.get(s, []):
                        what()

            pe.wait_ge(consts, N_CONSTS)
            for k in range(KT):
                pe.wait_ge(x_landed[k // (KT // 2)], 16)
                if k >= 2:
                    pe.wait_ge(x_done, k - 1)
                for i in range(QT):
                    ins = pe.transpose(turned[k % 2][:, P * i:P * i + P], x_nat[:, i, P * k:P * k + P], ident[:, :])
                ins.then_inc(x_turned, 1)
            pe.wait_ge(sel_done, 1)
            sum_squares(0)
            with pe.Fori(0, DEPTH) as l:
                half0 = l * (U_ALL // 2)

                readers = [None, None, (c_src_done, 2 * l + 1), (c_src_done, 2 * l + 2),
                           (g_th_done, l + 1), (f_step, 6 * l + 1), (swap_done, l * 10 + 1), (swap_done, l * 10 + 2),
                           (v_raw_done, l * 10 + 1), (swap_done, l * 10 + 3)]

                def kv(n, **more):
                    unit_piece(0, 24, half0 + n // 2, n % 2, kv_widths[n], free=readers[n], **more)

                def hidden(a):
                    pe.wait_ge(c_blk_done, 2 * l + a + 1)
                    for j in range(CJ):
                        ins = pe.matmul(turned[a][:, 0:GROUPS * N_PAD], c_w1[:, a, j, :],
                                        c_blk[:, a, j, :, :].rearrange("p g n -> p (g n)"),
                                        start=(j == 0), stop=(j == CJ - 1))
                    ins.then_inc(c_hid_mm, 1)

                kv(0, each_k=lambda k: (h_lo_done[k % 2], KT // 2 * l + k // 2 + 1))
                for n in range(1, 5):
                    kv(n)
                pe.wait_ge(pads, 2 + 5 * l + 3)
                pe.wait_ge(c_landed, 160 * (l + 1))
                hidden(0)
                pe.wait_ge(g_th_done, l + 1)
                apart(pe)
                for i in range(QT):
                    ins = pe.transpose(misc[:, 48 * i:48 * i + 48], g_th[:, P * i:P * i + P],
                                       ident[0:3 * HEADS, 0:3 * HEADS])
                ins.then_inc(g_turned, 1)
                kv(5)
                hidden(1)
                kv(6)
                pe.wait_ge(c_hid_done, 2 * l + 1)
                pe.matmul(scores[0][0:HD, 0:64], c_w2[:, 0, :], c_hid[:, 0, :], start=True,
                          stop=True).then_inc(c_out_mm, 1)
                pe.wait_ge(c_hid_done, 2 * l + 2)
                for g in range(GROUPS):
                    ins = pe.matmul(scores[1][0:N_PAD, HD * g:HD * g + HD], c_hid[:, 1, N_PAD * g:N_PAD * g + N_PAD],
                                    c_w2[:, 1, :], start=True, stop=True)
                ins.then_inc(c_out_mm, 1)
                kv(7)
                pe.wait_ge(gates_done, 2 * l + 1)
                turn_v(l * 10, z_silu[:, 0, :])
                kv(8)
                kv(9)
                pe.wait_ge(v_lo_done, l * 10 + 1)
                turn_v(l * 10 + 1, z_silu[:, 1, :])
                pe.wait_ge(pads, 2 + 5 * l + 5)
                apart(pe)
                bodies(pe, l, body)

                for mixer in range(2):
                    unit_piece(0, 24, half0 + U_MERGE // 2 + 1, mixer, hi=yt_hi[:, mixer], lo=yt_lo[:, mixer],
                               each_k=lambda k: (yt_lo_done, KT * l + KT // 2 * mixer + k // 2 + 1),
                               free=(m_th_done, 2 * KT * l + mixer + 1))
                with pe.Fori(1, KT) as e:
                    half = half0 + U_MERGE // 2 + 2 * e
                    for n in range(2):
                        unit_piece(0, 24, half, n, free=(m_part, 2 * KT * l + 2 * e + n + 1))
                    for mixer in range(2):
                        unit_piece(0, 24, half + 1, mixer, hi=yt_hi[:, mixer], lo=yt_lo[:, mixer],
                                   free=(m_th_done, 2 * KT * l + 2 * e + mixer + 1))

                def out_unit(j, par, each_k=None):
                    unit_piece(0, 24, half0 + U_OUT // 2 + j, par, hi=m_hi, lo=m_lo, each_k=each_k,
                               free=(x_done, KT * (l + 1) + 2 * j + par - 1))

                out_unit(0, 0, each_k=lambda k: (m_lo_done, KT * l + k + 1))
                out_unit(0, 1)
                with pe.Fori(1, KT // 2) as j:
                    out_unit(j, 0)
                    out_unit(j, 1)
                sum_squares(l + 1)
            for m in range(2 * QT):
                half, i = divmod(m, QT)
                pe.wait_ge(h_raw_done, KT * DEPTH + QT * (half + 1))
                if m >= 2:
                    pe.wait_ge(o_copied[m % 2], m // 2)
                for c in range(4):
                    ins = pe.transpose(turned[m % 2][:, P * c:P * c + P],
                                       o_t[:, 4 * half + c, P * i:P * i + P], ident[:, :])
                ins.then_inc(o_turned, 1)


_INS = ["x", "norm_g", "w_in", "b_forget", "cmp_pe_k", "cmp_w1_k", "cmp_w2_k", "cmp_pe_v", "cmp_w1_v",
        "cmp_w2_v", "w_proj_nsa", "w_proj_fox", "w_out", "final_g"]


def rope_tables():
    inv = np.float32(10000.0) ** (-np.arange(0, HD, 2, dtype=np.float32) / np.float32(HD))
    ang = (np.arange(T, dtype=np.float32)[None, :] * inv[:, None]).astype(np.float32)
    cos, sin = np.cos(ang), np.sin(ang)
    return (np.concatenate([cos] * 4).astype(np.float32),
            np.concatenate([-sin, sin] * 2).astype(np.float32))


def kernel(**inputs):
    import concourse.bacc as _bacc
    from concourse.bass_utils import run_bass_kernel_spmd as _run

    nc = _bacc.Bacc("TRN2", target_bir_lowering=False, num_devices=1)
    arrays, args = {}, []
    for name in _INS:
        a = np.ascontiguousarray(inputs[name])
        arrays[f"in_{name}_dram"] = a
        args.append(nc.dram_tensor(f"in_{name}_dram", a.shape, mybir.dt.from_np(a.dtype), kind="ExternalInput").ap())
    for name, a in zip(("rope_cos", "rope_sin"), rope_tables()):
        arrays[f"in_{name}_dram"] = a
        args.append(nc.dram_tensor(f"in_{name}_dram", a.shape, mybir.dt.from_np(a.dtype), kind="ExternalInput").ap())
    args.append(nc.dram_tensor("out_0_dram", (1, T, D), F32, kind="ExternalOutput").ap())
    bass_trunk(nc, *args)
    r = _run(nc, [arrays], core_ids=[0])
    return r.results[0]["out_0_dram"]
```
